# Optimizing a Trainium2 kernel written in Bass

```python
import math
import jax
import jax.numpy as jnp
from jax import lax
import numpy as np
import jax, jax.numpy as jnp

D_MODEL = 1024
BATCH = 1
SEQ = 256
DEPTH = 2

N_A_LAYERS = DEPTH // 2
N_B_LAYERS = DEPTH - N_A_LAYERS
N_DENSE = (DEPTH + 1) // 2
N_MOE = DEPTH // 2

CONV_K = 31

N_HEADS = 16
HEAD_DIM = D_MODEL // N_HEADS
MOBA_BLOCK = 256
MOBA_TOPK = 3
Q_CHUNK = 32

D_FF = ((8 * D_MODEL // 3 + 255) // 256) * 256
N_EXPERTS = 8
TOP_K_EXPERTS = 2
D_FF_EXPERT = 7 * D_MODEL // 2

ALPHA = (2.0 * DEPTH) ** 0.25
BETA = (8.0 * DEPTH) ** -0.25

LN_EPS = 1e-5
NEG_INF = -1e30
ADA_INIT = 0.5


def layer_norm(x, g, b):
    xf = x.astype(jnp.float32)
    mu = jnp.mean(xf, axis=-1, keepdims=True)
    xc = xf - mu
    var = jnp.mean(xc * xc, axis=-1, keepdims=True)
    y = xc * lax.rsqrt(var + LN_EPS)
    return (y * g.astype(jnp.float32) + b.astype(jnp.float32)).astype(x.dtype)

def alibi_slopes(n_heads):
    return jnp.exp2(-8.0 * jnp.arange(1, n_heads + 1, dtype=jnp.float32) / n_heads)

def swiglu(h, w13, w2):
    a, b = jnp.split(h @ w13, 2, axis=-1)
    return (jax.nn.silu(a) * b) @ w2

def conv_module(h, w_in, b_in, w_dw, b_dw, g_n, b_n, w_out, b_out):
    a, g = jnp.split(h @ w_in + b_in, 2, axis=-1)
    u = a * jax.nn.sigmoid(g)
    u = lax.conv_general_dilated(
        u, w_dw[:, None, :], window_strides=(1,), padding=[(CONV_K - 1, 0)],
        dimension_numbers=("NWC", "WIO", "NWC"),
        feature_group_count=u.shape[-1]) + b_dw
    u = jax.nn.silu(layer_norm(u, g_n, b_n))
    return u @ w_out + b_out

def moe_swiglu(h, router_w, router_b, w13, w2):
    logits = (h @ router_w).astype(jnp.float32) + router_b.astype(jnp.float32)
    top_val, top_idx = lax.top_k(logits, TOP_K_EXPERTS)
    top_w = jax.nn.softmax(top_val, axis=-1)
    gates = jnp.sum(jax.nn.one_hot(top_idx, N_EXPERTS, dtype=jnp.float32) * top_w[..., None], axis=-2)
    gates = gates.astype(h.dtype)
    y = jnp.zeros_like(h)
    for e in range(N_EXPERTS):
        y = y + gates[..., e:e + 1] * swiglu(h, w13[e], w2[e])
    return y

def shared_kv(h, w_kv):
    B, S, _ = h.shape
    n_blk = -(-S // MOBA_BLOCK)
    pad = n_blk * MOBA_BLOCK - S
    k, v = jnp.split(h @ w_kv, 2, axis=-1)
    k = k.reshape(B, S, N_HEADS, HEAD_DIM).transpose(0, 2, 1, 3)
    v = v.reshape(B, S, N_HEADS, HEAD_DIM).transpose(0, 2, 1, 3)
    k_pad = jnp.pad(k, ((0, 0), (0, 0), (0, pad), (0, 0)))
    v_pad = jnp.pad(v, ((0, 0), (0, 0), (0, pad), (0, 0)))
    k_mean = jnp.mean(k_pad.reshape(B, N_HEADS, n_blk, MOBA_BLOCK, HEAD_DIM).astype(jnp.float32), axis=3)
    return k_pad, v_pad, k_mean

def moba_attention(q, k_pad, v_pad, k_mean, slopes):
    B, S, H, Dh = q.shape
    n_blk = k_mean.shape[2]
    topk = min(MOBA_TOPK, n_blk)
    kb = k_pad.reshape(B, H, n_blk, MOBA_BLOCK, Dh)
    vb = v_pad.reshape(B, H, n_blk, MOBA_BLOCK, Dh)
    n_chunk = S // Q_CHUNK
    q_chunks = q.transpose(0, 2, 1, 3).reshape(B, H, n_chunk, Q_CHUNK, Dh).transpose(2, 0, 1, 3, 4)
    scale = Dh ** -0.5
    b_idx = jnp.arange(B)[:, None, None, None]
    h_idx = jnp.arange(H)[None, :, None, None]
    blk_pos = jnp.arange(MOBA_BLOCK)

    def chunk(args):
        ci, qc = args
        start = ci * Q_CHUNK
        blk = start // MOBA_BLOCK
        t = start + jnp.arange(Q_CHUNK)
        gate = jnp.einsum("bhqd,bhnd->bhqn", qc.astype(jnp.float32), k_mean)
        gate = jnp.where(jnp.arange(n_blk) < blk, gate, -jnp.inf)
        _, idx = lax.top_k(gate, topk)
        valid = idx < blk
        k_sel = kb[b_idx, h_idx, idx]
        v_sel = vb[b_idx, h_idx, idx]
        dist_sel = (t[:, None, None] - (idx[..., None] * MOBA_BLOCK + blk_pos)).astype(jnp.float32)
        s_sel = jnp.einsum("bhqd,bhqnkd->bhqnk", qc, k_sel).astype(jnp.float32) * scale
        s_sel = s_sel - slopes[:, None, None, None] * dist_sel
        s_sel = jnp.where(valid[..., None], s_sel, NEG_INF)
        k_own = lax.dynamic_slice_in_dim(k_pad, blk * MOBA_BLOCK, MOBA_BLOCK, axis=2)
        v_own = lax.dynamic_slice_in_dim(v_pad, blk * MOBA_BLOCK, MOBA_BLOCK, axis=2)
        dist_own = t[:, None] - (blk * MOBA_BLOCK + blk_pos)[None, :]
        s_own = jnp.einsum("bhqd,bhkd->bhqk", qc, k_own).astype(jnp.float32) * scale
        s_own = s_own - slopes[:, None, None] * dist_own.astype(jnp.float32)
        s_own = jnp.where(dist_own >= 0, s_own, NEG_INF)
        scores = jnp.concatenate([s_sel.reshape(B, H, Q_CHUNK, topk * MOBA_BLOCK), s_own], axis=-1)
        p = jax.nn.softmax(scores, axis=-1).astype(v_pad.dtype)
        p_sel = p[..., :topk * MOBA_BLOCK].reshape(B, H, Q_CHUNK, topk, MOBA_BLOCK)
        p_own = p[..., topk * MOBA_BLOCK:]
        return (jnp.einsum("bhqnk,bhqnkd->bhqd", p_sel, v_sel)
                + jnp.einsum("bhqk,bhkd->bhqd", p_own, v_own))

    outs = lax.map(chunk, (jnp.arange(n_chunk), q_chunks))
    return outs.transpose(1, 0, 3, 2, 4).reshape(B, S, H * Dh)

def first_inputs(seed: int = 0) -> dict:
    key = jax.random.key(seed)
    ks = jax.random.split(key, 32)
    D = D_MODEL

    def nrm(k, shape, std):
        return jax.random.normal(k, shape, dtype=jnp.float32) * std

    return {
        "x": nrm(ks[0], (BATCH, SEQ, D), 1.0),
        "c": nrm(ks[1], (BATCH, D), 1.0),
        "ada_w": nrm(ks[2], (DEPTH, D, 6 * D), ADA_INIT * D ** -0.5),
        "ada_b": nrm(ks[3], (DEPTH, 6 * D), 0.01),
        "ln_g": 1.0 + nrm(ks[4], (DEPTH, 2, D), 0.05),
        "ln_b": nrm(ks[5], (DEPTH, 2, D), 0.01),
        "conv_in_w": nrm(ks[6], (N_A_LAYERS, D, 2 * D), D ** -0.5),
        "conv_in_b": nrm(ks[7], (N_A_LAYERS, 2 * D), 0.01),
        "conv_dw_w": nrm(ks[8], (N_A_LAYERS, CONV_K, D), CONV_K ** -0.5),
        "conv_dw_b": nrm(ks[9], (N_A_LAYERS, D), 0.01),
        "conv_norm_g": 1.0 + nrm(ks[10], (N_A_LAYERS, D), 0.05),
        "conv_norm_b": nrm(ks[11], (N_A_LAYERS, D), 0.01),
        "conv_out_w": nrm(ks[12], (N_A_LAYERS, D, D), BETA * D ** -0.5),
        "conv_out_b": nrm(ks[13], (N_A_LAYERS, D), 0.01),
        "kv_ada_w": nrm(ks[14], (D, 2 * D), ADA_INIT * D ** -0.5),
        "kv_ada_b": nrm(ks[15], (2 * D,), 0.01),
        "w_kv": nrm(ks[16], (D, 2 * D), D ** -0.5),
        "w_q": nrm(ks[17], (N_B_LAYERS, D, D), D ** -0.5),
        "w_o": nrm(ks[18], (N_B_LAYERS, D, D), BETA * D ** -0.5),
        "ffn_w13": nrm(ks[19], (N_DENSE, D, 2 * D_FF), D ** -0.5),
        "ffn_w2": nrm(ks[20], (N_DENSE, D_FF, D), BETA * D_FF ** -0.5),
        "router_w": nrm(ks[21], (N_MOE, D, N_EXPERTS), D ** -0.5),
        "router_b": nrm(ks[22], (N_MOE, N_EXPERTS), 0.01),
        "moe_w13": nrm(ks[23], (N_MOE, N_EXPERTS, D, 2 * D_FF_EXPERT), D ** -0.5),
        "moe_w2": nrm(ks[24], (N_MOE, N_EXPERTS, D_FF_EXPERT, D), BETA * D_FF_EXPERT ** -0.5),
    }

def first_block(x, c, ada_w, ada_b, ln_g, ln_b, conv_in_w, conv_in_b, conv_dw_w, conv_dw_b,
              conv_norm_g, conv_norm_b, conv_out_w, conv_out_b, kv_ada_w, kv_ada_b, w_kv,
              w_q, w_o, ffn_w13, ffn_w2, router_w, router_b, moe_w13, moe_w2):
    B, S, D = x.shape
    slopes = alibi_slopes(N_HEADS)
    c_act = jax.nn.silu(c)
    k_pad = v_pad = k_mean = None
    for l in range(DEPTH):
        if l == N_A_LAYERS:
            kv_shift, kv_scale = jnp.split(c_act @ kv_ada_w + kv_ada_b, 2, axis=-1)
            h_kv = x * (1.0 + kv_scale[:, None, :]) + kv_shift[:, None, :]
            k_pad, v_pad, k_mean = shared_kv(h_kv, w_kv)
        sh1, sc1, g1, sh2, sc2, g2 = jnp.split(c_act @ ada_w[l] + ada_b[l], 6, axis=-1)
        h = x * (1.0 + sc1[:, None, :]) + sh1[:, None, :]
        if l < N_A_LAYERS:
            out = conv_module(h, conv_in_w[l], conv_in_b[l], conv_dw_w[l], conv_dw_b[l],
                              conv_norm_g[l], conv_norm_b[l], conv_out_w[l], conv_out_b[l])
        else:
            j = l - N_A_LAYERS
            q = (h @ w_q[j]).reshape(B, S, N_HEADS, HEAD_DIM)
            out = moba_attention(q, k_pad, v_pad, k_mean, slopes) @ w_o[j]
        x = layer_norm(ALPHA * x + (1.0 + g1[:, None, :]) * out, ln_g[l, 0], ln_b[l, 0])
        h = x * (1.0 + sc2[:, None, :]) + sh2[:, None, :]
        if l % 2 == 0:
            f = swiglu(h, ffn_w13[l // 2], ffn_w2[l // 2])
        else:
            f = moe_swiglu(h, router_w[l // 2], router_b[l // 2], moe_w13[l // 2], moe_w2[l // 2])
        x = layer_norm(ALPHA * x + (1.0 + g2[:, None, :]) * f, ln_g[l, 1], ln_b[l, 1])
    return x


DEPTH_2 = 1

CHUNK = 64
N_PREV_CHUNKS = 8
BAND = (N_PREV_CHUNKS + 1) * CHUNK
HEAD_DIM_2 = 64
N_HEADS_ATTN = 8
N_HEADS_RWKV = 8
D_ATTN = N_HEADS_ATTN * HEAD_DIM_2
D_RWKV = N_HEADS_RWKV * HEAD_DIM_2
REL_CLIP = 128
DECAY_LORA = 64
AAA_LORA = 64
MV_LORA = 32
GATE_LORA = 160
N_GROUPS = 4
EXPERTS_PER_GROUP = 8
N_EXPERTS_2 = N_GROUPS * EXPERTS_PER_GROUP
TOP_K_IN_GROUP = 2
D_EXPERT = 256
D_PLE = 256
DEEPNORM_ALPHA = (2 * DEPTH_2) ** 0.25
DEEPNORM_BETA = (8 * DEPTH_2) ** -0.25
GN_EPS = 64e-5
NEG_INF_2 = -1e30

Q0 = 0
K0 = D_ATTN
V0 = 2 * D_ATTN
RW0 = 3 * D_ATTN
RW_COLS = 3 * D_RWKV + DECAY_LORA + AAA_LORA + GATE_LORA
GATE0 = RW0 + RW_COLS
N_IN = GATE0 + 2 * D_MODEL


def layer_norm_2(x, g, b):
    x32 = x.astype(jnp.float32)
    mu = jnp.mean(x32, axis=-1, keepdims=True)
    var = jnp.mean(jnp.square(x32 - mu), axis=-1, keepdims=True)
    y = (x32 - mu) * lax.rsqrt(var + LN_EPS)
    return (y * g.astype(jnp.float32) + b.astype(jnp.float32)).astype(x.dtype)

def chunked_band_attention(q, k, v, rel_bias):
    B, S, _ = q.shape
    nc = S // CHUNK
    q = q.reshape(B, nc, CHUNK, N_HEADS_ATTN, HEAD_DIM_2)
    pad = ((0, 0), (N_PREV_CHUNKS * CHUNK, 0), (0, 0))
    kp = jnp.pad(k, pad).reshape(B, nc + N_PREV_CHUNKS, CHUNK, N_HEADS_ATTN, HEAD_DIM_2)
    vp = jnp.pad(v, pad).reshape(B, nc + N_PREV_CHUNKS, CHUNK, N_HEADS_ATTN, HEAD_DIM_2)
    kb = jnp.concatenate([kp[:, j:j + nc] for j in range(N_PREV_CHUNKS + 1)], axis=2)
    vb = jnp.concatenate([vp[:, j:j + nc] for j in range(N_PREV_CHUNKS + 1)], axis=2)
    scores = jnp.einsum("bcqhd,bckhd->bhcqk", q, kb).astype(jnp.float32) * (HEAD_DIM_2 ** -0.5)
    qi = jnp.arange(CHUNK)[:, None]
    kj = jnp.arange(BAND)[None, :]
    dist = qi - (kj - N_PREV_CHUNKS * CHUNK)
    idx = jnp.clip(dist, -REL_CLIP, REL_CLIP) + REL_CLIP
    bias = rel_bias[:, idx].astype(jnp.float32)
    key_chunk = jnp.arange(nc)[:, None] - N_PREV_CHUNKS + (jnp.arange(BAND) // CHUNK)[None, :]
    valid = key_chunk >= 0
    scores = jnp.where(valid[None, None, :, None, :], scores + bias[None, :, None], NEG_INF_2)
    prob = jax.nn.softmax(scores, axis=-1).astype(v.dtype)
    out = jnp.einsum("bhcqk,bckhd->bcqhd", prob, vb)
    return out.reshape(B, S, D_ATTN)

def rwkv7_scan(r, w, k, v, a, b):
    B, S, H, N = r.shape
    xs = tuple(jnp.swapaxes(t.astype(jnp.float32), 0, 1) for t in (r, w, k, v, a, b))

    def step(state, inp):
        rt, wt, kt, vt, at, bt = inp
        sa = jnp.einsum("bhij,bhj->bhi", state, at)
        state = state * wt[:, :, None, :] + sa[..., None] * bt[:, :, None, :] + vt[..., None] * kt[:, :, None, :]
        return state, jnp.einsum("bhij,bhj->bhi", state, rt)

    state0 = jnp.zeros((B, H, N, N), jnp.float32)
    _, ys = lax.scan(step, state0, xs)
    return jnp.swapaxes(ys, 0, 1)

def rwkv7_time_mix(cols, mu, v_first, decay_base, decay_up, aaa_base, aaa_up, gate_up,
                   k_k, k_a, r_k, gn_g, gn_b, vres):
    B, S, _ = cols.shape
    prev = jnp.pad(cols, ((0, 0), (1, 0), (0, 0)))[:, :-1]
    cols = cols + (prev - cols) * mu
    splits = [D_RWKV, 2 * D_RWKV, 3 * D_RWKV, 3 * D_RWKV + DECAY_LORA, 3 * D_RWKV + DECAY_LORA + AAA_LORA]
    r, k, v, wd, ad, gd = jnp.split(cols, splits, axis=-1)
    w_log = -jax.nn.softplus(-(decay_base + jnp.tanh(wd) @ decay_up)) - 0.5
    decay = jnp.exp(-jnp.exp(w_log.astype(jnp.float32)))
    a = jax.nn.sigmoid(aaa_base + ad @ aaa_up)
    g = jax.nn.sigmoid(gd) @ gate_up
    heads = lambda t: t.reshape(B, S, N_HEADS_RWKV, HEAD_DIM_2)
    kk = heads(k * k_k).astype(jnp.float32)
    kk = kk * lax.rsqrt(jnp.maximum(jnp.sum(kk * kk, axis=-1, keepdims=True), 1e-24))
    k = k * (1.0 + (a - 1.0) * k_a)
    if vres is None:
        v_first = v
    else:
        vres_base, vres_down, vres_up = vres
        v = v + (v_first - v) * jax.nn.sigmoid(vres_base + (v @ vres_down) @ vres_up)
    r_h, k_h, v_h, a_h = heads(r), heads(k), heads(v), heads(a)
    y = rwkv7_scan(r_h, heads(decay), k_h, v_h, -kk, kk * a_h.astype(jnp.float32))
    m = jnp.mean(y, axis=-1, keepdims=True)
    var = jnp.mean(jnp.square(y - m), axis=-1, keepdims=True)
    yn = ((y - m) * lax.rsqrt(var + GN_EPS)).reshape(B, S, D_RWKV)
    yn = yn * gn_g.astype(jnp.float32) + gn_b.astype(jnp.float32)
    bonus = (jnp.sum(r_h * k_h * r_k, axis=-1, keepdims=True) * v_h).reshape(B, S, D_RWKV)
    out = (yn.astype(cols.dtype) + bonus) * g
    return out, v_first

def hier_moe(x, w_grp, b_grp, w_exp, b_exp, e_gate, e_up, e_down):
    B, S, D = x.shape
    T = B * S
    xt = x.reshape(T, D)
    glog = (xt @ w_grp + b_grp).astype(jnp.float32)
    gprob = jax.nn.softmax(glog, axis=-1)
    grp = jnp.argmax(glog, axis=-1)
    g_gate = jnp.take_along_axis(gprob, grp[:, None], axis=1)
    elog = (xt @ w_exp + b_exp).astype(jnp.float32).reshape(T, N_GROUPS, EXPERTS_PER_GROUP)
    sel = jnp.take_along_axis(elog, grp[:, None, None], axis=1)[:, 0]
    top_v, top_i = lax.top_k(sel, TOP_K_IN_GROUP)
    wk = jax.nn.softmax(top_v, axis=-1) * g_gate
    eid = grp[:, None] * EXPERTS_PER_GROUP + top_i
    comb = jnp.sum(jax.nn.one_hot(eid, N_EXPERTS_2, dtype=jnp.float32) * wk[..., None], axis=1).astype(x.dtype)
    out = jnp.zeros_like(xt)
    for e in range(N_EXPERTS_2):
        h = jax.nn.silu(xt @ e_gate[e]) * (xt @ e_up[e])
        out = out + (h * comb[:, e:e + 1]) @ e_down[e]
    return out.reshape(B, S, D)

def second_inputs(seed: int = 0) -> dict:
    key = jax.random.key(seed)
    keys = iter(jax.random.split(key, 48))
    nrm = lambda shape, s: jax.random.normal(next(keys), shape, jnp.float32) * s
    uni = lambda shape, lo, hi: jax.random.uniform(next(keys), shape, jnp.float32, lo, hi)
    col_scale = jnp.ones((N_IN,), jnp.float32)
    col_scale = col_scale.at[V0:RW0].set(DEEPNORM_BETA)
    col_scale = col_scale.at[RW0 + 2 * D_RWKV:RW0 + 3 * D_RWKV].set(DEEPNORM_BETA)
    return {
        "x": nrm((BATCH, SEQ, D_MODEL), 1.0),
        "p": nrm((DEPTH_2, BATCH, SEQ, D_PLE), 1.0),
        "ln_in_g": 1.0 + nrm((D_MODEL,), 0.02),
        "ln_in_b": nrm((D_MODEL,), 0.02),
        "rel_bias": nrm((N_HEADS_ATTN, 2 * REL_CLIP + 1), 0.1),
        "w_in": nrm((DEPTH_2, D_MODEL, N_IN), D_MODEL ** -0.5) * col_scale,
        "tok_mix": uni((DEPTH_2, RW_COLS), 0.0, 1.0),
        "decay_base": uni((DEPTH_2, D_RWKV), -6.0, -1.0),
        "decay_up": nrm((DEPTH_2, DECAY_LORA, D_RWKV), DECAY_LORA ** -0.5),
        "aaa_base": nrm((DEPTH_2, D_RWKV), 0.1),
        "aaa_up": nrm((DEPTH_2, AAA_LORA, D_RWKV), AAA_LORA ** -0.5),
        "gate_up": nrm((DEPTH_2, GATE_LORA, D_RWKV), GATE_LORA ** -0.5),
        "k_k": 0.85 + nrm((DEPTH_2, D_RWKV), 0.02),
        "k_a": 1.0 + nrm((DEPTH_2, D_RWKV), 0.02),
        "r_k": nrm((DEPTH_2, N_HEADS_RWKV, HEAD_DIM_2), 0.1),
        "vres_base": nrm((DEPTH_2 - 1, D_RWKV), 0.1),
        "vres_down": nrm((DEPTH_2 - 1, D_RWKV, MV_LORA), D_RWKV ** -0.5),
        "vres_up": nrm((DEPTH_2 - 1, MV_LORA, D_RWKV), MV_LORA ** -0.5),
        "gn_g": 1.0 + nrm((DEPTH_2, D_RWKV), 0.02),
        "gn_b": nrm((DEPTH_2, D_RWKV), 0.02),
        "w_branch_attn": nrm((DEPTH_2, D_ATTN, D_MODEL), D_ATTN ** -0.5 * DEEPNORM_BETA),
        "w_branch_rwkv": nrm((DEPTH_2, D_RWKV, D_MODEL), D_RWKV ** -0.5 * DEEPNORM_BETA),
        "w_out": nrm((DEPTH_2, D_MODEL, D_MODEL), D_MODEL ** -0.5 * DEEPNORM_BETA),
        "router_grp": nrm((DEPTH_2, D_MODEL, N_GROUPS), D_MODEL ** -0.5),
        "router_grp_bias": nrm((DEPTH_2, N_GROUPS), 0.01),
        "router_exp": nrm((DEPTH_2, D_MODEL, N_EXPERTS_2), D_MODEL ** -0.5),
        "router_exp_bias": nrm((DEPTH_2, N_EXPERTS_2), 0.01),
        "exp_gate": nrm((DEPTH_2, N_EXPERTS_2, D_MODEL, D_EXPERT), D_MODEL ** -0.5),
        "exp_up": nrm((DEPTH_2, N_EXPERTS_2, D_MODEL, D_EXPERT), D_MODEL ** -0.5),
        "exp_down": nrm((DEPTH_2, N_EXPERTS_2, D_EXPERT, D_MODEL), D_EXPERT ** -0.5 * DEEPNORM_BETA),
        "ple_proj": nrm((DEPTH_2, D_PLE, D_MODEL), D_PLE ** -0.5 * DEEPNORM_BETA),
        "ple_gate": nrm((DEPTH_2, D_MODEL, D_MODEL), D_MODEL ** -0.5),
        "ln_g": 1.0 + nrm((DEPTH_2, 3, D_MODEL), 0.02),
        "ln_b": nrm((DEPTH_2, 3, D_MODEL), 0.02),
    }

def second_block(x, p, ln_in_g, ln_in_b, rel_bias, w_in, tok_mix, decay_base, decay_up,
              aaa_base, aaa_up, gate_up, k_k, k_a, r_k, vres_base, vres_down, vres_up,
              gn_g, gn_b, w_branch_attn, w_branch_rwkv, w_out, router_grp, router_grp_bias,
              router_exp, router_exp_bias, exp_gate, exp_up, exp_down, ple_proj, ple_gate,
              ln_g, ln_b):
    x = layer_norm_2(x, ln_in_g, ln_in_b)
    v_first = None
    for i in range(DEPTH_2):
        proj = x @ w_in[i]
        y_attn = chunked_band_attention(proj[..., Q0:K0], proj[..., K0:V0], proj[..., V0:RW0], rel_bias)
        vres = None if i == 0 else (vres_base[i - 1], vres_down[i - 1], vres_up[i - 1])
        y_rwkv, v_first = rwkv7_time_mix(proj[..., RW0:GATE0], tok_mix[i], v_first, decay_base[i],
                                         decay_up[i], aaa_base[i], aaa_up[i], gate_up[i], k_k[i],
                                         k_a[i], r_k[i], gn_g[i], gn_b[i], vres)
        gate_a = jax.nn.sigmoid(proj[..., GATE0:GATE0 + D_MODEL])
        gate_b = jax.nn.sigmoid(proj[..., GATE0 + D_MODEL:])
        mixed = (gate_a * (y_attn @ w_branch_attn[i]) + gate_b * (y_rwkv @ w_branch_rwkv[i])) @ w_out[i]
        x = layer_norm_2(DEEPNORM_ALPHA * x + mixed, ln_g[i, 0], ln_b[i, 0])
        moe = hier_moe(x, router_grp[i], router_grp_bias[i], router_exp[i], router_exp_bias[i],
                       exp_gate[i], exp_up[i], exp_down[i])
        x = layer_norm_2(DEEPNORM_ALPHA * x + moe, ln_g[i, 1], ln_b[i, 1])
        ple = (p[i] @ ple_proj[i]) * jax.nn.sigmoid(x @ ple_gate[i])
        x = layer_norm_2(DEEPNORM_ALPHA * x + ple, ln_g[i, 2], ln_b[i, 2])
    return x


def setup_inputs(seed=0):
    out = dict(first_inputs(seed))
    for name, value in second_inputs(seed + 1).items():
        if name != "x":
            out[name + "_2"] = value
    return out


def reference(
    x, c, ada_w, ada_b, ln_g, ln_b, conv_in_w, conv_in_b, conv_dw_w, conv_dw_b, conv_norm_g,
    conv_norm_b, conv_out_w, conv_out_b, kv_ada_w, kv_ada_b, w_kv, w_q, w_o, ffn_w13, ffn_w2,
    router_w, router_b, moe_w13, moe_w2, p_2, ln_in_g_2, ln_in_b_2, rel_bias_2, w_in_2,
    tok_mix_2, decay_base_2, decay_up_2, aaa_base_2, aaa_up_2, gate_up_2, k_k_2, k_a_2, r_k_2,
    vres_base_2, vres_down_2, vres_up_2, gn_g_2, gn_b_2, w_branch_attn_2, w_branch_rwkv_2,
    w_out_2, router_grp_2, router_grp_bias_2, router_exp_2, router_exp_bias_2, exp_gate_2,
    exp_up_2, exp_down_2, ple_proj_2, ple_gate_2, ln_g_2, ln_b_2,
):
    x = first_block(
        x, c, ada_w, ada_b, ln_g, ln_b, conv_in_w, conv_in_b, conv_dw_w, conv_dw_b, conv_norm_g,
        conv_norm_b, conv_out_w, conv_out_b, kv_ada_w, kv_ada_b, w_kv, w_q, w_o, ffn_w13,
        ffn_w2, router_w, router_b, moe_w13, moe_w2,
    )
    return second_block(
        x, p_2, ln_in_g_2, ln_in_b_2, rel_bias_2, w_in_2, tok_mix_2, decay_base_2, decay_up_2,
        aaa_base_2, aaa_up_2, gate_up_2, k_k_2, k_a_2, r_k_2, vres_base_2, vres_down_2,
        vres_up_2, gn_g_2, gn_b_2, w_branch_attn_2, w_branch_rwkv_2, w_out_2, router_grp_2,
        router_grp_bias_2, router_exp_2, router_exp_bias_2, exp_gate_2, exp_up_2, exp_down_2,
        ple_proj_2, ple_gate_2, ln_g_2, ln_b_2,
    )


_drawn_inputs = setup_inputs


def setup_inputs(seed=0):
    import zlib

    import numpy as np

    out = dict(_drawn_inputs(seed))
    spreads = {}
    factors = {'ada_b': 3.056,
     'conv_in_b': 4.486,
     'conv_dw_b': 4.397,
     'conv_norm_b': 5.362,
     'conv_out_b': 3.159,
     'kv_ada_b': 4.901,
     'router_b': 2.863,
     'rel_bias_2': 36.92,
     'decay_up_2': 7.658,
     'aaa_base_2': 6.919,
     'k_k_2': 54.183,
     'k_a_2': 8.0,
     'r_k_2': 3.43,
     'gn_g_2': 29.677,
     'gn_b_2': 38.956,
     'router_grp_bias_2': 8.0,
     'router_exp_bias_2': 21.713,
     'w_branch_attn_2': 2.682}
    for name, (base, spread) in spreads.items():
        noise = np.random.default_rng([zlib.crc32(name.encode()), seed]).standard_normal(out[name].shape)
        drawn = base * np.exp(spread * noise) if base else spread * noise
        out[name] = jnp.asarray(drawn.astype(out[name].dtype))
    for name, factor in factors.items():
        out[name] = (out[name] * factor).astype(out[name].dtype)
    return out
```

```python
import math
from contextlib import ExitStack

import concourse.bass as bass
from concourse import mybir

F32 = mybir.dt.float32
F32R = mybir.dt.float32r
I32 = mybir.dt.int32
ALU = mybir.AluOpType
ACT = mybir.ActivationFunctionType
AX = mybir.AxisListType.X

P = 128
UNIT = 2048
SLOTS = 128
RAW, SPLIT = 6, 3
LN_EPS = 1e-5
GN_EPS = 64e-5
NEG = -1e30


class Tally:

    def __init__(self, nc, ctx, known):
        self.nc, self.ctx, self.known = nc, ctx, known
        self.sems, self.count, self.marks = {}, {}, {}
        self.banks, self.rot, self.occupant = {}, {}, {}

    def sem(self, name):
        if name not in self.sems:
            self.sems[name] = self.ctx.enter_context(self.nc.semaphore(name.replace(" ", "_")))
        return self.sems[name]

    def mark(self, label, sem, value):
        self.marks[label] = (sem, value)

    def at(self, label):
        if label not in self.marks and not self.known:
            return self.sem("stored"), 1
        sem, value = self.marks.get(label) or self.known[label]
        return self.sem(sem), value


class Engine:

    def __init__(self, tally, eng, name):
        self.t, self.eng, self.name = tally, eng, name
        self.stage = "start"
        self.last = None

    def tick(self, label=None):
        name = f"{self.name} {self.stage}"
        self.t.count[name] = self.t.count.get(name, 0) + 1
        self.last = (name, self.t.count[name])
        if label:
            self.t.mark(label, *self.last)
        return self.t.sem(name)

    def own(self):
        return self.t.sem(self.last[0]), self.last[1]


class Moe:

    def __init__(self, name, experts, together, chunks, first, groups, f):
        self.name, self.E, self.G, self.first, self.groups = name, experts, together, first, groups
        self.NG = experts // together
        self.NCH = chunks * together
        self.per = 3 * self.NCH
        self.units = self.NG * self.per
        self.f = f

    @staticmethod
    def unit(c, what):
        if what < 2:
            return what if isinstance(c, int) and c == 0 else 3 * c - 1 + what
        return 3 * c + 4

    def down(self, c):
        return self.per - 1 if isinstance(c, int) and c == self.NCH - 1 else self.unit(c, 2)


def col_rows():
    at, n = {}, 0
    for name, rows in (("conv_dw_w", 31), ("conv_dw_b", 1), ("conv_norm_g", 1), ("conv_norm_b", 1),
                       ("conv_out_b", 1), ("conv_in_b", 2), ("ada_b", 12), ("kv_ada_b", 2),
                       ("ln_g", 4), ("ln_b", 4), ("ln_in_g_2", 1), ("ln_in_b_2", 1), ("ln_g_2", 3),
                       ("ln_b_2", 3), ("c", 1), ("tok_mix_2", 3), ("decay_base_2", 1),
                       ("aaa_base_2", 1), ("k_k_2", 1), ("k_a_2", 1), ("r_k_2", 1), ("gn_g_2", 1),
                       ("gn_b_2", 1)):
        at[name] = n
        n += rows
    return at, n


def block_pair(nc, A, out, known):
    D, S = 1024, A["x"].shape[1]
    KT, TT = D // P, S // P
    DEPTH = A["ada_w"].shape[0]
    ALPHA = (2.0 * DEPTH) ** 0.25
    HEADS, HEADS2, DA = 16, 8, 512
    ALPHA2 = 2.0 ** 0.25
    TAPS = A["conv_dw_w"].shape[1]
    PAD = TAPS - 1
    FF = A["ffn_w2"].shape[1]
    NP = FF // 256
    ROW, NROW = col_rows()
    NV = 14

    units = []

    def kmajor(w, c0, cols, kt=KT):
        return w[0:kt * P, c0:c0 + cols].rearrange("(k p) n -> p k n", p=P)

    def add(key, w, c0, cols=256, kt=KT, split=True, r0=0):
        src = w[r0:r0 + kt * P, c0:c0 + cols].rearrange("(k p) n -> p k n", p=P)
        units.append((key, split, kt, cols, src))

    def ada(l, v0, v1):
        for j in range(4 * v0, 4 * v1):
            add(("ada", l, j), A["ada_w"][l], 256 * j, split=False)

    ada(0, 0, 2)
    w = A["conv_in_w"][0]
    for j in range(4):
        add(("conv a", j), w, 256 * j)
        add(("conv g", j), w, D + 256 * j)
    ada(0, 2, 6)
    for j in range(8):
        add(("ada", 2, j), A["kv_ada_w"], 256 * j, split=False)
    for j in range(4):
        add(("conv_out", j), A["conv_out_w"][0], 256 * j)
    w13, w2 = A["ffn_w13"][0], A["ffn_w2"][0]
    late = [("ada", 1, j) for j in range(24)]

    def down(j):
        add(("ffn2", j), w2, 0, D, 2, r0=256 * j)
        for _ in range(3):
            if late:
                key = late.pop(0)
                add(key, A["ada_w"][1], 256 * key[2], split=False)

    for j in range(NP):
        add(("ffn a", j), w13, 256 * j)
        add(("ffn b", j), w13, FF + 256 * j)
        if j:
            down(j - 1)
    down(NP - 1)
    for j in range(4):
        add(("k", j), A["w_kv"], 256 * j)
    for j in range(4):
        add(("v", j), A["w_kv"], D + 256 * j)
    for j in range(4):
        add(("q", j), A["w_q"][0], 256 * j)
    for j in range(4):
        add(("wo", j), A["w_o"][0], 256 * j)

    m1 = Moe("m1", experts=8, together=1, chunks=A["moe_w2"].shape[2] // 256, first=len(units), groups=1,
             f=A["moe_w2"].shape[2])
    for i in range(m1.units):
        units.append(((m1.name, i), True, KT // 2, 512, None))
    w = A["w_in_2"][0]
    RW0 = 3 * DA
    for j in range(7):
        add(("rw", j), w, RW0 + 256 * j)
    add(("rw", 7), w, RW0 + A["tok_mix_2"].shape[1] - P, P)
    for j in range(2):
        add(("v2", j), w, 2 * DA + 256 * j)
    for j in range(2):
        add(("q2", j), w, 256 * j)
    for j in range(2):
        add(("k2", j), w, DA + 256 * j)
    G0 = RW0 + A["tok_mix_2"].shape[1]
    for j in range(4):
        add(("ga", j), w, G0 + 256 * j)
    for j in range(2):
        add(("wa", j), A["w_branch_attn_2"][0], 512 * j, 512, 4)
    for j in range(4):
        add(("gb", j), w, G0 + D + 256 * j)
    for j in range(2):
        add(("wb", j), A["w_branch_rwkv_2"][0], 512 * j, 512, 4)
    for j in range(4):
        add(("w_out", j), A["w_out_2"][0], 256 * j)
    m2 = Moe("m2", experts=32, together=4, chunks=1, first=len(units), groups=4, f=256)
    for i in range(m2.units):
        units.append(((m2.name, i), True, KT // 2, 512, None))
    for j in range(4):
        add(("pg", j), A["ple_gate_2"][0], 256 * j)
    add(("pp", 0), A["ple_proj_2"][0], 0, D, 2)

    at_unit = {u[0]: n for n, u in enumerate(units)}
    split_before = [0]
    for u in units:
        split_before.append(split_before[-1] + u[1])

    with ExitStack() as ctx:
        T = Tally(nc, ctx, known)

        def sb(name, shape, dt=F32):
            return ctx.enter_context(nc.sbuf_tensor(name, shape, dt))

        ring_raw = sb("ring_raw", [P, RAW, UNIT])
        ring_hi = sb("ring_hi", [P, SPLIT, UNIT], F32R)
        ring_lo = sb("ring_lo", [P, SPLIT, UNIT], F32R)
        bank = [ctx.enter_context(nc.psum_tensor(f"bank{i}", [P, 512], F32)) for i in range(8)]
        xT = sb("xT", [P, KT, S])
        Hh, Hl = sb("Hh", [P, KT, S], F32R), sb("Hl", [P, KT, S], F32R)
        g_at = nc.sbuf_base
        Gh, Gl = sb("Gh", [P, KT, S], F32R), sb("Gl", [P, KT, S], F32R)
        GhF = nc.alloc_sbuf_tensor_at("GhF", [P, KT, S], F32, offset=g_at)
        GlF = nc.alloc_sbuf_tensor_at("GlF", [P, KT, S], F32, offset=g_at + 4 * KT * S)
        tA, tB, tC, tD = (sb(n, [P, KT, S]) for n in ("tA", "tB", "tC", "tD"))
        cols = sb("cols", [P, KT, NROW])
        mods = sb("mods", [P, NV, KT])
        uT = sb("uT", [P, KT, PAD + S])
        ccol = sb("ccol", [P, KT])
        gb = sb("gb", [P, KT])
        ident = sb("ident", [P, P])
        means = sb("means", [P, P])
        stat = sb("stat", [P, 2, S])
        eps = sb("eps", [P, 2])
        alibi = sb("alibi", [P, 3 * P])
        pr = sb("pr", [P, 3, 3 * P])
        prT = sb("prT", [P, 3, 3 * P])
        small = sb("small", [P, 3, 6])
        ones = sb("ones", [P, P])
        before = sb("before", [P, P])
        slots = sb("slots", [P, P])
        part = sb("part", [P, 1])
        lower = sb("lower", [P, 8, 8])
        psel_r = sb("psel_r", [P, TT, P], F32R)
        EM, GM = 32, 4
        rw = sb("rw", [P, KT, EM + GM])
        rbias = sb("rbias", [P, EM + GM])
        RT = pr[:, :, :].rearrange("p a b -> p (a b)")[:, 0:12 * TT * EM].rearrange("p (r a e) -> p r a e", r=12, a=TT)
        scr = sb("scr", [P, KT, S])
        m_iu = sb("m_iu", [P, P])[:, :]
        eLC = sb("eLC", [P, 4, 4])
        rmax = sb("rmax", [P, TT, 8])
        pos = sb("pos", [P, 9, TT, GM])
        gates = sb("gates", [P, 9, TT, GM])
        mask = sb("mask", [P, 9, GM])
        posg = sb("posg", [P, TT, GM])
        gateg = sb("gateg", [P, 2, TT, GM])
        maskg = sb("maskg", [P, 2, GM])
        ge = sb("ge", [P, 2, GM])
        most = sb("most", [P, 2])
        overflow = sb("overflow", [P, 1], I32)

        raw_landed = [ctx.enter_context(nc.semaphore(f"raw_landed{i}")) for i in range(RAW)]
        for i in range(RAW):
            T.sems[f"raw_landed {i}"] = raw_landed[i]

        def view(ring, slot, kt, n):
            return ring[:, slot, 0:kt * n].rearrange("p (k n) -> p k n", k=kt)

        def weights(n):
            key, split, kt, c, _ = units[n]
            if split:
                s = split_before[n] % SPLIT
                return view(ring_hi, s, kt, c), view(ring_lo, s, kt, c)
            return view(ring_raw, n % RAW, kt, c), None

        def landed(e, n):
            e.eng.wait_ge(T.sem(f"raw_landed {n % RAW}"), 32 * (n // RAW + 1))

        GROUPS = {"A": [0, 1, 2, 3], "B": [4, 5], "C": [6, 7], "D": [4, 5, 6, 7]}

        def take(pe, job, group="A"):
            i = T.rot.get(group, 0)
            T.rot[group] = i + 1
            b = GROUPS[group][i % len(GROUPS[group])]
            if T.occupant.get(b):
                pe.eng.wait_ge(*T.at("ev " + T.occupant[b]))
            T.occupant[b] = job
            T.banks[job] = b
            return bank[b]

        def ps(job):
            return bank[T.known.get("bank", {}).get(job, 0)]

        VEC = lambda l, v: 6 * l + v
        def mod(l, v, kt):
            return mods[:, VEC(l, v), kt:kt + 1]

        def col(name, kt, i=0):
            r = ROW[name] + i
            return cols[:, kt, r:r + 1]

        flat = lambda t: t[:, :, :].rearrange("p a b -> p (a b)")
        uF = flat(uT)
        relb = uF[:, 0:HEADS2 * S].rearrange("p (h k) -> p h k", h=HEADS2)
        rel = flat(tC)[0:HEADS2, 1024:1024 + 3 * P]
        du, gu1, gu2 = (flat(scr)[:, 512 * i:512 * i + 512] for i in range(3))
        Q2, K2 = tD[:, 0:4, :], tD[:, 4:8, :]
        V2 = tC[:, 0:4, :].rearrange("p (a k) t -> p a (k t)", a=TT)
        MA = GlF[:, :, :]
        prF, prTF, sF, gF = flat(pr), flat(prT), flat(scr), flat(GhF)
        m_su, m_sl, m_d16 = (alibi[:, P * i:P * i + P] for i in range(3))
        m_o32, m_o64, m_d64 = prF[:, 1024:1152], prTF[:, 1024:1152], uF[:, 2048:2176]
        four = lambda t: t.rearrange("p (i n) -> p i n", i=4)
        bc4 = lambda m: m.unsqueeze(1).to_broadcast([P, 4, P])
        rt_, kt_, bt_, at_ = tA[:, 0:4, :], tA[:, 4:8, :], tC[:, 4:8, :], tD[:, 0:4, :]
        bonus, gg = tC[:, 0:4, :], tD[:, 4:8, :]
        Vtok = tB[:, 4:8, :].rearrange("p (a k) t -> p a (k t)", a=TT)
        XA = flat(tB)[:, 0:1024].rearrange("p (h t) -> p h t", h=HEADS2)
        ArbT = uF[:, 0:1024].rearrange("p (h t) -> p h t", h=HEADS2)
        ArkT = uF[:, 1024:2048].rearrange("p (h t) -> p h t", h=HEADS2)
        mA, mAt, mS, mSt = prF[:, 0:512], prF[:, 512:1024], prTF[:, 0:512], prTF[:, 512:1024]
        mT = stat[:, :, :].rearrange("p a b -> p (a b)")
        ktok, btok, ZV, Pm = (gF[:, 512 * i:512 * i + 512] for i in range(4))
        U, Sbd = sF[:, 0:512], sF[:, 512:1024]
        yT = scr[:, 4:8, :]

        tok_hi = Gh[:, :, :].rearrange("p (a k) t -> p a (k t)", a=TT)
        tok_lo = Gl[:, :, :].rearrange("p (a k) t -> p a (k t)", a=TT)
        xg_hi, xg_lo = Hh[:, :, 0:P], Hl[:, :, 0:P]
        mh_hi, mh_lo = Hh[:, 0:2, P:2 * P], Hl[:, 0:2, P:2 * P]
        ysb = tA[:, 0:4, :].rearrange("p k t -> p (k t)")
        pself = [tA[:, 4 + i, :].rearrange("p (a s) -> p a s", a=TT) for i in range(2)]
        pselT = [tA[:, 6 + i, :] for i in range(2)]

        nxt = {"act": 0, "dve": 0}

        def split_hi(act, upto):
            while nxt["act"] <= min(upto, len(units) - 1):
                n = nxt["act"]
                if units[n][4] is None:
                    break
                nxt["act"] += 1
                key, split, kt, c, _ = units[n]
                if not split:
                    continue
                i = split_before[n]
                landed(act, n)
                if i >= SPLIT:
                    act.eng.wait_ge(T.sem("unit_done"), after_split(i - SPLIT) + 1)
                nc.scalar.activation(ring_hi[:, i % SPLIT, 0:kt * c], ring_raw[:, n % RAW, 0:kt * c],
                                     ACT.Copy).then_inc(T.sem("hi_done"), 1)

        def split_lo(dve, upto):
            while nxt["dve"] <= min(upto, len(units) - 1):
                n = nxt["dve"]
                if units[n][4] is None:
                    break
                nxt["dve"] += 1
                key, split, kt, c, _ = units[n]
                if not split:
                    continue
                i = split_before[n]
                landed(dve, n)
                dve.eng.wait_ge(T.sem("hi_done"), i + 1)
                if i >= SPLIT:
                    dve.eng.wait_ge(T.sem("unit_done"), after_split(i - SPLIT) + 1)
                nc.vector.tensor_tensor(ring_lo[:, i % SPLIT, 0:kt * c], ring_raw[:, n % RAW, 0:kt * c],
                                        ring_hi[:, i % SPLIT, 0:kt * c].bitcast(F32),
                                        ALU.subtract).then_inc(T.sem("lo_done"), 1)

        split_units = [n for n, u in enumerate(units) if u[1]]
        after_split = lambda i: split_units[i]

        def attention(pe, name, heads, Q, K, V):
            mm = nc.tensor.matmul
            bank_o = {}
            for i in range(heads + 3):
                if i < heads:
                    h = i
                    b = take(pe, f"{name} s {h}")
                    k, r = h // 2, slice(64 * (h % 2), 64 * (h % 2) + 64)
                    pe.eng.wait_ge(*T.at(f"{name} qT {k // 2}"))
                    pe.eng.wait_ge(*T.at(f"{name} kT {k // 2}"))
                    mm(b[:, 0:P], Q[r, k, 0:P], K[r, k, 0:P], start=True, stop=True)
                    mm(b[:, P:3 * P], Q[r, k, P:S], K[r, k, :], start=True, stop=True).then_inc(pe.tick(f"mm {name} s {h}"), 1)
                if 2 <= i < heads + 2:
                    h = i - 2
                    b = take(pe, f"{name} pT {h}", "B")
                    pe.eng.wait_ge(*T.at(f"{name} p {h}"))
                    for c in range(3):
                        last = nc.tensor.transpose(b[:, c * P:(c + 1) * P], pr[:, h % 3, c * P:(c + 1) * P],
                                                   ident[:, :])
                    last.then_inc(pe.tick(f"mm {name} pT {h}"), 1)
                if i >= 3:
                    h = i - 3
                    k, r = h // 2, slice(64 * (h % 2), 64 * (h % 2) + 64)
                    if h % 2 == 0:
                        bank_o[k] = take(pe, f"{name} o {k}", "C")
                    b = bank_o[k]
                    pe.eng.wait_ge(*T.at(f"{name} pT {h}"))
                    pe.eng.wait_ge(*T.at(f"{name} v"))
                    hs = slice(64 * h, 64 * h + 64)
                    mm(b[r, 0:S], V[:, 0, hs], prT[:, h % 3, 0:2 * P], start=True, stop=False,
                       skip_group_check=True)
                    mm(b[r, P:S], V[:, 1, hs], prT[:, h % 3, 2 * P:3 * P], start=False, stop=True,
                               skip_group_check=True).then_inc(pe.tick(f"mm {name} o {h}"), 1)

        def rwkv_pe(pe):
            mm = nc.tensor.matmul
            pe.stage = "rwkv"

            def job(name, label, body, waits=()):
                b = take(pe, name)
                for label in waits:
                    pe.eng.wait_ge(*T.at(label))
                body(b).then_inc(pe.tick("mm " + name), 1)

            def each(n, one):
                def body(b):
                    for i in range(n):
                        last = one(b, i)
                    return last
                return body

            pe.eng.wait_ge(*T.at("lora landed"))
            for j in range(2):
                blk = lambda w, i: w[:, (2 * j + i) * P:(2 * j + i + 1) * P]
                job(f"zw {j}", "", each(2, lambda b, i: mm(b[:, i * S:(i + 1) * S], blk(du[0:64, :], i),
                                                           tB[0:64, 7, :], start=True, stop=True)), ["tanh w"])
                job(f"za {j}", "", each(2, lambda b, i: mm(b[:, i * S:(i + 1) * S], blk(du[64:P, :], i),
                                                           tB[64:P, 4, :], start=True, stop=True)), ["mix 7"])

                def gate(b, i):
                    mm(b[:, i * S:(i + 1) * S], blk(gu1, i), tB[:, 5, :], start=True, stop=False)
                    return mm(b[:, i * S:(i + 1) * S], blk(gu2, i), tB[:, 6, :], start=False, stop=True)
                job(f"gg {j}", "", each(2, gate), ["sigmoid g"])
            pe.eng.wait_ge(*T.at("chunk masks"))
            for a in range(TT):
                job(f"vtok {a}", "", each(4, lambda b, i: nc.tensor.transpose(
                    b[:, i * P:(i + 1) * P], tB[:, i, a * P:(a + 1) * P], ident[:, :])), ["mix 7"])
            for name, tile, w in (("ss", lambda k: tC[:, k, :], "k squared"), ("rk", lambda k: tC[:, k, :], "r k")):
                for j in range(2):
                    job(f"{name} {j}", "", each(2, lambda b, i: mm(b[:, i * S:(i + 1) * S], m_d64,
                                                                   tile(2 * j + i), start=True, stop=True)), [w])
            pe.eng.wait_ge(*T.at("decayed"))
            for a in range(TT):
                cs = slice(a * P, (a + 1) * P)
                for name, src in (("ktok", kt_), ("btok", bt_)):
                    job(f"{name} {a}", "", each(4, lambda b, i: nc.tensor.transpose(
                        b[:, i * P:(i + 1) * P], src[:, i, cs], ident[:, :])))
                for q in range(2):
                    r = slice(64 * q, 64 * q + 64)
                    n = f"{a} {q}"

                    def outer(l, rr):
                        return each(4, lambda b, i: mm(b[:, i * P:(i + 1) * P], l[r, i, cs], rr[r, i, cs],
                                                       start=True, stop=True))
                    job(f"A {n}", "", outer(at_, bt_))
                    job(f"At {n}", "", outer(bt_, at_))
                    job(f"Arb {n}", "", outer(bt_, rt_))
                    job(f"Ark {n}", "", outer(kt_, rt_))
                    job(f"Mak {n}", "", outer(kt_, at_))
                    pe.eng.wait_ge(*T.at(f"Mak {n}"))
                    pe.eng.wait_ge(*T.at("Vtok"))
                    job(f"ZV {n}", "", each(4, lambda b, i: mm(
                        b[:, i * 64:i * 64 + 64], mS[:, i * P:(i + 1) * P],
                        Vtok[:, a, 128 * i + 64 * q:128 * i + 64 * q + 64], start=True, stop=True)))
                    X = lambda i: XA[:, 2 * i + q, :]

                    def prod(l, rr):
                        return each(4, lambda b, i: mm(b[:, i * P:(i + 1) * P], l(i), rr(i), start=True, stop=True))
                    f4 = lambda t: (lambda i: t[:, i * P:(i + 1) * P])
                    pe.eng.wait_ge(*T.at(f"TX {n} 0"))
                    for lev in range(3):
                        job(f"S2 {n} {lev}", "", prod(f4(mSt), f4(mS)))
                        if lev < 2:
                            job(f"S2t {n} {lev}", "", prod(f4(mS), f4(mSt)))
                        pe.eng.wait_ge(*T.at(f"S2 {n} {lev}"))
                        job(f"TS {n} {lev}", "", prod(X, f4(mS)))
                        job(f"XS {n} {lev}", "", prod(f4(mS), X))
                        pe.eng.wait_ge(*T.at(f"TX {n} {lev + 1}"))
                    for o in range(2):
                        pe.eng.wait_ge(*T.at(f"off {n} {o}"))
                        job(f"Q {n} {o}", "", prod(f4(mSt), f4(mT)))
                        pe.eng.wait_ge(*T.at(f"Q {n} {o}"))
                        if o == 0:
                            job(f"TQ {n} {o}", "", prod(X, f4(mS)))
                        job(f"XQ {n} {o}", "", prod(f4(mS), X))
                        pe.eng.wait_ge(*T.at(f"TX {n} {4 + o}"))
                ys = take(pe, f"ys {a}", "C")
                for cc in range(2):
                    c = 2 * a + cc
                    b0 = slice(64 * cc, 64 * cc + 64)
                    t64 = slice(a * P + 64 * cc, a * P + 64 * cc + 64)
                    pe.eng.wait_ge(*T.at(f"S {c}"))
                    job(f"P {c}", "", each(4, lambda b, i: mm(b[b0, i * P:(i + 1) * P], at_[:, i, t64],
                                                              Sbd[:, i * P:(i + 1) * P], start=True, stop=True)))
                    for i in range(4):
                        last = mm(ys[:, i * P + 64 * cc:i * P + 64 * cc + 64], Sbd[:, i * P:(i + 1) * P],
                                  rt_[:, i, t64], start=True, stop=True)
                    last.then_inc(pe.tick(f"mm ys {a}"), 1)
                    pe.eng.wait_ge(*T.at(f"P {c}"))
                    job(f"U {c}", "", each(8, lambda b, h: mm(b[b0, 64 * h:64 * h + 64], XA[b0, h, b0],
                                                              Pm[b0, 64 * h:64 * h + 64], start=True, stop=True)))
                    pe.eng.wait_ge(*T.at(f"U {c}"))
                    pe.eng.wait_ge(*T.at(f"tok {a}"))

                    def state(b, i):
                        ks = slice(i * P, (i + 1) * P)
                        mm(b[:, ks], ktok[b0, ks], Vtok[b0, a, ks], start=True, stop=False)
                        return mm(b[:, ks], btok[b0, ks], U[b0, ks], start=False, stop=True)
                    if c < 3:
                        job(f"S {c}", "", each(4, state))
                yu = take(pe, f"yu {a}", "B")
                pe.eng.wait_ge(*T.at(f"Ark {a} 1"))
                pe.eng.wait_ge(*T.at(f"Arb {a} 1"))
                for h in range(HEADS2):
                    o = yu[64 * (h % 2):64 * (h % 2) + 64, (h // 2) * P:(h // 2 + 1) * P]
                    hs = slice(64 * h, 64 * h + 64)
                    mm(o, U[:, hs], ArbT[:, h, :], start=True, stop=False, skip_group_check=True)
                    last = mm(o, Vtok[:, a, hs], ArkT[:, h, :], start=False, stop=True, skip_group_check=True)
                last.then_inc(pe.tick(f"mm yu {a}"), 1)
            for name, tile, w in (("gm", lambda k: yT[:, k, :], "y 1"), ("gv", lambda k: GhF[:, k, :], "y squared")):
                for j in range(2):
                    job(f"{name} {j}", "", each(2, lambda b, i: mm(b[:, i * S:(i + 1) * S], m_d64,
                                                                   tile(2 * j + i), start=True, stop=True)), [w])

        def rwkv_act(act):
            run = nc.scalar.activation
            act.stage = "rwkv"
            act.eng.wait_ge(*T.at("mix 7"))
            run(tB[0:64, 7, :], tB[0:64, 4, :], ACT.Tanh).then_inc(act.tick("tanh w"), 1)
            run(tB[:, 5:7, :], tB[:, 5:7, :], ACT.Sigmoid).then_inc(act.tick("sigmoid g"), 1)
            for j in range(2):
                act.eng.wait_ge(*T.at(f"mm zw {j}"))
                for i in range(2):
                    run(tC[:, 2 * j + i, :], ps(f"zw {j}")[:, i * S:(i + 1) * S], ACT.Sigmoid,
                                 bias=col("decay_base_2", 2 * j + i)).then_inc(act.tick(f"ev zw {j}"), 1)
                act.eng.wait_ge(*T.at(f"mm za {j}"))
                for i in range(2):
                    run(tC[:, 4 + 2 * j + i, :], ps(f"za {j}")[:, i * S:(i + 1) * S], ACT.Sigmoid,
                                 bias=col("aaa_base_2", 2 * j + i)).then_inc(act.tick(f"ev za {j}"), 1)
                act.eng.wait_ge(*T.at(f"mm gg {j}"))
                run(gg[:, 2 * j:2 * j + 2, :], ps(f"gg {j}")[:, :].rearrange("p (k t) -> p k t", k=2),
                             ACT.Copy).then_inc(act.tick(f"ev gg {j}"), 1)
            T.mark("w a g", *act.last)
            for a in range(TT):
                act.eng.wait_ge(*T.at(f"mm vtok {a}"))
                run(Vtok[:, a, :], ps(f"vtok {a}")[:, :], ACT.Copy).then_inc(act.tick(f"ev vtok {a}"), 1)
            T.mark("Vtok", *act.last)
            act.eng.wait_ge(*T.at("k k_k"))
            act.eng.wait_ge(*T.at("ld done"))
            run(tC[:, 0:4, :], tD[:, 0:4, :], ACT.Square).then_inc(act.tick("k squared"), 1)
            act.eng.wait_ge(*T.at("norm2"))
            run(tC[:, 0:4, :], tC[:, 0:4, :], ACT.Sqrt).then_inc(act.tick("norm"), 1)
            act.eng.wait_ge(*T.at("L done"))
            act.eng.wait_ge(*T.at("mm wa 1.1"))
            run(GhF[:, 0:4, :], four(uF[:, 0:1024]), ACT.Exp).then_inc(act.tick(), 1)
            run(GhF[:, 4:8, :], four(uF[:, 0:1024]), ACT.Exp, scale=-1.0).then_inc(act.tick(), 1)
            run(four(uF[:, 1024:2048]), four(uF[:, 1024:2048]), ACT.Exp).then_inc(act.tick(), 1)
            ends = GhF[:, 0:4, :].rearrange("p k (c t) -> p k c t", t=64)[:, :, :, 63]
            act.eng.wait_ge(*act.own())
            run(eLC[:, :, :], ends, ACT.Copy).then_inc(act.tick("exps"), 1)
            act.eng.wait_ge(*T.at("decayed"))
            for a in range(TT):
                for name, dst in (("ktok", ktok), ("btok", btok)):
                    act.eng.wait_ge(*T.at(f"mm {name} {a}"))
                    if a:
                        act.eng.wait_ge(*T.at("mm S 1"))
                        act.eng.wait_ge(*T.at(f"mm ys {0}"))
                    run(dst, ps(f"{name} {a}")[:, :], ACT.Copy).then_inc(act.tick(f"ev {name} {a}"), 1)
                T.mark(f"tok {a}", *act.last)
                for q in range(2):
                    n = f"{a} {q}"
                    act.eng.wait_ge(*T.at(f"mm ZV {n}"))
                    zv = ZV.rearrange("p (i q v) -> p i q v", i=4, q=2)[:, :, q, :]
                    if a and q == 0:
                        act.eng.wait_ge(*T.at("P 1"))
                    run(zv, ps(f"ZV {n}")[:, 0:256].rearrange("p (i v) -> p i v", i=4), ACT.Copy).then_inc(act.tick(f"ev ZV {n}"), 1)
                    for lev in range(3):
                        last = f"S2t {n} {lev}" if lev < 2 else f"S2 {n} {lev}"
                        act.eng.wait_ge(*T.at("mm " + last))
                        act.eng.wait_ge(*T.at(f"TX {n} {lev}"))
                        run(mS, ps(f"S2 {n} {lev}")[:, :], ACT.Copy).then_inc(act.tick(f"ev S2 {n} {lev}"), 1)
                        if lev < 2:
                            run(mSt, ps(f"S2t {n} {lev}")[:, :], ACT.Copy).then_inc(act.tick(f"ev S2t {n} {lev}"), 1)
                        T.mark(f"S2 {n} {lev}", *act.last)
                    for o in range(2):
                        act.eng.wait_ge(*T.at(f"mm Q {n} {o}"))
                        run(mS, ps(f"Q {n} {o}")[:, :], ACT.Copy).then_inc(act.tick(f"ev Q {n} {o}"), 1)
                        T.mark(f"Q {n} {o}", *act.last)
                for cc in range(2):
                    c = 2 * a + cc
                    b0 = slice(64 * cc, 64 * cc + 64)
                    act.eng.wait_ge(*T.at(f"mm U {c}"))
                    if a:
                        act.eng.wait_ge(*T.at("mm yu 0"))
                    run(U[b0, :], ps(f"U {c}")[b0, :], ACT.Copy).then_inc(act.tick(f"ev U {c}"), 1)
                    T.mark(f"U {c}", *act.last)
                act.eng.wait_ge(*T.at(f"mm ys {a}"))
                run(yT[:, :, a * P:(a + 1) * P], four(ps(f"ys {a}")[:, :]), ACT.Copy).then_inc(act.tick(f"ev ys {a}"), 1)
            act.eng.wait_ge(*T.at("y centred"))
            run(GhF[:, 0:4, :], yT, ACT.Square).then_inc(act.tick("y squared"), 1)
            for j in range(2):
                act.eng.wait_ge(*T.at(f"mm gv {j}"))
                run(GhF[:, 4 + 2 * j:6 + 2 * j, :], ps(f"gv {j}")[:, :].rearrange("p (k t) -> p k t", k=2),
                             ACT.Sqrt, scale=1.0 / 64, bias=eps[:, 1:2]).then_inc(act.tick(f"ev gv {j}"), 1)
            T.mark("y std", *act.last)
            act.eng.wait_ge(*T.at("y out"))
            run(Gh[:, 0:4, :], yT, ACT.Copy).then_inc(act.tick("Gh wb"), 1)

        def rwkv_dve(dve):
            tt, ts, stt = nc.vector.tensor_tensor, nc.vector.tensor_scalar, nc.vector.scalar_tensor_tensor
            dve.stage = "rwkv"
            dve.eng.wait_ge(*T.at("w a g"))
            dve.eng.wait_ge(*T.at("routing constants"))
            for j in range(2):
                s = slice(2 * j, 2 * j + 2)
                ts(tC[:, s, :], tC[:, s, :], -math.exp(-0.5), None, ALU.mult).then_inc(dve.tick(), 1)
            dve.eng.wait_ge(*T.at("mix 7"))
            for k in range(4):
                ts(tD[:, k, :], tA[:, 4 + k, :], col("k_k_2", k), None, ALU.mult).then_inc(dve.tick(), 1)
            T.mark("k k_k", *dve.last)
            dve.eng.wait_ge(*dve.own())
            for k in range(4):
                for c in range(4):
                    cs = slice(64 * c, 64 * c + 64)
                    nc.vector.tensor_tensor_scan(uF[:, 256 * k + 64 * c:256 * k + 64 * c + 64],
                                                          ones[:, 0:64], tC[:, k, cs], 0.0, ALU.mult, ALU.add).then_inc(dve.tick(), 1)
            dve.eng.wait_ge(*dve.own())
            tt(four(uF[:, 1024:2048]), four(uF[:, 0:1024]), tC[:, 0:4, :], ALU.subtract).then_inc(dve.tick("L done"), 1)
            T.mark("ld done", *dve.last)
            for j in range(2):
                dve.eng.wait_ge(*T.at(f"mm ss {j}"))
                ts(tC[:, 2 * j:2 * j + 2, :], ps(f"ss {j}")[:, :].rearrange("p (k t) -> p k t", k=2),
                            1e-24, None, ALU.max).then_inc(dve.tick(f"ev ss {j}"), 1)
            T.mark("norm2", *dve.last)
            dve.eng.wait_ge(*T.at("norm"))
            nc.vector.reciprocal(tC[:, 0:4, :], tC[:, 0:4, :]).then_inc(dve.tick(), 1)
            dve.eng.wait_ge(*dve.own())
            tt(tD[:, 0:4, :], tD[:, 0:4, :], tC[:, 0:4, :], ALU.mult).then_inc(dve.tick(), 1)
            dve.eng.wait_ge(*dve.own())
            for k in range(4):
                ts(tC[:, k, :], tC[:, 4 + k, :], 1.0, col("k_a_2", k), ALU.subtract, ALU.mult).then_inc(dve.tick(), 1)
            dve.eng.wait_ge(*dve.own())
            tt(tC[:, 4:8, :], tC[:, 4:8, :], tD[:, 0:4, :], ALU.mult).then_inc(dve.tick(), 1)
            dve.eng.wait_ge(*dve.own())
            for k in range(4):
                stt(tA[:, 4 + k, :], tC[:, k, :], 1.0, tA[:, 4 + k, :], ALU.add, ALU.mult).then_inc(dve.tick(), 1)
            dve.eng.wait_ge(*dve.own())
            for k in range(4):
                stt(tC[:, k, :], tA[:, 4 + k, :], col("r_k_2", k), tA[:, k, :], ALU.mult, ALU.mult).then_inc(dve.tick(), 1)
            T.mark("r k", *dve.last)
            dve.eng.wait_ge(*dve.own())
            dve.eng.wait_ge(*T.at("exps"))
            tt(rt_, rt_, GhF[:, 0:4, :], ALU.mult).then_inc(dve.tick(), 1)
            tt(kt_, kt_, GhF[:, 4:8, :], ALU.mult).then_inc(dve.tick(), 1)
            tt(bt_, bt_, GhF[:, 4:8, :], ALU.mult).then_inc(dve.tick(), 1)
            stt(at_.rearrange("p k t -> p (k t)"), at_.rearrange("p k t -> p (k t)"), -1.0,
                         uF[:, 1024:2048], ALU.mult, ALU.mult).then_inc(dve.tick(), 1)
            T.mark("decayed", *dve.last)
            for j in range(2):
                s = slice(2 * j, 2 * j + 2)
                dve.eng.wait_ge(*T.at(f"mm rk {j}"))
                dve.eng.wait_ge(*T.at("mm rk 1"))
                tt(tC[:, s, :], tB[:, s, :], ps(f"rk {j}")[:, :].rearrange("p (k t) -> p k t", k=2),
                            ALU.mult).then_inc(dve.tick(f"ev rk {j}"), 1)
            nc.vector.memset(Sbd, 0.0).then_inc(dve.tick("S 0"), 1)
            dve.eng.wait_ge(*T.at("chunk masks"))
            dve.eng.wait_ge(*T.at("ev vtok 1"))
            for a in range(TT):
                for q in range(2):
                    n = f"{a} {q}"

                    def masked(job, dst, mask, waits=()):
                        dve.eng.wait_ge(*T.at("mm " + job))
                        for label in waits:
                            dve.eng.wait_ge(*T.at(label))
                        tt(dst, four(ps(job)[:, :]), bc4(mask), ALU.mult).then_inc(dve.tick("ev " + job), 1)
                        T.mark(job, *dve.last)
                    by_head = lambda t: t.rearrange("p (i q) t -> p i q t", q=2)[:, :, q, :]
                    masked(f"A {n}", four(mA), m_sl)
                    masked(f"At {n}", four(mAt), m_su)
                    late = ["mm yu 0"] if a else []
                    masked(f"Arb {n}", by_head(ArbT), m_iu, late)
                    masked(f"Ark {n}", by_head(ArkT), m_iu)
                    masked(f"Mak {n}", four(mS), m_su)
                    dve.eng.wait_ge(*T.at(f"mm ZV {n}"))
                    tt(four(mS), four(mA), bc4(m_d16), ALU.mult).then_inc(dve.tick(), 1)
                    tt(four(mSt), four(mAt), bc4(m_d16), ALU.mult).then_inc(dve.tick(), 1)
                    dve.eng.wait_ge(*dve.own())
                    if a:
                        dve.eng.wait_ge(*T.at("mm U 1"))
                    tt(four(mT), four(mS), bc4(ident[:, :]), ALU.add).then_inc(dve.tick(), 1)
                    tt(by_head(XA), four(mSt), bc4(ident[:, :]), ALU.add).then_inc(dve.tick(f"TX {n} 0"), 1)

                    def add(job, dst):
                        dve.eng.wait_ge(*T.at("mm " + job))
                        tt(dst, dst, four(ps(job)[:, :]), ALU.add).then_inc(dve.tick("ev " + job), 1)
                    for lev in range(3):
                        dve.eng.wait_ge(*T.at(f"mm XS {n} {lev}"))
                        add(f"TS {n} {lev}", four(mT))
                        add(f"XS {n} {lev}", by_head(XA))
                        T.mark(f"TX {n} {lev + 1}", *dve.last)
                    for o, mk in enumerate((m_o32, m_o64)):
                        dve.eng.wait_ge(*T.at(f"TX {n} {3 + o}"))
                        tt(four(mSt), four(mAt), bc4(mk), ALU.mult).then_inc(dve.tick(f"off {n} {o}"), 1)
                        dve.eng.wait_ge(*T.at(f"mm XQ {n} {o}"))
                        if o == 0:
                            add(f"TQ {n} {o}", four(mT))
                        add(f"XQ {n} {o}", by_head(XA))
                        T.mark(f"TX {n} {4 + o}", *dve.last)
                for cc in range(2):
                    c = 2 * a + cc
                    b0 = slice(64 * cc, 64 * cc + 64)
                    dve.eng.wait_ge(*T.at(f"mm P {c}"))
                    dve.eng.wait_ge(*T.at(f"ev ZV {a} 1"))
                    tt(Pm[b0, :], ps(f"P {c}")[b0, :], ZV[b0, :], ALU.add).then_inc(dve.tick(f"ev P {c}"), 1)
                    T.mark(f"P {c}", *dve.last)
                    if c < 3:
                        dve.eng.wait_ge(*T.at(f"mm S {c}"))
                        tt(Sbd, Sbd, ps(f"S {c}")[:, :], ALU.add).then_inc(dve.tick(f"ev S {c}"), 1)
                        dve.eng.wait_ge(*dve.own())
                        tt(four(Sbd), four(Sbd), bc4(m_d64), ALU.mult).then_inc(dve.tick(), 1)
                        dve.eng.wait_ge(*dve.own())
                        tt(four(Sbd), four(Sbd), eLC[:, :, c].unsqueeze(2).to_broadcast([P, 4, P]),
                                    ALU.mult).then_inc(dve.tick(f"S {c + 1}"), 1)
                dve.eng.wait_ge(*T.at(f"ev ys {a}"))
                dve.eng.wait_ge(*T.at(f"mm yu {a}"))
                o = yT[:, :, a * P:(a + 1) * P]
                tt(o, o, four(ps(f"yu {a}")[:, :]), ALU.add).then_inc(dve.tick(f"ev yu {a}"), 1)
                T.mark(f"y {a}", *dve.last)
            for j in range(2):
                o = yT[:, 2 * j:2 * j + 2, :].rearrange("p k t -> p (k t)")
                dve.eng.wait_ge(*T.at(f"mm gm {j}"))
                dve.eng.wait_ge(*T.at("mm gm 1"))
                stt(o, ps(f"gm {j}")[:, :], -1.0 / 64, o, ALU.mult, ALU.add).then_inc(dve.tick(f"ev gm {j}"), 1)
            T.mark("y centred", *dve.last)
            dve.eng.wait_ge(*T.at("y std"))
            nc.vector.reciprocal(GhF[:, 4:8, :], GhF[:, 4:8, :]).then_inc(dve.tick(), 1)
            dve.eng.wait_ge(*dve.own())
            tt(yT, yT, GhF[:, 4:8, :], ALU.mult).then_inc(dve.tick(), 1)
            dve.eng.wait_ge(*dve.own())
            for k in range(4):
                ts(yT[:, k, :], yT[:, k, :], col("gn_g_2", k), col("gn_b_2", k), ALU.mult, ALU.add).then_inc(dve.tick(), 1)
            dve.eng.wait_ge(*dve.own())
            tt(yT, yT, bonus, ALU.add).then_inc(dve.tick(), 1)
            dve.eng.wait_ge(*dve.own())
            tt(yT, yT, gg, ALU.mult).then_inc(dve.tick("y out"), 1)
            dve.eng.wait_ge(*T.at("Gh wb"))
            tt(Gh[:, 4:8, :], yT, Gh[:, 0:4, :].bitcast(F32), ALU.subtract).then_inc(dve.tick("Gl wb"), 1)

        def moe_pe(pe, m, H):
            mm, eng, nm = nc.tensor.matmul, pe.eng, m.name
            n_log = m.E + (m.groups if m.groups > 1 else 0)
            b = take(pe, nm + " logits")
            pe.eng.wait_ge(*T.at(f"{nm} router landed"))
            pe.eng.wait_ge(*T.at(f"Hf {nm}"))
            for a in range(TT):
                for k in range(KT):
                    last = mm(b[:, a * n_log:(a + 1) * n_log], H[:, k, a * P:(a + 1) * P], rw[:, k, 0:n_log],
                              start=(k == 0), stop=(k == KT - 1))
            last.then_inc(pe.tick(f"mm {nm} logits"), 1)
            for j in range(4):
                b = take(pe, f"{nm} tok {j}")
                for a in range(TT):
                    for k in range(2):
                        last = nc.tensor.transpose(b[:, (2 * a + k) * P:(2 * a + k + 1) * P],
                                                   H[:, 2 * j + k, a * P:(a + 1) * P], ident[:, :])
                last.then_inc(pe.tick(f"mm {nm} tok {j}"), 1)
            b = take(pe, nm + " count")
            pe.eng.wait_ge(*T.at(f"{nm} sel"))
            pe.eng.wait_ge(*T.at("routing constants"))
            sel = RT[:, 0, :, 0:m.E]
            mm(b[:, 0:m.E], before[:, :], sel[:, 0, :], start=True, stop=True)
            mm(b[:, m.E:2 * m.E], ones[:, :], sel[:, 0, :], start=True, stop=False)
            mm(b[:, m.E:2 * m.E], before[:, :], sel[:, 1, :], start=False, stop=True)
            for a in range(TT):
                last = mm(b[:, 2 * m.E:3 * m.E], ones[:, :], sel[:, a, :], start=(a == 0), stop=(a == 1))
            last.then_inc(pe.tick(f"mm {nm} count"), 1)
            for b_ in range(8):
                if T.occupant.get(b_):
                    pe.eng.wait_ge(*T.at("ev " + T.occupant[b_]))
                T.occupant[b_] = None

            S_ = lambda what: T.sem(f"{nm}_{what}")
            U, SB = m.first, split_before[m.first]

            def halves(g, i0, more=None):
                v = g * m.per + (SB + i0 + 1)
                if more is not None:
                    v = v + more
                eng.wait_ge(T.sem("hi_done"), v)
                eng.wait_ge(T.sem("lo_done"), v)
                s = (SB + i0) % SPLIT
                return ring_hi[:, s, :], ring_lo[:, s, :]

            def up(g, c, h, par, more=None, q=None):
                i0 = m.unit(c, h)
                if h == 0:
                    eng.wait_ge(S_("hidden"), q + 1)
                wh, wl = halves(g, i0, more)
                o = bank[(par + c) % 2][:, :]
                wh = wh.rearrange("p (k n) -> p k n", n=512)
                wl = wl.rearrange("p (k n) -> p k n", n=512)
                for k in range(4):
                    kk = 4 * h + k
                    mm(o, xg_hi[:, kk, :], wh[:, k, :], start=(kk == 0), stop=False)
                    mm(o, xg_lo[:, kk, :], wh[:, k, :], start=False, stop=False)
                    last = mm(o, xg_hi[:, kk, :], wl[:, k, :], start=False, stop=(kk == KT - 1))
                last.then_inc(T.sem("unit_done"), 1)

            def turn(c, par, q):
                eng.wait_ge(S_("hidden"), q + 3)
                for k in range(2):
                    last = nc.tensor.transpose(bank[2][:, k * P:(k + 1) * P],
                                               tC[:, 2 + (par + c) % 2, k * P:(k + 1) * P], ident[:, :])
                last.then_inc(S_("turned"), 1)

            def down(g, c, i0, more, q):
                wh, wl = halves(g, i0, more)
                eng.wait_ge(S_("turned_lo"), q + 1)
                wh = wh.rearrange("p (k n) -> p k n", n=D)
                wl = wl.rearrange("p (k n) -> p k n", n=D)
                end = isinstance(c, int) and c == m.NCH - 1
                for n in range(2):
                    o = bank[4 + n][:, :]
                    for k in range(2):
                        ns = slice(512 * n, 512 * n + 512)
                        first = isinstance(c, int) and c == 0 and k == 0
                        mm(o, mh_hi[:, k, :], wh[:, k, ns], start=first, stop=False, skip_group_check=True)
                        mm(o, mh_lo[:, k, :], wh[:, k, ns], start=False, stop=False, skip_group_check=True)
                        last = mm(o, mh_hi[:, k, :], wl[:, k, ns], start=False, stop=(end and k == 1),
                                  skip_group_check=True)
                last.then_inc(T.sem("unit_done"), 1)

            def gather(par, g):
                eng.wait_ge(S_("selected"), g + 1)
                for a in range(TT):
                    nc.tensor.transpose(bank[3][:, a * P:(a + 1) * P], pself[par][:, a, :], ident[:, :])
                for a in range(TT):
                    last = mm(bank[3][:, 2 * P:2 * P + m.G], pself[par][:, a, :], gateg[:, par, a, 0:m.G],
                              start=(a == 0), stop=(a == 1))
                last.then_inc(S_("sel_turned"), 1)
                for r in range(4):
                    src = tok_hi if r < 2 else tok_lo
                    if r == 2:
                        eng.wait_ge(S_("gathered_hi"), g * 2 + 2)
                    o = bank[6 + r % 2]
                    for k in range(4):
                        kk = 4 * (r % 2) + k
                        for a in range(TT):
                            last = mm(o[:, k * P:(k + 1) * P], src[:, a, kk * P:(kk + 1) * P], psel_r[:, a, :],
                                      start=(a == 0), stop=(a == 1))
                    last.then_inc(S_("gathering"), 1)

            def scatter(par, g):
                eng.wait_ge(S_("y"), g * 2 + 2)
                eng.wait_ge(S_("selT"), g + 1)
                for r in range(4):
                    if r < 2:
                        eng.wait_ge(S_("gathered_lo"), g * 2 + 2)
                    else:
                        eng.wait_ge(S_("scattered"), g * 4 + (r - 1))
                    o = bank[6 + r % 2]
                    for k in range(2):
                        kk = 2 * r + k
                        last = mm(o[:, k * S:(k + 1) * S], ysb[:, kk * P:(kk + 1) * P], pselT[par],
                                  start=True, stop=True)
                    last.then_inc(S_("scatter"), 1)

            pe.eng.wait_ge(*T.at(f"{nm} tok_hi"))
            pe.eng.wait_ge(*T.at(f"{nm} tok_lo"))
            pe.eng.wait_ge(*T.at(f"{nm} cleared"))
            gather(0, 0)
            with eng.Fori(0, m.NG // 2) as it:
                for par in range(2):
                    g = it * 2 + par
                    q0 = g * m.NCH
                    bp = (par * m.NCH) % 2
                    eng.wait_ge(S_("gathered_hi"), g * 2 + 2)
                    eng.wait_ge(S_("gathered_lo"), g * 2 + 2)
                    up(g, 0, 0, bp, q=q0)
                    scatter(1 - par, g)
                    up(g, 0, 1, bp)
                    for c in range(1, m.NCH):
                        if m.G == 1 and 2 <= c < m.NCH - 2:
                            continue
                        if m.G == 1 and c == m.NCH - 2:
                            with eng.Fori(0, (m.NCH - 4) // 2) as jt:
                                for d in range(2):
                                    qc = q0 + jt * 2
                                    up(g, 2 + d, 0, bp, jt * 6, q=qc + (2 + d))
                                    turn(1 + d, bp, qc + (1 + d))
                                    up(g, 2 + d, 1, bp, jt * 6)
                                    down(g, None, m.unit(1 + d, 2), jt * 6, qc + (1 + d))
                        up(g, c, 0, bp, q=q0 + c)
                        turn(c - 1, bp, q0 + (c - 1))
                        up(g, c, 1, bp)
                        down(g, c - 1, m.unit(c - 1, 2), None, q0 + (c - 1))
                    gather(1 - par, g + 1)
                    turn(m.NCH - 1, bp, q0 + (m.NCH - 1))
                    down(g, m.NCH - 1, m.per - 1, None, q0 + (m.NCH - 1))
            scatter(1, m.NG)
            T.mark(f"{nm} scatter", f"{nm}_scatter", 4 * (m.NG + 1))
            T.mark("ev moe", f"{nm}_scattered", 4 * (m.NG + 1))

        def moe_act(act, m):
            run, eng, nm = nc.scalar.activation, act.eng, m.name
            act.eng.wait_ge(*T.at(f"{nm} shifted"))
            for a in range(TT):
                run(RT[:, 1, a, 0:m.E], RT[:, 2, a, 0:m.E], ACT.Exp, bias=rmax[:, a, 1:2],
                             accum_out=rmax[:, a, 2:3]).then_inc(act.tick(f"{nm} exps"), 1)
            if m.groups > 1:
                for a in range(TT):
                    run(RT[:, 3, a, 0:m.groups], RT[:, 4, a, 0:m.groups], ACT.Exp,
                                 bias=rmax[:, a, 4:5], accum_out=rmax[:, a, 5:6]).then_inc(act.tick(f"{nm} exps"), 1)
            for j in range(4):
                act.eng.wait_ge(*T.at(f"mm {nm} tok {j}"))
                run(tok_hi[:, :, 256 * j:256 * j + 256],
                             bank_view(ps(f"{nm} tok {j}")), ACT.Copy).then_inc(act.tick(f"{nm} tok_hi {j}"), 1)
            T.mark(f"{nm} tok_hi", *act.last)
            S_ = lambda what: T.sem(f"{nm}_{what}")
            U, SB = m.first, split_before[m.first]

            def hi(g, i0, more=None):
                r, s = (U + i0) % RAW, (SB + i0) % SPLIT
                v = g * (32 * m.per // RAW) + 32 * ((U + i0) // RAW + 1)
                if more is not None:
                    v = v + more * 32
                eng.wait_ge(raw_landed[r], v)
                v = g * m.per + (U + i0 - SPLIT + 1)
                if more is not None:
                    v = v + more * 6
                eng.wait_ge(T.sem("unit_done"), v)
                run(ring_hi[:, s, :], ring_raw[:, r, :], ACT.Copy).then_inc(T.sem("hi_done"), 1)

            def silu(c, bp, q):
                eng.wait_ge(T.sem("unit_done"), q)
                run(tC[:, (bp + c) % 2, :], bank[(bp + c) % 2][:, 0:256], ACT.Silu).then_inc(S_("silu"), 1)

            def turned(q):
                eng.wait_ge(S_("turned"), q + 1)
                run(mh_hi, bank[2][:, 0:256].rearrange("p (k s) -> p k s", k=2), ACT.Copy)\
                    .then_inc(S_("turned_hi"), 1)

            def gathered(par, g):
                eng.wait_ge(S_("sel_turned"), g + 1)
                run(pselT[par], bank[3][:, 0:2 * P], ACT.Copy).then_inc(S_("selT"), 1)
                for r in range(2):
                    eng.wait_ge(S_("gathering"), g * 4 + (r + 1))
                    run(xg_hi[:, 4 * r:4 * r + 4, :], bank[6 + r][:, :].rearrange("p (k s) -> p k s", k=4),
                        ACT.Copy).then_inc(S_("gathered_hi"), 1)

            hi(0, 0)
            act.eng.wait_ge(*T.at(f"{nm} cleared"))
            gathered(0, 0)
            hi(0, 1)
            with eng.Fori(0, m.NG // 2) as it:
                for par in range(2):
                    g = it * 2 + par
                    q0 = g * m.NCH
                    bp = (par * m.NCH) % 2
                    ud = lambda i0: g * m.per + (U + i0 + 1)
                    hi(g, m.unit(1, 0))
                    silu(0, bp, ud(1))
                    hi(g, m.unit(1, 1))
                    for c in range(1, m.NCH):
                        if m.G == 1 and 2 <= c < m.NCH - 2:
                            continue
                        if m.G == 1 and c == m.NCH - 2:
                            with eng.Fori(0, (m.NCH - 4) // 2) as jt:
                                for d in range(2):
                                    hi(g, m.unit(1 + d, 2), jt)
                                    turned(q0 + jt * 2 + (1 + d))
                                    hi(g, m.unit(3 + d, 0), jt)
                                    silu(2 + d, bp, ud(m.unit(2 + d, 1)) + jt * 6)
                                    hi(g, m.unit(3 + d, 1), jt)
                        hi(g, m.unit(c - 1, 2))
                        turned(q0 + (c - 1))
                        if c < m.NCH - 1:
                            hi(g, m.unit(c + 1, 0))
                            silu(c, bp, ud(m.unit(c, 1)))
                            hi(g, m.unit(c + 1, 1))
                        else:
                            hi(g, m.per - 1)
                            silu(c, bp, ud(m.unit(c, 1)))
                            gathered(1 - par, g + 1)
                            turned(q0 + c)
                            hi(g, m.per)
                            eng.wait_ge(T.sem("unit_done"), ud(m.per - 1))
                            for n in range(2):
                                if n == 0:
                                    eng.wait_ge(S_("scatter"), g * 4 + 4)
                                run(ysb[:, 512 * n:512 * n + 512], bank[4 + n][:, :], ACT.Copy)\
                                    .then_inc(S_("y"), 1)
                            hi(g, m.per + 1)
            nxt["act"] = m.first + m.units + 2

        def bank_view(b):
            return b[:, :].rearrange("p (a c) -> p a c", a=TT)

        def moe_dve(dve, m):
            tt, ts, stt = nc.vector.tensor_tensor, nc.vector.tensor_scalar, nc.vector.scalar_tensor_tensor
            eng, nm, E = dve.eng, m.name, m.E
            R = m.groups
            n_log = E + (R if R > 1 else 0)
            L, sel, sh = RT[:, 5, :, :], RT[:, 0, :, :], RT[:, 2, :, :]
            dve.eng.wait_ge(*T.at(f"mm {nm} logits"))
            lg = ps(f"{nm} logits")
            for a in range(TT):
                tt(L[:, a, 0:E], lg[:, a * n_log:a * n_log + E], rbias[:, 0:E], ALU.add).then_inc(dve.tick(), 1)
                if R > 1:
                    tt(RT[:, 4, a, 0:R], lg[:, a * n_log + E:(a + 1) * n_log], rbias[:, E:E + R], ALU.add).then_inc(dve.tick(), 1)
            T.mark(f"ev {nm} logits", *dve.last)
            dve.eng.wait_ge(*dve.own())
            dve.eng.wait_ge(*T.at("routing constants"))

            def rank(src, n, k, dst):
                shape = [P, k, n, n]
                v = src.rearrange("p (g e) -> p g e", g=k)
                other, own = v.unsqueeze(2).to_broadcast(shape), v.unsqueeze(3).to_broadcast(shape)
                w1 = tC[:, 4, 0:k * n * n].rearrange("p (g e j) -> p g e j", g=k, e=n)
                w2 = tC[:, 5, 0:k * n * n].rearrange("p (g e j) -> p g e j", g=k, e=n)
                tt(w1, other, own, ALU.is_equal).then_inc(dve.tick(), 1)
                tt(w2, other, own, ALU.is_gt).then_inc(dve.tick(), 1)
                dve.eng.wait_ge(*dve.own())
                tt(w1, w1, lower[:, 0:n, 0:n].unsqueeze(1).to_broadcast(shape), ALU.mult).then_inc(dve.tick(), 1)
                dve.eng.wait_ge(*dve.own())
                tt(w1, w1, w2, ALU.add).then_inc(dve.tick(), 1)
                dve.eng.wait_ge(*dve.own())
                nc.vector.tensor_reduce(dst, w1.rearrange("p g e j -> p (g e) j"), AX, ALU.add).then_inc(dve.tick(), 1)
                dve.eng.wait_ge(*dve.own())

            for a in range(TT):
                rank(L[:, a, 0:E], 8, R, sel[:, a, 0:E])
                ts(sel[:, a, 0:E], sel[:, a, 0:E], 1.5, None, ALU.is_lt).then_inc(dve.tick(), 1)
                dve.eng.wait_ge(*dve.own())
                if R > 1:
                    rank(RT[:, 4, a, 0:R], R, 1, RT[:, 6, a, 0:R])
                    ts(RT[:, 6, a, 0:R], RT[:, 6, a, 0:R], 0.5, None, ALU.is_lt).then_inc(dve.tick(), 1)
                    dve.eng.wait_ge(*dve.own())
                    s3 = sel[:, a, 0:E].rearrange("p (g e) -> p g e", g=R)
                    tt(s3, s3, RT[:, 6, a, 0:R].unsqueeze(2).to_broadcast([P, R, 8]), ALU.mult).then_inc(dve.tick(), 1)
                    dve.eng.wait_ge(*dve.own())
                T.mark(f"{nm} sel", *dve.last)
            for a in range(TT):
                ts(sh[:, a, 0:E], sel[:, a, 0:E], -NEG, NEG, ALU.mult, ALU.add).then_inc(dve.tick(), 1)
                dve.eng.wait_ge(*dve.own())
                tt(sh[:, a, 0:E], sh[:, a, 0:E], L[:, a, 0:E], ALU.add).then_inc(dve.tick(), 1)
                dve.eng.wait_ge(*dve.own())
                nc.vector.tensor_reduce(rmax[:, a, 1:2], sh[:, a, 0:E], AX, ALU.max, negate=True).then_inc(dve.tick(), 1)
                if R > 1:
                    nc.vector.tensor_reduce(rmax[:, a, 4:5], RT[:, 4, a, 0:R], AX, ALU.max, negate=True).then_inc(dve.tick(), 1)
            T.mark(f"{nm} shifted", *dve.last)
            for j in range(4):
                dve.eng.wait_ge(*T.at(f"{nm} tok_hi {j}"))
                cs = slice(256 * j, 256 * j + 256)
                tt(tok_lo[:, :, cs], bank_view(ps(f"{nm} tok {j}")), tok_hi[:, :, cs].bitcast(F32),
                            ALU.subtract).then_inc(dve.tick(f"ev {nm} tok {j}"), 1)
            T.mark(f"{nm} tok_lo", *dve.last)
            dve.eng.wait_ge(*T.at(f"mm {nm} count"))
            cb = ps(f"{nm} count")
            cum, tot, off = RT[:, 7, :, :], RT[:, 8, 0, :], RT[:, 8, 1, :]
            nc.vector.tensor_copy(cum[:, :, 0:E], cb[:, 0:2 * E].rearrange("p (a e) -> p a e", a=TT)).then_inc(dve.tick(), 1)
            nc.vector.tensor_copy(tot[:, 0:E], cb[:, 2 * E:3 * E]).then_inc(dve.tick(f"ev {nm} count"), 1)
            nc.vector.memset(off[:, 0:E], 0.0).then_inc(dve.tick(), 1)
            nc.vector.memset(pos[:, :, :, :], -1.0).then_inc(dve.tick(), 1)
            nc.vector.memset(gates[:, :, :, :], 0.0).then_inc(dve.tick(), 1)
            nc.vector.memset(mask[:, :, :], 0.0).then_inc(dve.tick(), 1)
            dve.eng.wait_ge(*dve.own())
            o3 = off[:, 0:E].rearrange("p (g i) -> p g i", i=m.G)
            t3 = tot[:, 0:E].rearrange("p (g i) -> p g i", i=m.G)
            for i in range(1, m.G):
                tt(o3[:, :, i], o3[:, :, i - 1], t3[:, :, i - 1], ALU.add).then_inc(dve.tick(), 1)
                dve.eng.wait_ge(*dve.own())
            lo_, hi_ = RT[:, 9, 0, 0:E], RT[:, 9, 1, 0:E]
            tt(hi_, off[:, 0:E], tot[:, 0:E], ALU.add).then_inc(dve.tick(), 1)
            dve.eng.wait_ge(*dve.own())
            nc.vector.tensor_reduce(most[:, 0:1], hi_, AX, ALU.max).then_inc(dve.tick(), 1)
            dve.eng.wait_ge(*dve.own())
            nc.vector.tensor_copy(overflow[:, :], most[:, 0:1]).then_inc(dve.tick(f"{nm} overflow"), 1)
            tt(lo_, off[:, 0:E], part[:, 0:1].to_broadcast([P, E]), ALU.is_le).then_inc(dve.tick(), 1)
            dve.eng.wait_ge(*dve.own())
            tt(hi_, hi_, part[:, 0:1].to_broadcast([P, E]), ALU.is_gt).then_inc(dve.tick(), 1)
            dve.eng.wait_ge(*dve.own())
            tt(mask[:, 0:m.NG, 0:m.G], lo_.rearrange("p (g i) -> p g i", i=m.G),
                        hi_.rearrange("p (g i) -> p g i", i=m.G), ALU.mult).then_inc(dve.tick(), 1)
            for a in range(TT):
                c = cum[:, a, 0:E]
                stt(c, c, 1.0, off[:, 0:E], ALU.add, ALU.add).then_inc(dve.tick(), 1)
                dve.eng.wait_ge(*dve.own())
                tt(c, c, sel[:, a, 0:E], ALU.mult).then_inc(dve.tick(), 1)
                dve.eng.wait_ge(*dve.own())
                ts(pos[:, 0:m.NG, a, 0:m.G], c.rearrange("p (g i) -> p g i", i=m.G), -1.0, None, ALU.add).then_inc(dve.tick(), 1)
            dve.eng.wait_ge(*T.at(f"{nm} exps"))
            for a in range(TT):
                nc.vector.reciprocal(rmax[:, a, 3:4], rmax[:, a, 2:3]).then_inc(dve.tick(), 1)
                if R > 1:
                    nc.vector.reciprocal(rmax[:, a, 6:7], rmax[:, a, 5:6]).then_inc(dve.tick(), 1)
                    dve.eng.wait_ge(*dve.own())
                    tt(rmax[:, a, 3:4], rmax[:, a, 3:4], rmax[:, a, 6:7], ALU.mult).then_inc(dve.tick(), 1)
                dve.eng.wait_ge(*dve.own())
                ts(gates[:, 0:m.NG, a, 0:m.G], RT[:, 1, a, 0:E].rearrange("p (g i) -> p g i", i=m.G),
                            rmax[:, a, 3:4], None, ALU.mult).then_inc(dve.tick(), 1)
            S_ = lambda what: T.sem(f"{nm}_{what}")
            U, SB = m.first, split_before[m.first]
            nc.vector.memset(tB[:, :, :], 0.0).then_inc(dve.tick(), 1)
            nc.vector.memset(pselT[1], 0.0).then_inc(dve.tick(), 1)
            nc.vector.memset(ysb, 0.0).then_inc(dve.tick(f"{nm} cleared"), 1)
            nc.vector.memset(tC[:, 2, :], 0.0).then_inc(S_("hidden"), 1)
            nc.vector.memset(tC[:, 3, :], 0.0).then_inc(S_("hidden"), 1)
            nc.vector.memset(ge[:, 0, :], 0.0).then_inc(S_("y"), 1)
            nc.vector.memset(ge[:, 1, :], 0.0).then_inc(S_("y"), 1)

            def lo(g, i0, more=None):
                r, s = (U + i0) % RAW, (SB + i0) % SPLIT
                v = g * m.per + (SB + i0 + 1)
                if more is not None:
                    v = v + more * 6
                eng.wait_ge(T.sem("hi_done"), v)
                tt(ring_lo[:, s, :], ring_raw[:, r, :], ring_hi[:, s, :].bitcast(F32),
                   ALU.subtract).then_inc(T.sem("lo_done"), 1)

            def hidden(c, bp, par, q):
                eng.wait_ge(S_("silu"), q + 1)
                i = 0 if m.G == 1 else c
                stt(tC[:, 2 + (bp + c) % 2, :], tC[:, (bp + c) % 2, :], ge[:, par, i:i + 1],
                    bank[(bp + c) % 2][:, 256:512], ALU.mult, ALU.mult).then_inc(S_("hidden"), 1)

            def turned(q):
                eng.wait_ge(S_("turned_hi"), q + 1)
                tt(mh_lo, bank[2][:, 0:256].rearrange("p (k s) -> p k s", k=2), mh_hi.bitcast(F32),
                   ALU.subtract).then_inc(S_("turned_lo"), 1)

            def select(par, g):
                steps = 3 + TT * m.G + 1
                n = [0]

                def step(ins):
                    n[0] += 1
                    ins.then_inc(S_("step"), 1)
                    eng.wait_ge(S_("step"), g * steps + n[0])

                step(nc.vector.tensor_copy(posg[:, :, 0:m.G], pos[:, bass.ds(g, 1), :, 0:m.G]
                                           .rearrange("p o a i -> p (o a) i")))
                step(nc.vector.tensor_copy(gateg[:, par, :, 0:m.G], gates[:, bass.ds(g, 1), :, 0:m.G]
                                           .rearrange("p o a i -> p (o a) i")))
                step(nc.vector.tensor_copy(maskg[:, par, 0:m.G], mask[:, bass.ds(g, 1), 0:m.G]
                                           .rearrange("p o i -> p (o i)")))
                for i in range(m.G):
                    for a in range(TT):
                        o = pself[par][:, a, :]
                        if i == 0:
                            step(ts(o, slots[:, :], posg[:, a, 0:1], None, ALU.is_equal))
                        else:
                            step(stt(o, slots[:, :], posg[:, a, i:i + 1], o, ALU.is_equal, ALU.add))
                step(nc.vector.tensor_copy(psel_r[:, :, :], pself[par]))
                nc.vector.tensor_copy(small[:, 0, 0:1], part[:, 0:1]).then_inc(S_("selected"), 1)

            def gathered(par, g):
                eng.wait_ge(S_("selT"), g + 1)
                tt(ge[:, par, 0:m.G], bank[3][:, 2 * P:2 * P + m.G], maskg[:, par, 0:m.G], ALU.mult)\
                    .then_inc(S_("gate"), 1)
                for r in range(2):
                    eng.wait_ge(S_("gathering"), g * 4 + (r + 3))
                    nc.vector.tensor_copy(xg_lo[:, 4 * r:4 * r + 4, :],
                                          bank[6 + r][:, :].rearrange("p (k s) -> p k s", k=4))\
                        .then_inc(S_("gathered_lo"), 1)
                eng.wait_ge(S_("gate"), g + 1)

            def scattered(g):
                for r in range(4):
                    eng.wait_ge(S_("scatter"), g * 4 + (r + 1))
                    o = tB[:, 2 * r:2 * r + 2, :]
                    tt(o, o, bank[6 + r % 2][:, :].rearrange("p (k t) -> p k t", k=2), ALU.add)\
                        .then_inc(S_("scattered"), 1)

            dve.eng.wait_ge(*dve.own())
            select(0, 0)
            lo(0, 0)
            gathered(0, 0)
            lo(0, 1)
            with eng.Fori(0, m.NG // 2) as it:
                for par in range(2):
                    g = it * 2 + par
                    q0 = g * m.NCH
                    bp = (par * m.NCH) % 2
                    lo(g, m.unit(1, 0))
                    scattered(g)
                    hidden(0, bp, par, q0)
                    lo(g, m.unit(1, 1))
                    for c in range(1, m.NCH):
                        if m.G == 1 and 2 <= c < m.NCH - 2:
                            continue
                        if m.G == 1 and c == m.NCH - 2:
                            with eng.Fori(0, (m.NCH - 4) // 2) as jt:
                                for d in range(2):
                                    qc = q0 + jt * 2
                                    lo(g, m.unit(1 + d, 2), jt)
                                    turned(qc + (1 + d))
                                    lo(g, m.unit(3 + d, 0), jt)
                                    hidden(2 + d, bp, par, qc + (2 + d))
                                    lo(g, m.unit(3 + d, 1), jt)
                        lo(g, m.unit(c - 1, 2))
                        turned(q0 + (c - 1))
                        if c < m.NCH - 1:
                            lo(g, m.unit(c + 1, 0))
                            hidden(c, bp, par, q0 + c)
                            lo(g, m.unit(c + 1, 1))
                        else:
                            lo(g, m.per - 1)
                            select(1 - par, g + 1)
                            hidden(c, bp, par, q0 + c)
                            gathered(1 - par, g + 1)
                            turned(q0 + c)
                            lo(g, m.per)
                            lo(g, m.per + 1)
            scattered(m.NG)
            T.mark(f"{nm} done", f"{nm}_scattered", 4 * (m.NG + 1))
            nxt["dve"] = m.first + m.units + 2

        rest_w = scr[:, :, :]
        rest_down = scr[:, :, :].rearrange("p (k j) t -> p k (j t)", k=2)
        rest_gates = tC[:, 6, :].rearrange("p (a e) -> p a e", a=TT)
        rest_col = tC[:, 7, :].rearrange("p (a m) -> p a m", a=TT)
        rest_h = tC[:, 0:2, :]

        def rest_chunks(eng, m):
            per = m.NCH // m.G
            return per, m.E * per

        def when_full(engine, m):
            engine.eng.wait_ge(*T.at(f"{m.name} overflow"))
            return engine.eng.If(engine.eng.value_load(overflow[0:1, 0:1], min_val=0, max_val=4 * S) > SLOTS)

        def rest_sp(sp, m, w_gate, w_up, w_down):
            eng, R = sp.eng, lambda what: T.sem(f"{m.name}_rest_{what}")
            per, total = rest_chunks(eng, m)
            with when_full(sp, m):
                with eng.Fori(0, m.E) as e:
                    with eng.Fori(0, per) as c:
                        n = e * per + c
                        eng.wait_ge(R("dve"), n * 7 + 1)
                        for h in range(2):
                            eng.dma_start(rest_w[:, 4 * h:4 * h + 4, :], w_gate(e, slice(512 * h, 512 * h + 512), c))\
                               .then_inc(R("load"), 16)
                        eng.wait_ge(R("pe"), n * 4 + 2)
                        for h in range(2):
                            eng.dma_start(rest_w[:, 4 * h:4 * h + 4, :], w_up(e, slice(512 * h, 512 * h + 512), c))\
                               .then_inc(R("load"), 16)
                        eng.wait_ge(R("pe"), n * 4 + 3)
                        for k in range(2):
                            eng.dma_start(rest_down[:, k:k + 1, :], w_down(e, c, k)).then_inc(R("load"), 16)

        def rest_pe(pe, m, H):
            mm, eng, R = nc.tensor.matmul, pe.eng, lambda what: T.sem(f"{m.name}_rest_{what}")
            per, total = rest_chunks(eng, m)
            with when_full(pe, m):
                with eng.Fori(0, total) as n:
                    eng.wait_ge(R("dve"), n * 7 + 1)
                    for a in range(TT):
                        last = mm(bank[2][:, a * P:(a + 1) * P], rest_col[:, a, :], ident[:, :], start=True, stop=True)
                    last.then_inc(R("pe"), 1)
                    for what in range(2):
                        eng.wait_ge(R("load"), n * 96 + 32 * (what + 1))
                        for b in range(2):
                            for k in range(KT):
                                last = mm(bank[what][:, b * S:(b + 1) * S], rest_w[:, k, b * P:(b + 1) * P],
                                          H[:, k, :], start=(k == 0), stop=(k == KT - 1))
                        last.then_inc(R("pe"), 1)
                    eng.wait_ge(R("load"), n * 96 + 96)
                    eng.wait_ge(R("dve"), n * 7 + 3)
                    for cb in range(KT):
                        for k in range(2):
                            last = mm(bank[4 + cb // 2][:, (cb % 2) * S:(cb % 2 + 1) * S],
                                      rest_down[:, k, cb * P:(cb + 1) * P], rest_h[:, k, :],
                                      start=(k == 0), stop=(k == 1))
                    last.then_inc(R("pe"), 1)
                eng.wait_ge(R("dve"), total * 7)

        def rest_act(act, m):
            eng, R = act.eng, lambda what: T.sem(f"{m.name}_rest_{what}")
            per, total = rest_chunks(eng, m)
            with when_full(act, m):
                with eng.Fori(0, total) as n:
                    eng.wait_ge(R("pe"), n * 4 + 2)
                    nc.scalar.activation(rest_h, bank[0][:, :].rearrange("p (k t) -> p k t", k=2), ACT.Silu)\
                        .then_inc(R("act"), 1)
                eng.wait_ge(R("dve"), total * 7)

        def rest_dve(dve, m):
            tt, eng, R = nc.vector.tensor_tensor, dve.eng, lambda what: T.sem(f"{m.name}_rest_{what}")
            per, total = rest_chunks(eng, m)
            dve.eng.wait_ge(*T.at(f"{m.name} done"))
            with when_full(dve, m):
                for a in range(TT):
                    nc.vector.scalar_tensor_tensor(
                        rest_gates[:, a, 0:m.E].rearrange("p (g i) -> p g i", i=m.G), pos[:, 0:m.NG, a, 0:m.G],
                        SLOTS - 0.5, gates[:, 0:m.NG, a, 0:m.G], ALU.is_ge, ALU.mult).then_inc(R("gates"), 1)
                eng.wait_ge(R("gates"), TT)
                with eng.Fori(0, m.E) as e:
                    with eng.Fori(0, per) as c:
                        n = e * per + c
                        nc.vector.tensor_copy(rest_col, rest_gates[:, :, bass.ds(e, 1)].to_broadcast([P, TT, P]))\
                            .then_inc(R("dve"), 1)
                        eng.wait_ge(R("act"), n + 1)
                        eng.wait_ge(R("pe"), n * 4 + 3)
                        tt(rest_h, rest_h, bank[1][:, :].rearrange("p (k t) -> p k t", k=2), ALU.mult)\
                            .then_inc(R("dve"), 1)
                        eng.wait_ge(R("dve"), n * 7 + 2)
                        tt(rest_h, rest_h, bank[2][:, 0:S].unsqueeze(1).to_broadcast([P, 2, S]), ALU.mult)\
                            .then_inc(R("dve"), 1)
                        eng.wait_ge(R("pe"), n * 4 + 4)
                        for j in range(4):
                            o = tB[:, 2 * j:2 * j + 2, :]
                            tt(o, o, bank[4 + j][:, :].rearrange("p (k t) -> p k t", k=2), ALU.add)\
                                .then_inc(R("dve"), 1)
                        eng.wait_ge(R("dve"), n * 7 + 7)

        def softmax_exp(act, name, heads, dst):
            run = nc.scalar.activation
            for i in range(heads + 3):
                if i < heads:
                    h = i
                    act.eng.wait_ge(*T.at(f"{name} max {h}"))
                    sm = small[:, h % 3, :]
                    run(pr[:, h % 3, 0:P], pr[:, h % 3, 0:P], ACT.Exp, bias=sm[:, 0:1],
                                 accum_out=sm[:, 2:3]).then_inc(act.tick(), 1)
                    run(pr[:, h % 3, P:3 * P], pr[:, h % 3, P:3 * P], ACT.Exp, bias=sm[:, 1:2],
                                 accum_out=sm[:, 3:4]).then_inc(act.tick(f"{name} exp {h}"), 1)
                if 2 <= i < heads + 2:
                    h = i - 2
                    act.eng.wait_ge(*T.at(f"mm {name} pT {h}"))
                    if h >= 3:
                        act.eng.wait_ge(*T.at(f"mm {name} o {h - 3}"))
                    run(prT[:, h % 3, :], ps(f"{name} pT {h}")[:, 0:3 * P], ACT.Copy).then_inc(act.tick(f"ev {name} pT {h}"), 1)
                    T.mark(f"{name} pT {h}", *act.last)
                if i >= 3 and (i - 3) % 2 == 1:
                    k = (i - 3) // 2
                    act.eng.wait_ge(*T.at(f"mm {name} o {2 * k + 1}"))
                    run(dst[:, k, :], ps(f"{name} o {k}")[:, 0:S], ACT.Copy).then_inc(act.tick(f"hi {name} o {k}"), 1)

        def softmax_rest(dve, name, heads, bias, lo, hi):
            tt, ts, stt = nc.vector.tensor_tensor, nc.vector.tensor_scalar, nc.vector.scalar_tensor_tensor
            dve.eng.wait_ge(*T.at("alibi"))
            for i in range(heads + 5):
                if i < heads:
                    h = i
                    dve.eng.wait_ge(*T.at(f"mm {name} s {h}"))
                    if h >= 3:
                        dve.eng.wait_ge(*T.at(f"mm {name} pT {h - 3}"))
                    b, sm = ps(f"{name} s {h}"), small[:, h % 3, :]
                    for c0, w in ((0, P), (P, 2 * P)):
                        tab, slope = bias(h, c0, w)
                        o, s = pr[:, h % 3, c0:c0 + w], b[:, c0:c0 + w]
                        if slope is None:
                            tt(o, s, tab, ALU.add).then_inc(dve.tick(f"ev {name} s {h}"), 1)
                        else:
                            stt(o, tab, slope, s, ALU.mult, ALU.add).then_inc(dve.tick(f"ev {name} s {h}"), 1)
                    dve.eng.wait_ge(*dve.own())
                    for m, (c0, w) in enumerate(((0, P), (P, 2 * P))):
                        nc.vector.tensor_reduce(sm[:, m:m + 1], pr[:, h % 3, c0:c0 + w], AX, ALU.max,
                                                         negate=True).then_inc(dve.tick(f"{name} max {h}"), 1)
                if 1 <= i < heads + 1:
                    h = i - 1
                    sm = small[:, h % 3, :]
                    dve.eng.wait_ge(*T.at(f"{name} exp {h}"))
                    nc.vector.reciprocal(sm[:, 4:6], sm[:, 2:4]).then_inc(dve.tick(), 1)
                    dve.eng.wait_ge(*dve.own())
                    for m, (c0, w) in enumerate(((0, P), (P, 2 * P))):
                        o = pr[:, h % 3, c0:c0 + w]
                        ts(o, o, sm[:, 4 + m:5 + m], None, ALU.mult).then_inc(dve.tick(f"{name} p {h}"), 1)
                if i >= 5 and (i - 5) % 2 == 1:
                    k = (i - 5) // 2
                    dve.eng.wait_ge(*T.at(f"hi {name} o {k}"))
                    tt(lo[:, k, :], ps(f"{name} o {k}")[:, 0:S], hi[:, k, :].bitcast(F32),
                                ALU.subtract).then_inc(dve.tick(f"ev {name} o {k}"), 1)


        block = ctx.enter_context(nc.Block())

        @block.sync
        def _(eng):
            sp = Engine(T, eng, "sp")

            def small_load(label, dst, src):
                eng.dma_start(dst, src).then_inc(T.sem(label), 16)
                T.count[label] = T.count.get(label, 0) + 16
                T.mark(label, label, T.count[label])

            rows = tA[:, 0:4, :].rearrange("p k t -> p (k t)")
            sp.eng.wait_ge(*T.at("rows cleared"))
            flat = lambda ap: ap
            sources = [
                ("conv_dw_w", A["conv_dw_w"][0], TAPS, D), ("conv_dw_b", A["conv_dw_b"], 1, D),
                ("conv_norm_g", A["conv_norm_g"], 1, D), ("conv_norm_b", A["conv_norm_b"], 1, D),
                ("conv_out_b", A["conv_out_b"], 1, D),
                ("conv_in_b", A["conv_in_b"].rearrange("a (r d) -> (a r) d", d=D), 2, D),
                ("ada_b", A["ada_b"].rearrange("a (r d) -> (a r) d", d=D), 12, D),
                ("kv_ada_b", A["kv_ada_b"].rearrange("(r d) -> r d", d=D), 2, D),
                ("ln_g", A["ln_g"].rearrange("a b d -> (a b) d"), 4, D),
                ("ln_b", A["ln_b"].rearrange("a b d -> (a b) d"), 4, D),
                ("ln_in_g_2", A["ln_in_g_2"].rearrange("(r d) -> r d", r=1), 1, D),
                ("ln_in_b_2", A["ln_in_b_2"].rearrange("(r d) -> r d", r=1), 1, D),
                ("ln_g_2", A["ln_g_2"][0], 3, D), ("ln_b_2", A["ln_b_2"][0], 3, D),
                ("c", A["c"], 1, D),
                ("tok_mix_2", A["tok_mix_2"][:, 0:D], 1, D),
            ]
            for name, src, n, width in sources:
                r = ROW[name]
                small_load("rows landed", rows[r:r + n, 0:width], src)
            r = ROW["tok_mix_2"] + 1
            rest = A["tok_mix_2"].shape[1] - D
            small_load("rows landed", rows[r:r + 1, 0:rest], A["tok_mix_2"][:, D:D + rest])
            small_load("rows landed", rows[r + 1:r + 2, 0:P], A["tok_mix_2"][:, D + rest - P:D + rest])
            for name in ("decay_base_2", "aaa_base_2", "k_k_2", "k_a_2", "gn_g_2", "gn_b_2"):
                r = ROW[name]
                small_load("rows landed", rows[r:r + 1, 0:512], A[name])
            r = ROW["r_k_2"]
            small_load("rows landed", rows[r:r + 1, 0:512], A["r_k_2"].rearrange("a h d -> a (h d)"))
            x_in = tB[:, :, :].rearrange("p (a k) t -> p a (k t)", a=TT)
            small_load("x landed", x_in, A["x"][0].rearrange("(a p) d -> p a d", p=P))

            small_load("m1 router landed", rw[:, :, 0:8], A["router_w"][0].rearrange("(k p) n -> p k n", p=P))
            small_load("m1 router landed", rbias[:, 0:8], A["router_b"].to_broadcast([P, 8]))

            def moe_load(m, w_gate, w_up, w_down):
                base, sbase = m.first, split_before[m.first]

                def load(i, g, parts):
                    i0, more = i if isinstance(i, tuple) else (i, None)
                    slot = (base + i0) % RAW
                    done = g * m.per + (sbase + i0 - RAW + 1)
                    if more is not None:
                        done = done + more
                    eng.wait_ge(T.sem("hi_done"), done)
                    eng.wait_ge(T.sem("lo_done"), done)
                    for dst, src in parts:
                        eng.dma_start(dst, src).then_inc(raw_landed[slot], 16)

                def columns(i, g, e, c, h):
                    i0 = i[0] if isinstance(i, tuple) else i
                    v = view(ring_raw, (base + i0) % RAW, KT // 2, 512)
                    r = slice(h * 512, (h + 1) * 512)
                    load(i, g, [(v[:, :, 0:256], w_gate(e, r, c)), (v[:, :, 256:512], w_up(e, r, c))])

                def rows(i, g, e, c):
                    i0 = i[0] if isinstance(i, tuple) else i
                    v = view(ring_raw, (base + i0) % RAW, 2, D)
                    load(i, g, [(v[:, k:k + 1, :], w_down(e, c, k)) for k in range(2)])

                with eng.Fori(0, m.NG // 2) as it:
                    for par in range(2):
                        g = it * 2 + par
                        ec = (lambda c: (g, c)) if m.G == 1 else (lambda c: (g * m.G + c, 0))
                        for h in range(2):
                            columns(h, g, *ec(0), h)
                        for c in range(1, m.NCH):
                            if m.G == 1 and 2 <= c < m.NCH - 2:
                                continue
                            if m.G == 1 and c == m.NCH - 2:
                                with eng.Fori(0, (m.NCH - 4) // 2) as jt:
                                    for q in range(2):
                                        cc = jt * 2 + (2 + q)
                                        for h in range(2):
                                            columns((m.unit(2 + q, h), jt * 6), g, g, cc, h)
                                        rows((m.unit(1 + q, 2), jt * 6), g, g, jt * 2 + (1 + q))
                            for h in range(2):
                                columns(m.unit(c, h), g, *ec(c), h)
                            rows(m.unit(c - 1, 2), g, *ec(c - 1))
                        rows(m.per - 1, g, *ec(m.NCH - 1))

            def m1_w(half):
                w = A["moe_w13"][0]
                return lambda e, r, c: w[bass.ds(e, 1), r, bass.ds(c * 256 + half * m1.f, 256)]\
                    .rearrange("a (k p) n -> p (a k) n", p=P)

            def m1_down(e, c, k):
                return A["moe_w2"][0][bass.ds(e, 1), bass.ds(c * 256 + k * P, P), :].rearrange("a p n -> p a n")

            def m2_w(name):
                w = A[name][0]
                return lambda e, r, c: w[bass.ds(e, 1), r, :].rearrange("a (k p) n -> p (a k) n", p=P)

            def m2_down(e, c, k):
                return A["exp_down_2"][0][bass.ds(e, 1), k * P:(k + 1) * P, :].rearrange("a p n -> p a n")

            def second_small():
                sp.eng.wait_ge(*T.at("shifted"))
                n_rel = A["rel_bias_2"].shape[1]
                rb = A["rel_bias_2"]
                back = bass.AP(rb.tensor, rb.offset + n_rel - 1, [[n_rel, HEADS2], [-1, n_rel]])
                with nc.allow_non_contiguous_dma(reason="a small table, read backwards"):
                    small_load("rel landed", rel[:, P - 1:P - 1 + n_rel], back)
                sp.eng.wait_ge(*T.at("rel ready"))
                for h in range(HEADS2):
                    row = rel[h:h + 1, :]
                    src = bass.AP(row.tensor, row.offset + P - 1, [list(row.ap[0]), [-1, P], [1, S]])
                    small_load("bias landed", relb[:, h, :], src)
                small_load("lora landed", du[0:64, :], A["decay_up_2"][0])
                small_load("lora landed", du[64:P, :], A["aaa_up_2"][0])
                small_load("lora landed", gu1, A["gate_up_2"][0, 0:P, :])
                sp.eng.wait_ge(*T.at("gu2 cleared"))
                small_load("lora landed", gu2[96:P, :], A["gate_up_2"][0, P:P + 32, :])

            for n, (key, split, kt, c, src) in enumerate(units):
                if src is None:
                    if n == m1.first:
                        moe_load(m1, m1_w(0), m1_w(1), m1_down)
                    if n == m2.first:
                        moe_load(m2, m2_w("exp_gate_2"), m2_w("exp_up_2"), m2_down)
                    continue
                if n == m1.first + m1.units + 2:
                    rest_sp(sp, m1, m1_w(0), m1_w(1), m1_down)
                if n == m2.first + m2.units + 2:
                    rest_sp(sp, m2, m2_w("exp_gate_2"), m2_w("exp_up_2"), m2_down)
                if key == ("q2", 0):
                    second_small()
                if key == ("gb", 0):
                    sp.eng.wait_ge(*T.at("m1 done"))
                    small_load("m2 router landed", rw[:, :, 0:32], A["router_exp_2"][0].rearrange("(k p) n -> p k n", p=P))
                    small_load("m2 router landed", rw[:, :, 32:36], A["router_grp_2"][0].rearrange("(k p) n -> p k n", p=P))
                    small_load("m2 router landed", rbias[:, 0:32], A["router_exp_bias_2"].to_broadcast([P, 32]))
                    small_load("m2 router landed", rbias[:, 32:36], A["router_grp_bias_2"].to_broadcast([P, 4]))
                if key == ("pg", 0):
                    sp.eng.wait_ge(*T.at("y out"))
                    sp.eng.wait_ge(*T.at("Hf m2"))
                    small_load("p landed", tD[:, 0:2, :], A["p_2"][0, 0].rearrange("(a p) d -> p a d", p=P))
                if n >= RAW:
                    m = n - RAW
                    if units[m][1]:
                        sp.eng.wait_ge(T.sem("hi_done"), split_before[m] + 1)
                        sp.eng.wait_ge(T.sem("lo_done"), split_before[m] + 1)
                    else:
                        sp.eng.wait_ge(T.sem("unit_done"), m + 1)
                dst = view(ring_raw, n % RAW, kt, c)
                half = kt // 2
                for h in range(2):
                    eng.dma_start(dst[:, h * half:(h + 1) * half, :], src[:, h * half:(h + 1) * half, :])\
                       .then_inc(raw_landed[n % RAW], 16)

            y = tB[:, :, :].rearrange("p (a k) t -> p a (k t)", a=TT)
            for a in range(TT):
                sp.eng.wait_ge(*T.at(f"out {a}"))
                eng.dma_start(out[0, a * P:(a + 1) * P, :], y[:, a, :]).then_inc(T.sem("stored"), 16)
            eng.wait_ge(T.sem("stored"), 16 * TT)

        @block.gpsimd
        def _(eng):
            pool = Engine(T, eng, "pool")
            eng.memset(tA[:, 0:4, :], 0.0).then_inc(pool.tick("rows cleared"), 1)
            eng.memset(ident[:, :], 0.0).then_inc(pool.tick(), 1)
            pool.eng.wait_ge(*pool.own())
            eng.affine_select(out=ident[:, :], in_=ident[:, :], compare_op=ALU.not_equal, fill=1.0,
                                        base=0, pattern=[[-1, P]], channel_multiplier=1).then_inc(pool.tick("ident"), 1)
            eng.memset(means[:, :], 1.0 / D).then_inc(pool.tick("means"), 1)
            eng.memset(eps[:, 0:1], LN_EPS).then_inc(pool.tick(), 1)
            eng.memset(eps[:, 1:2], GN_EPS).then_inc(pool.tick("eps"), 1)
            eng.memset(uT[:, :, 0:PAD], 0.0).then_inc(pool.tick("u padded"), 1)
            eng.memset(ones[:, :], 1.0).then_inc(pool.tick(), 1)
            eng.memset(before[:, :], 1.0).then_inc(pool.tick(), 1)
            eng.memset(lower[:, :, :], 1.0).then_inc(pool.tick(), 1)
            eng.iota(slots[:, :], pattern=[[1, P]], base=0, channel_multiplier=0,
                               allow_small_or_imprecise_dtypes=True).then_inc(pool.tick(), 1)
            eng.iota(part[:, :], pattern=[[0, 1]], base=0, channel_multiplier=1,
                               allow_small_or_imprecise_dtypes=True).then_inc(pool.tick(), 1)
            pool.eng.wait_ge(*pool.own())
            eng.affine_select(out=before[:, :], in_=before[:, :], compare_op=ALU.is_gt, fill=0.0,
                                        base=0, pattern=[[1, P]], channel_multiplier=-1).then_inc(pool.tick(), 1)
            eng.affine_select(out=lower[:, :, :], in_=lower[:, :, :], compare_op=ALU.is_gt, fill=0.0,
                                        base=0, pattern=[[1, 8], [-1, 8]], channel_multiplier=0).then_inc(pool.tick("routing constants"), 1)
            eng.iota(alibi[:, 0:P], pattern=[[1, P]], base=0, channel_multiplier=-1,
                               allow_small_or_imprecise_dtypes=True).then_inc(pool.tick(), 1)
            eng.iota(alibi[:, P:3 * P], pattern=[[1, 2 * P]], base=-P, channel_multiplier=-1,
                               allow_small_or_imprecise_dtypes=True).then_inc(pool.tick(), 1)
            pool.eng.wait_ge(*pool.own())
            for c0, base in ((0, 0), (P, -P)):
                w = P if c0 == 0 else 2 * P
                eng.affine_select(out=alibi[:, c0:c0 + w], in_=alibi[:, c0:c0 + w],
                                            compare_op=ALU.is_ge, fill=NEG, base=-base,
                                            pattern=[[-1, w]], channel_multiplier=1).then_inc(pool.tick("alibi"), 1)

            pool.eng.wait_ge(*T.at("a1 done"))

            def keep_blocks(m, n):
                v = m.rearrange("p (b j) -> p b j", j=n)
                pool.eng.wait_ge(*pool.own())
                eng.affine_select(out=v, in_=v, compare_op=ALU.is_ge, fill=0.0, base=0,
                                            pattern=[[-n, P // n], [0, n]], channel_multiplier=1).then_inc(pool.tick(), 1)
                pool.eng.wait_ge(*pool.own())
                eng.affine_select(out=v, in_=v, compare_op=ALU.is_ge, fill=0.0, base=n - 1,
                                            pattern=[[n, P // n], [0, n]], channel_multiplier=-1).then_inc(pool.tick(), 1)

            for m, sign, op in ((m_su, 1, ALU.is_gt), (m_sl, -1, ALU.is_gt), (m_iu, 1, ALU.is_ge)):
                eng.memset(m, 1.0).then_inc(pool.tick(), 1)
                pool.eng.wait_ge(*pool.own())
                eng.affine_select(out=m, in_=m, compare_op=op, fill=0.0, base=0,
                                            pattern=[[sign, P]], channel_multiplier=-sign).then_inc(pool.tick(), 1)
                keep_blocks(m, 64)
            eng.memset(m_d16, 1.0).then_inc(pool.tick(), 1)
            keep_blocks(m_d16, 16)
            pool.eng.wait_ge(*T.at("shifted"))
            eng.memset(gu2, 0.0).then_inc(pool.tick("gu2 cleared"), 1)
            pool.eng.wait_ge(*T.at("a2 done"))
            pool.eng.wait_ge(*T.at("Gh b2"))
            for m, n in ((m_o32, 32), (m_o64, 64), (m_d64, 64)):
                eng.memset(m, 1.0).then_inc(pool.tick(), 1)
                keep_blocks(m, n)
            pool.eng.wait_ge(*pool.own())
            eng.tensor_tensor(m_o64, m_o64, m_o32, ALU.subtract).then_inc(pool.tick(), 1)
            pool.eng.wait_ge(*pool.own())
            eng.tensor_tensor(m_o32, m_o32, m_d16, ALU.subtract).then_inc(pool.tick("chunk masks"), 1)

        @block.tensor
        def _(eng):
            pe = Engine(T, eng, "pe")
            mm = nc.tensor.matmul

            def ready(n):
                if units[n][1]:
                    pe.eng.wait_ge(T.sem("hi_done"), split_before[n] + 1)
                    pe.eng.wait_ge(T.sem("lo_done"), split_before[n] + 1)
                else:
                    landed(pe, n)

            def unit_end(ins, n, job=None):
                ins.then_inc(T.sem("unit_done"), 1)
                if job:
                    T.mark("mm " + job, "unit_done", n + 1)

            def columns(key, job, Xh, Xl):
                n = at_unit[key]
                kt, c = units[n][2], units[n][3]
                jobs = [job] if c <= 2 * P else [f"{job}.{i}" for i in range(c // (2 * P))]
                banks = [take(pe, i) for i in jobs]
                ready(n)
                wh, wl = weights(n)
                for blk in range(c // P):
                    o = banks[blk // 2][:, (blk % 2) * S:(blk % 2 + 1) * S]
                    for k in range(kt):
                        cs = slice(blk * P, (blk + 1) * P)
                        mm(o, wh[:, k, cs], Xh[:, k, :], start=(k == 0), stop=False)
                        mm(o, wh[:, k, cs], Xl[:, k, :], start=False, stop=False)
                        last = mm(o, wl[:, k, cs], Xh[:, k, :], start=False, stop=(k == kt - 1))
                unit_end(last, n)
                for i in jobs:
                    T.mark("mm " + i, "unit_done", n + 1)

            def rows_of(key, job, Xh, Xl):
                n = at_unit[key]
                b = take(pe, job)
                ready(n)
                wh, wl = weights(n)
                kt, c = units[n][2], units[n][3]
                for t in range(TT):
                    o = b[:, t * c:(t + 1) * c]
                    ts = slice(t * P, (t + 1) * P)
                    for k in range(kt):
                        mm(o, Xh[:, k, ts], wh[:, k, :], start=(k == 0), stop=False)
                        mm(o, Xl[:, k, ts], wh[:, k, :], start=False, stop=False)
                        last = mm(o, Xh[:, k, ts], wl[:, k, :], start=False, stop=(k == kt - 1))
                unit_end(last, n, job)

            def adaptive(l, j):
                n = at_unit[("ada", l, j)]
                b = take(pe, f"ada {l} {j}")
                ready(n)
                w, _ = weights(n)
                for blk in range(2):
                    for k in range(KT):
                        last = mm(b[:, blk:blk + 1], w[:, k, blk * P:(blk + 1) * P], ccol[:, k:k + 1],
                                  start=(k == 0), stop=(k == KT - 1))
                unit_end(last, n, f"ada {l} {j}")

            def transposes(job, pairs, group="A"):
                b = take(pe, job, group)
                for o, src in pairs:
                    last = nc.tensor.transpose(b[:, o * P:(o + 1) * P], src, ident[:, :])
                last.then_inc(pe.tick("mm " + job), 1)

            def ln_stats(name, z):
                b = take(pe, "ln " + name)
                pe.eng.wait_ge(*T.at("means"))
                for k in range(KT):
                    pe.eng.wait_ge(*T.at(f"z {name} {k}"))
                    last = mm(b[:, 0:S], means[:, :], z[:, k, :], start=(k == 0), stop=(k == KT - 1))
                last.then_inc(pe.tick(f"mm mean {name}"), 1)
                b = take(pe, "lv " + name)
                for k in range(KT):
                    pe.eng.wait_ge(*T.at(f"square {name} {k // 4}"))
                    last = mm(b[:, 0:S], means[:, :], tC[:, k, :], start=(k == 0), stop=(k == KT - 1))
                last.then_inc(pe.tick(f"mm var {name}"), 1)

            pe.eng.wait_ge(*T.at("rows landed"))
            pe.eng.wait_ge(*T.at("ident"))
            rows = tA[:, 0:4, :].rearrange("p k t -> p (k t)")
            for j in range(2):
                transposes(f"cols {j}", [(k, rows[:, (4 * j + k) * P:(4 * j + k + 1) * P]) for k in range(4)])
            pe.eng.wait_ge(*T.at("x landed"))
            x_in = tB[:, :, :].rearrange("p (a k) t -> p a (k t)", a=TT)
            for j in range(4):
                transposes(f"x {j}", [(2 * k + a, x_in[:, a, (2 * j + k) * P:(2 * j + k + 1) * P])
                                      for k in range(2) for a in range(TT)])
            pe.stage = "conv"
            pe.eng.wait_ge(*T.at("ccol"))
            for j in range(8):
                adaptive(0, j)
            pe.eng.wait_ge(*T.at("Hh conv"))
            pe.eng.wait_ge(*T.at("Hl conv"))
            for j in range(4):
                columns(("conv a", j), f"conv a {j}", Hh, Hl)
                columns(("conv g", j), f"conv g {j}", Hh, Hl)
            for j in range(8, 24):
                adaptive(0, j)
            for j in range(8):
                adaptive(2, j)
            ln_stats("conv", tA)
            pe.eng.wait_ge(*T.at("Gh conv"))
            pe.eng.wait_ge(*T.at("Gl conv"))
            for j in range(4):
                columns(("conv_out", j), f"out0 {j}", Gh, Gl)
            ln_stats("ln0", tA)
            pe.stage = "ffn"
            pe.eng.wait_ge(*T.at("Hh ffn"))
            pe.eng.wait_ge(*T.at("Hl ffn"))
            acc = [take(pe, f"ffn acc {i}", "D") for i in range(4)]
            late = list(range(24))

            def ffn_down(j):
                n = at_unit[("ffn2", j)]
                pe.eng.wait_ge(*T.at(f"fh {j}"))
                pe.eng.wait_ge(*T.at(f"fl {j}"))
                ready(n)
                wh, wl = weights(n)
                for cb in range(KT):
                    cs = slice(cb * P, (cb + 1) * P)
                    o = acc[cb // 2][:, (cb % 2) * S:(cb % 2 + 1) * S]
                    for k in range(2):
                        g = 2 * (j % 4) + k
                        first = j == 0 and cb % 2 == 0 and k == 0
                        end = j == NP - 1 and k == 1
                        mm(o, wh[:, k, cs], Gh[:, g, :], start=first, stop=False, skip_group_check=True)
                        mm(o, wh[:, k, cs], Gl[:, g, :], start=False, stop=False, skip_group_check=True)
                        last = mm(o, wl[:, k, cs], Gh[:, g, :], start=False, stop=end, skip_group_check=True)
                unit_end(last, n)
                T.mark(f"ffn down {j}", "unit_done", n + 1)
                for _ in range(3):
                    if late:
                        adaptive(1, late.pop(0))

            for j in range(NP):
                columns(("ffn a", j), f"ffn a {j}", Hh, Hl)
                columns(("ffn b", j), f"ffn b {j}", Hh, Hl)
                if j:
                    ffn_down(j - 1)
            ffn_down(NP - 1)
            ln_stats("ln1", tA)
            pe.stage = "attn"
            pe.eng.wait_ge(*T.at("Hh kv"))
            pe.eng.wait_ge(*T.at("Hl kv"))
            for j in range(4):
                columns(("k", j), f"k {j}", Hh, Hl)
            for j in range(4):
                rows_of(("v", j), f"v {j}", Hh, Hl)
            pe.eng.wait_ge(*T.at("Gh q"))
            pe.eng.wait_ge(*T.at("Gl q"))
            for j in range(4):
                columns(("q", j), f"q {j}", Gh, Gl)
            attention(pe, "a1", HEADS, tD, tB, tC[:, :, :].rearrange("p (a k) t -> p a (k t)", a=TT))
            pe.eng.wait_ge(*T.at("Hh wo"))
            pe.eng.wait_ge(*T.at("Hl wo"))
            for j in range(4):
                columns(("wo", j), f"wo {j}", Hh, Hl)
            ln_stats("ln2", tA)
            pe.stage = "m1"
            moe_pe(pe, m1, tD)
            rest_pe(pe, m1, tD)
            ln_stats("ln3", tA)
            pe.stage = "b2"
            ln_stats("ln4", tA)
            pe.eng.wait_ge(*T.at("Hh b2"))
            pe.eng.wait_ge(*T.at("Hl b2"))
            for j in range(8):
                columns(("rw", j), f"rw {j}", Hh, Hl)
            for j in range(2):
                rows_of(("v2", j), f"v2 {j}", Hh, Hl)
            for key in ("q2", "k2"):
                for j in range(2):
                    columns((key, j), f"{key} {j}", Hh, Hl)
            for j in range(4):
                columns(("ga", j), f"ga {j}", Hh, Hl)
            attention(pe, "a2", HEADS2, Q2, K2, V2)
            pe.eng.wait_ge(*T.at("Gh b2"))
            pe.eng.wait_ge(*T.at("Gl b2"))
            for j in range(2):
                columns(("wa", j), f"wa {j}", Gh[:, 0:4, :], Gh[:, 4:8, :])
            rwkv_pe(pe)
            for j in range(4):
                columns(("gb", j), f"gb {j}", Hh, Hl)
            pe.eng.wait_ge(*T.at("Gh wb"))
            pe.eng.wait_ge(*T.at("Gl wb"))
            for j in range(2):
                columns(("wb", j), f"wb {j}", Gh[:, 0:4, :], Gh[:, 4:8, :])
            pe.eng.wait_ge(*T.at("Hh mix"))
            pe.eng.wait_ge(*T.at("Hl mix"))
            for j in range(4):
                columns(("w_out", j), f"w_out {j}", Hh, Hl)
            ln_stats("ln5", tA)
            pe.stage = "m2"
            moe_pe(pe, m2, xT)
            rest_pe(pe, m2, xT)
            ln_stats("ln6", tA)
            pe.stage = "ple"
            pe.eng.wait_ge(*T.at("p landed"))
            transposes("pT", [(2 * k + a, tD[:, a, k * P:(k + 1) * P]) for k in range(2) for a in range(TT)])
            pe.eng.wait_ge(*T.at("Hh ple"))
            pe.eng.wait_ge(*T.at("Hl ple"))
            for j in range(4):
                columns(("pg", j), f"pg {j}", Hh, Hl)
            pe.eng.wait_ge(*T.at("Gh ple"))
            pe.eng.wait_ge(*T.at("Gl ple"))
            columns(("pp", 0), "pp", Gh[:, 0:2, :], Gl[:, 0:2, :])
            ln_stats("ln7", tA)
            pe.eng.wait_ge(*T.at("x out"))
            for a in range(TT):
                for j in range(2):
                    transposes(f"out {a} {j}", [(k, tD[:, 4 * j + k, a * P:(a + 1) * P]) for k in range(4)])

        @block.scalar
        def _(eng):
            act = Engine(T, eng, "act")
            run = nc.scalar.activation

            def halves_hi(name, dst, src):
                for j in range(4):
                    act.eng.wait_ge(*T.at(f"f {name} {j}"))
                    run(dst[:, 2 * j:2 * j + 2, :], src[:, 2 * j:2 * j + 2, :], ACT.Copy).then_inc(act.tick(f"hi {name} {j}"), 1)

            def ln(name):
                for h in range(2):
                    act.eng.wait_ge(*T.at(f"centred {name} {h}"))
                    run(tC[:, 4 * h:4 * h + 4, :], tA[:, 4 * h:4 * h + 4, :], ACT.Square).then_inc(act.tick(f"square {name} {h}"), 1)
                act.eng.wait_ge(*T.at(f"mm var {name}"))
                act.eng.wait_ge(*T.at("eps"))
                run(stat[:, 0, :], ps("lv " + name)[:, 0:S], ACT.Sqrt, bias=eps[:, 0:1]).then_inc(act.tick(f"ev lv {name}"), 1)
                T.mark(f"std {name}", *act.last)

            def bias_out(l, j, n):
                split_hi(act, n + 2)
                job = f"ada {l} {j}"
                act.eng.wait_ge(*T.at("mm " + job))
                act.eng.wait_ge(*T.at("bias"))
                v = VEC(l, j // 4)
                name, row = ("ada_b", v) if l < 2 else ("kv_ada_b", j // 4)
                for b in range(2):
                    k = 2 * (j % 4) + b
                    run(mods[:, v, k:k + 1], ps(job)[:, b:b + 1], ACT.Identity,
                                 bias=col(name, k, row)).then_inc(act.tick("ev " + job), 1)
                T.mark(f"mods {l} {j // 4}", *act.last)

            split_hi(act, 0)
            for j in range(2):
                act.eng.wait_ge(*T.at(f"mm cols {j}"))
                run(cols[:, 4 * j:4 * j + 4, :],
                             ps(f"cols {j}")[:, :].rearrange("p (k r) -> p k r", r=P)[:, :, 0:NROW], ACT.Copy).then_inc(act.tick(f"ev cols {j}"), 1)
            act.eng.wait_ge(*act.own())
            run(ccol[:, :], cols[:, :, ROW["c"]], ACT.Silu).then_inc(act.tick("ccol"), 1)
            for j in range(4):
                act.eng.wait_ge(*T.at(f"mm x {j}"))
                run(xT[:, 2 * j:2 * j + 2, :], ps(f"x {j}")[:, :].rearrange("p (k t) -> p k t", k=2),
                             ACT.Copy).then_inc(act.tick(f"ev x {j}"), 1)
            act.stage = "conv"
            for j in range(8):
                bias_out(0, j, at_unit[("ada", 0, j)])
            halves_hi("conv", Hh, tD)
            T.mark("Hh conv", *act.last)
            for j in range(4):
                split_hi(act, at_unit[("conv g", j)] + 2)
                act.eng.wait_ge(*T.at(f"mm conv g {j}"))
                for b in range(2):
                    k = 2 * j + b
                    run(tC[:, k, :], ps(f"conv g {j}")[:, b * S:(b + 1) * S], ACT.Sigmoid,
                                 bias=col("conv_in_b", k, 1)).then_inc(act.tick(f"ev conv g {j}"), 1)
                T.mark(f"gate {j}", *act.last)
            for j in range(8, 24):
                bias_out(0, j, at_unit[("ada", 0, j)])
            for j in range(8):
                bias_out(2, j, at_unit[("ada", 2, j)])
            split_hi(act, at_unit[("conv_out", 2)])
            ln("conv")
            for j in range(4):
                act.eng.wait_ge(*T.at(f"normed conv {j // 2}"))
                for k in (2 * j, 2 * j + 1):
                    run(tD[:, k, :], tA[:, k, :], ACT.Silu, bias=col("conv_norm_b", k),
                                 scale=col("conv_norm_g", k)).then_inc(act.tick(), 1)
                T.mark(f"f convo {j}", *act.last)
                act.eng.wait_ge(*act.own())
                run(Gh[:, 2 * j:2 * j + 2, :], tD[:, 2 * j:2 * j + 2, :], ACT.Copy).then_inc(act.tick(f"hi convo {j}"), 1)
            T.mark("Gh conv", *act.last)

            def gated(l, v, key, job, bias=None):
                for j in range(4):
                    split_hi(act, at_unit[(key, j)] + 2)
                    act.eng.wait_ge(*T.at(f"mm {job} {j}"))
                    act.eng.wait_ge(*T.at(f"mods {l} {v}"))
                    for b in range(2):
                        k = 2 * j + b
                        run(tB[:, k, :], ps(f"{job} {j}")[:, b * S:(b + 1) * S], ACT.Identity,
                                     scale=mod(l, v, k), bias=gb[:, k:k + 1] if bias else 0.0).then_inc(act.tick(f"ev {job} {j}"), 1)
                    T.mark(f"gated {job} {j}", *act.last)

            act.eng.wait_ge(*T.at("gb"))
            gated(0, 2, "conv_out", "out0", True)
            split_hi(act, at_unit[("ffn b", 0)] + 1)
            ln("ln0")
            halves_hi("ffnin", Hh, tD)
            T.mark("Hh ffn", *act.last)
            act.stage = "ffn"
            late = list(range(24))
            for j in range(NP + 1):
                if j < NP:
                    split_hi(act, at_unit[("ffn b", j)] + 2)
                    act.eng.wait_ge(*T.at(f"mm ffn a {j}"))
                    if j >= 4:
                        act.eng.wait_ge(*T.at(f"fh {j - 4}"))
                        act.eng.wait_ge(*T.at(f"fl {j - 4}"))
                    run(tB[:, 2 * (j % 4):2 * (j % 4) + 2, :],
                                 ps(f"ffn a {j}")[:, :].rearrange("p (k t) -> p k t", k=2), ACT.Silu).then_inc(act.tick(f"ev ffn a {j}"), 1)
                    act.eng.wait_ge(*T.at(f"f ffn {j}"))
                    if j >= 4:
                        act.eng.wait_ge(*T.at(f"ffn down {j - 4}"))
                    g = 2 * (j % 4)
                    run(Gh[:, g:g + 2, :], tC[:, g:g + 2, :], ACT.Copy).then_inc(act.tick(f"fh {j}"), 1)
                if j:
                    for _ in range(3):
                        if late:
                            i = late.pop(0)
                            bias_out(1, i, at_unit[("ada", 1, i)])
            split_hi(act, at_unit[("ffn2", NP - 1)] + 3)
            for i in range(4):
                act.eng.wait_ge(*T.at(f"ffn down {NP - 1}"))
                act.eng.wait_ge(*T.at("mods 0 5"))
                for b in range(2):
                    k = 2 * i + b
                    run(tB[:, k, :], ps(f"ffn acc {i}")[:, b * S:(b + 1) * S], ACT.Identity,
                                 scale=mod(0, 5, k)).then_inc(act.tick(f"ev ffn acc {i}"), 1)
                T.mark(f"gated ffn {i}", *act.last)
            ln("ln1")
            act.stage = "attn"
            halves_hi("kv", Hh, tD)
            T.mark("Hh kv", *act.last)
            halves_hi("q", Gh, tB)
            T.mark("Gh q", *act.last)
            for j in range(4):
                split_hi(act, at_unit[("k", j)] + 2)
                act.eng.wait_ge(*T.at(f"mm k {j}"))
                if j == 0:
                    act.eng.wait_ge(*T.at("Gl q"))
                run(tB[:, 2 * j:2 * j + 2, :], ps(f"k {j}")[:, :].rearrange("p (k t) -> p k t", k=2),
                             ACT.Copy).then_inc(act.tick(f"ev k {j}"), 1)
                T.mark(f"a1 kT {j}", *act.last)
            V = tC[:, :, :].rearrange("p (a k) t -> p a (k t)", a=TT)
            for j in range(4):
                split_hi(act, at_unit[("v", j)] + 2)
                act.eng.wait_ge(*T.at(f"mm v {j}"))
                run(V[:, :, 256 * j:256 * j + 256],
                             ps(f"v {j}")[:, :].rearrange("p (a c) -> p a c", a=TT), ACT.Copy).then_inc(act.tick(f"ev v {j}"), 1)
            T.mark("a1 v", *act.last)
            for j in range(4):
                split_hi(act, at_unit[("q", j)] + 2)
                act.eng.wait_ge(*T.at(f"mm q {j}"))
                run(tD[:, 2 * j:2 * j + 2, :], ps(f"q {j}")[:, :].rearrange("p (k t) -> p k t", k=2),
                             ACT.Copy, scale=0.125).then_inc(act.tick(f"ev q {j}"), 1)
                T.mark(f"a1 qT {j}", *act.last)
            softmax_exp(act, "a1", HEADS, Hh)
            T.mark("Hh wo", *act.last)
            gated(1, 2, "wo", "wo")
            ln("ln2")
            act.stage = "m1"
            moe_act(act, m1)
            rest_act(act, m1)
            act.eng.wait_ge(*T.at("m1 done"))
            for k in range(KT):
                run(tD[:, k, :], tB[:, k, :], ACT.Identity, scale=mod(1, 5, k)).then_inc(act.tick(f"gated m1 {k}"), 1)
            ln("ln3")
            act.stage = "b2"
            ln("ln4")
            halves_hi("b2", Hh, xT)
            T.mark("Hh b2", *act.last)
            for j in range(8):
                split_hi(act, at_unit[("rw", j)] + 2)
                act.eng.wait_ge(*T.at(f"mm rw {j}"))
                w = 2 if j < 7 else 1
                k = (2 * j) % 8
                if j >= 4:
                    act.eng.wait_ge(*T.at(f"mix {j - 4}"))
                run(uT[:, k:k + w, PAD:PAD + S],
                             ps(f"rw {j}")[:, 0:w * S].rearrange("p (k t) -> p k t", k=w), ACT.Copy).then_inc(act.tick(f"ev rw {j}"), 1)
            for j in range(2):
                split_hi(act, at_unit[("v2", j)] + 2)
                act.eng.wait_ge(*T.at(f"mm v2 {j}"))
                run(V2[:, :, 256 * j:256 * j + 256], bank_view(ps(f"v2 {j}")), ACT.Copy).then_inc(act.tick(f"ev v2 {j}"), 1)
            T.mark("a2 v", *act.last)
            for key, dst, sc in (("q2", Q2, 0.125), ("k2", K2, 1.0)):
                for j in range(2):
                    split_hi(act, at_unit[(key, j)] + 2)
                    act.eng.wait_ge(*T.at(f"mm {key} {j}"))
                    run(dst[:, 2 * j:2 * j + 2, :],
                                 ps(f"{key} {j}")[:, :].rearrange("p (k t) -> p k t", k=2), ACT.Copy, scale=sc).then_inc(act.tick(f"ev {key} {j}"), 1)
                    T.mark(f"a2 {key[0]}T {j}", *act.last)
            for j in range(4):
                split_hi(act, at_unit[("ga", j)] + 2)
                act.eng.wait_ge(*T.at(f"mm ga {j}"))
                run(MA[:, 2 * j:2 * j + 2, :], ps(f"ga {j}")[:, :].rearrange("p (k t) -> p k t", k=2),
                             ACT.Sigmoid).then_inc(act.tick(f"ev ga {j}"), 1)
            T.mark("gate a", *act.last)
            softmax_exp(act, "a2", HEADS2, Gh)
            T.mark("Gh b2", *act.last)
            split_hi(act, at_unit[("wa", 1)] + 2)
            rwkv_act(act)
            act.stage = "b2 end"
            for j in range(4):
                split_hi(act, at_unit[("gb", j)] + 2)
                act.eng.wait_ge(*T.at(f"mm gb {j}"))
                act.eng.wait_ge(*T.at("y out"))
                run(tA[:, 2 * j:2 * j + 2, :], ps(f"gb {j}")[:, :].rearrange("p (k t) -> p k t", k=2),
                             ACT.Sigmoid).then_inc(act.tick(f"ev gb {j}"), 1)
            T.mark("gate b", *act.last)
            split_hi(act, at_unit[("wb", 1)] + 2)
            halves_hi("mix", Hh, tC)
            T.mark("Hh mix", *act.last)
            for j in range(4):
                split_hi(act, at_unit[("w_out", j)] + 2)
            ln("ln5")
            act.stage = "m2"
            moe_act(act, m2)
            rest_act(act, m2)
            ln("ln6")
            act.stage = "ple"
            halves_hi("ple", Hh, xT)
            T.mark("Hh ple", *act.last)
            act.eng.wait_ge(*T.at("mm pT"))
            run(Gh[:, 0:2, :], ps("pT")[:, :].rearrange("p (k t) -> p k t", k=2), ACT.Copy).then_inc(act.tick("Gh ple"), 1)
            for j in range(4):
                split_hi(act, at_unit[("pg", j)] + 2)
                act.eng.wait_ge(*T.at(f"mm pg {j}"))
                run(tB[:, 2 * j:2 * j + 2, :], ps(f"pg {j}")[:, :].rearrange("p (k t) -> p k t", k=2),
                             ACT.Sigmoid).then_inc(act.tick(f"ev pg {j}"), 1)
                T.mark(f"gate p {j}", *act.last)
            ln("ln7")
            y = tB[:, :, :].rearrange("p (a k) t -> p a (k t)", a=TT)
            for a in range(TT):
                for j in range(2):
                    act.eng.wait_ge(*T.at(f"mm out {a} {j}"))
                    run(y[:, a, 512 * j:512 * j + 512], ps(f"out {a} {j}")[:, :], ACT.Copy).then_inc(act.tick(f"ev out {a} {j}"), 1)
                T.mark(f"out {a}", *act.last)

        @block.vector
        def _(eng):
            dve = Engine(T, eng, "dve")
            tt, ts, stt = nc.vector.tensor_tensor, nc.vector.tensor_scalar, nc.vector.scalar_tensor_tensor

            def halves_lo(name, dst, src, hi):
                for j in range(4):
                    s = slice(2 * j, 2 * j + 2)
                    dve.eng.wait_ge(*T.at(f"hi {name} {j}"))
                    tt(dst[:, s, :], src[:, s, :], hi[:, s, :].bitcast(F32), ALU.subtract).then_inc(dve.tick(), 1)

            def modulate(name, l, vs, vb, dst):
                dve.eng.wait_ge(*T.at(f"mods {l} {vs}"))
                dve.eng.wait_ge(*T.at(f"mods {l} {vb}"))
                for k in range(KT):
                    ts(dst[:, k, :], xT[:, k, :], mod(l, vs, k), mod(l, vb, k), ALU.mult, ALU.add).then_inc(dve.tick(), 1)
                    T.mark(f"f {name} {k // 2}", *dve.last)

            def ln(name):
                b = ps("ln " + name)
                dve.eng.wait_ge(*T.at(f"mm mean {name}"))
                for h in range(2):
                    s = slice(4 * h, 4 * h + 4)
                    tt(tA[:, s, :], tA[:, s, :], b[:, 0:S].unsqueeze(1).to_broadcast([P, 4, S]),
                                ALU.subtract).then_inc(dve.tick(f"centred {name} {h}"), 1)
                T.mark("ev ln " + name, *dve.last)
                dve.eng.wait_ge(*T.at(f"std {name}"))
                nc.vector.reciprocal(stat[:, 1, :], stat[:, 0, :]).then_inc(dve.tick(), 1)
                dve.eng.wait_ge(*dve.own())
                for h in range(2):
                    s = slice(4 * h, 4 * h + 4)
                    dve.eng.wait_ge(*T.at(f"square {name} {h}"))
                    tt(tA[:, s, :], tA[:, s, :], stat[:, 1, :].unsqueeze(1).to_broadcast([P, 4, S]),
                                ALU.mult).then_inc(dve.tick(f"normed {name} {h}"), 1)

            def affine(g, b, i):
                dve.eng.wait_ge(*dve.own())
                for k in range(KT):
                    ts(xT[:, k, :], tA[:, k, :], col(g, k, i), col(b, k, i), ALU.mult, ALU.add).then_inc(dve.tick(), 1)
                T.mark(f"x {g} {i}", *dve.last)
                dve.eng.wait_ge(*dve.own())

            def residual(name, job, key, l=None):
                for j in range(4):
                    if key:
                        split_lo(dve, at_unit[(key, j)] + 2)
                    dve.eng.wait_ge(*T.at(f"gated {job} {j}"))
                    for k in (2 * j, 2 * j + 1):
                        stt(tA[:, k, :], xT[:, k, :], ALPHA, tB[:, k, :], ALU.mult, ALU.add).then_inc(dve.tick(f"z {name} {k}"), 1)

            split_lo(dve, 0)
            dve.eng.wait_ge(*T.at("ev cols 1"))
            for l in range(2):
                for v in (1, 2, 4, 5):
                    c = cols[:, :, ROW["ada_b"] + VEC(l, v)]
                    nc.vector.tensor_scalar(c, c, 1.0, None, ALU.add).then_inc(dve.tick(), 1)
            c = cols[:, :, ROW["kv_ada_b"] + 1]
            nc.vector.tensor_scalar(c, c, 1.0, None, ALU.add).then_inc(dve.tick("bias"), 1)
            dve.stage = "conv"
            for j in range(4):
                dve.eng.wait_ge(*T.at(f"ev x {j}"))
            modulate("conv", 0, 1, 0, tD)
            halves_lo("conv", Hl, tD, Hh)
            T.mark("Hl conv", *dve.last)
            for j in range(4):
                split_lo(dve, at_unit[("conv g", j)] + 2)
                dve.eng.wait_ge(*T.at(f"mm conv a {j}"))
                dve.eng.wait_ge(*T.at(f"gate {j}"))
                dve.eng.wait_ge(*T.at("u padded"))
                for b in range(2):
                    k = 2 * j + b
                    stt(uT[:, k, PAD:PAD + S], ps(f"conv a {j}")[:, b * S:(b + 1) * S],
                                 col("conv_in_b", k), tC[:, k, :], ALU.add, ALU.mult).then_inc(dve.tick(f"ev conv a {j}"), 1)
            taps = []
            for i in range(TAPS):
                for k in range(KT):
                    if i == 0:
                        dve.eng.wait_ge(*dve.own())
                        if k == 0:
                            dve.eng.wait_ge(*T.at("ev cols 1"))
                            dve.eng.wait_ge(*T.at("mm cols 1"))
                        ins = ts(tA[:, k, :], uT[:, k, 0:S], col("conv_dw_w", k, 0), col("conv_dw_b", k),
                                 ALU.mult, ALU.add)
                    else:
                        dve.eng.wait_ge(*taps[-KT])
                        ins = stt(tA[:, k, :], uT[:, k, i:i + S], col("conv_dw_w", k, i), tA[:, k, :],
                                  ALU.mult, ALU.add)
                    ins.then_inc(dve.tick(f"z conv {k}"), 1)
                    taps.append(dve.own())
            split_lo(dve, at_unit[("conv_out", 2)])
            ln("conv")
            halves_lo("convo", Gl, tD, Gh)
            T.mark("Gl conv", *dve.last)
            dve.eng.wait_ge(*T.at("mods 0 2"))
            tt(gb[:, :], cols[:, :, ROW["conv_out_b"]], mods[:, VEC(0, 2), :], ALU.mult).then_inc(dve.tick("gb"), 1)
            residual("ln0", "out0", "conv_out")
            split_lo(dve, at_unit[("ffn b", 0)] + 1)
            ln("ln0")
            affine("ln_g", "ln_b", 0)
            modulate("ffnin", 0, 4, 3, tD)
            halves_lo("ffnin", Hl, tD, Hh)
            T.mark("Hl ffn", *dve.last)
            dve.stage = "ffn"
            for j in range(NP + 1):
                if j < NP:
                    split_lo(dve, at_unit[("ffn b", j)] + 2)
                    dve.eng.wait_ge(*T.at(f"mm ffn b {j}"))
                    dve.eng.wait_ge(*T.at(f"ev ffn a {j}"))
                    if j >= 4:
                        dve.eng.wait_ge(*T.at(f"fh {j - 4}"))
                        dve.eng.wait_ge(*T.at(f"ffn down {j - 4}"))
                    g = 2 * (j % 4)
                    tt(tC[:, g:g + 2, :], tB[:, g:g + 2, :],
                                ps(f"ffn b {j}")[:, :].rearrange("p (k t) -> p k t", k=2), ALU.mult).then_inc(dve.tick(f"ev ffn b {j}"), 1)
                    T.mark(f"f ffn {j}", *dve.last)
                    dve.eng.wait_ge(*T.at(f"fh {j}"))
                    tt(Gl[:, g:g + 2, :], tC[:, g:g + 2, :], Gh[:, g:g + 2, :].bitcast(F32),
                                ALU.subtract).then_inc(dve.tick(f"fl {j}"), 1)
            split_lo(dve, at_unit[("ffn2", NP - 1)] + 3)
            residual("ln1", "ffn", None)
            ln("ln1")
            affine("ln_g", "ln_b", 1)
            dve.stage = "attn"
            modulate("kv", 2, 1, 0, tD)
            halves_lo("kv", Hl, tD, Hh)
            T.mark("Hl kv", *dve.last)
            modulate("q", 1, 1, 0, tB)
            halves_lo("q", Gl, tB, Gh)
            T.mark("Gl q", *dve.last)
            for key in ("k", "v", "q"):
                for j in range(4):
                    split_lo(dve, at_unit[(key, j)] + (2 if key == "q" and j == 3 else 2))
            softmax_rest(dve, "a1", HEADS, lambda h, c0, w: (alibi[:, c0:c0 + w], 2.0 ** (-8.0 * (h + 1) / HEADS)), Hl, Hh)
            T.mark("Hl wo", *dve.last)
            T.mark("a1 done", *dve.last)
            residual("ln2", "wo", "wo")
            ln("ln2")
            affine("ln_g", "ln_b", 2)
            dve.stage = "m1"
            modulate("m1", 1, 4, 3, tD)
            T.mark("Hf m1", *dve.last)
            moe_dve(dve, m1)
            rest_dve(dve, m1)
            for k in range(KT):
                dve.eng.wait_ge(*T.at(f"gated m1 {k}"))
                stt(tA[:, k, :], xT[:, k, :], ALPHA, tD[:, k, :], ALU.mult, ALU.add).then_inc(dve.tick(f"z ln3 {k}"), 1)
            ln("ln3")
            dve.eng.wait_ge(*dve.own())
            for k in range(KT):
                ts(tA[:, k, :], tA[:, k, :], col("ln_g", k, 3), col("ln_b", k, 3), ALU.mult, ALU.add).then_inc(dve.tick(f"z ln4 {k}"), 1)
            dve.stage = "b2"
            ln("ln4")
            affine("ln_in_g_2", "ln_in_b_2", 0)
            for j in range(4):
                T.mark(f"f b2 {j}", *dve.last)
            halves_lo("b2", Hl, xT, Hh)
            T.mark("Hl b2", *dve.last)
            dve.eng.wait_ge(*T.at("mm mean ln4"))
            dve.eng.wait_ge(*T.at("mm var ln4"))
            for j in range(8):
                split_lo(dve, at_unit[("rw", j)] + 2)
                dve.eng.wait_ge(*T.at(f"ev rw {j}"))
                w = 2 if j < 7 else 1
                k = (2 * j) % 8
                u = uT[:, k:k + w, :]
                d = (tA if j < 4 else tB)[:, k:k + w, :]
                tt(d, u[:, :, PAD - 1:PAD - 1 + S], u[:, :, PAD:PAD + S], ALU.subtract).then_inc(dve.tick(), 1)
                dve.eng.wait_ge(*dve.own())
                for i in range(w):
                    blk = 2 * j + i
                    mu = (col("tok_mix_2", blk) if blk < 8 else col("tok_mix_2", blk - 8, 1) if blk < 14
                          else col("tok_mix_2", 0, 2))
                    stt(d[:, i, :], d[:, i, :], mu, u[:, i, PAD:PAD + S], ALU.mult, ALU.add).then_inc(dve.tick(f"mix {j}"), 1)
            T.mark("shifted", *dve.last)
            dve.eng.wait_ge(*T.at("rel landed"))
            nc.vector.tensor_copy(rel[:, 0:P - 1], rel[:, P - 1:P].to_broadcast([HEADS2, P - 1])).then_inc(dve.tick("rel ready"), 1)
            for key, n in (("v2", 2), ("q2", 2), ("k2", 2), ("ga", 4)):
                for j in range(n):
                    split_lo(dve, at_unit[(key, j)] + 2)
            dve.eng.wait_ge(*T.at("bias landed"))
            nc.vector.memset(relb[0:64, :, 3 * 64:4 * 64], NEG).then_inc(dve.tick(), 1)
            dve.eng.wait_ge(*dve.own())
            softmax_rest(dve, "a2", HEADS2, lambda h, c0, w: (relb[:, h, P:S] if c0 == 0 else relb[:, h, :], None),
                         Gh[:, 4:8, :], Gh)
            T.mark("Gl b2", *dve.last)
            T.mark("a2 done", *dve.last)
            split_lo(dve, at_unit[("wa", 1)] + 2)
            dve.eng.wait_ge(*T.at("gate a"))
            for j in range(2):
                for i in range(2):
                    dve.eng.wait_ge(*T.at(f"mm wa {j}.{i}"))
                    k = 4 * j + 2 * i
                    tt(MA[:, k:k + 2, :], MA[:, k:k + 2, :],
                                ps(f"wa {j}.{i}")[:, :].rearrange("p (k t) -> p k t", k=2), ALU.mult).then_inc(dve.tick(f"ev wa {j}.{i}"), 1)
            rwkv_dve(dve)
            dve.stage = "b2 end"
            for j in range(4):
                split_lo(dve, at_unit[("gb", j)] + 2)
            dve.eng.wait_ge(*T.at("gate b"))
            for j in range(2):
                split_lo(dve, at_unit[("wb", j)] + 2)
                for i in range(2):
                    dve.eng.wait_ge(*T.at(f"mm wb {j}.{i}"))
                    k = 4 * j + 2 * i
                    tt(tC[:, k:k + 2, :], tA[:, k:k + 2, :],
                                ps(f"wb {j}.{i}")[:, :].rearrange("p (k t) -> p k t", k=2), ALU.mult).then_inc(dve.tick(f"ev wb {j}.{i}"), 1)
                    dve.eng.wait_ge(*dve.own())
                    tt(tC[:, k:k + 2, :], tC[:, k:k + 2, :], MA[:, k:k + 2, :], ALU.add).then_inc(dve.tick(f"f mix {2 * j + i}"), 1)
            halves_lo("mix", Hl, tC, Hh)
            T.mark("Hl mix", *dve.last)
            for j in range(4):
                split_lo(dve, at_unit[("w_out", j)] + 2)
                dve.eng.wait_ge(*T.at(f"mm w_out {j}"))
                for b in range(2):
                    k = 2 * j + b
                    stt(tA[:, k, :], xT[:, k, :], ALPHA2, ps(f"w_out {j}")[:, b * S:(b + 1) * S],
                                 ALU.mult, ALU.add).then_inc(dve.tick(f"z ln5 {k}"), 1)
                T.mark(f"ev w_out {j}", *dve.last)
            ln("ln5")
            affine("ln_g_2", "ln_b_2", 0)
            dve.stage = "m2"
            T.mark("Hf m2", *dve.last)
            moe_dve(dve, m2)
            rest_dve(dve, m2)
            for k in range(KT):
                stt(tA[:, k, :], xT[:, k, :], ALPHA2, tB[:, k, :], ALU.mult, ALU.add).then_inc(dve.tick(f"z ln6 {k}"), 1)
            ln("ln6")
            affine("ln_g_2", "ln_b_2", 1)
            dve.stage = "ple"
            for j in range(4):
                T.mark(f"f ple {j}", *dve.last)
            halves_lo("ple", Hl, xT, Hh)
            T.mark("Hl ple", *dve.last)
            dve.eng.wait_ge(*T.at("Gh ple"))
            tt(Gl[:, 0:2, :], ps("pT")[:, :].rearrange("p (k t) -> p k t", k=2),
                        Gh[:, 0:2, :].bitcast(F32), ALU.subtract).then_inc(dve.tick("Gl ple"), 1)
            T.mark("ev pT", *dve.last)
            for j in range(4):
                split_lo(dve, at_unit[("pg", j)] + 2)
            for j in range(4):
                dve.eng.wait_ge(*T.at(f"gate p {j}"))
                dve.eng.wait_ge(*T.at(f"mm pp.{j}"))
                s = slice(2 * j, 2 * j + 2)
                tt(tB[:, s, :], tB[:, s, :], ps(f"pp.{j}")[:, :].rearrange("p (k t) -> p k t", k=2),
                            ALU.mult).then_inc(dve.tick(f"ev pp.{j}"), 1)
                dve.eng.wait_ge(*dve.own())
                for k in (2 * j, 2 * j + 1):
                    stt(tA[:, k, :], xT[:, k, :], ALPHA2, tB[:, k, :], ALU.mult, ALU.add).then_inc(dve.tick(f"z ln7 {k}"), 1)
            ln("ln7")
            dve.eng.wait_ge(*dve.own())
            for k in range(KT):
                ts(tD[:, k, :], tA[:, k, :], col("ln_g_2", k, 2), col("ln_b_2", k, 2), ALU.mult, ALU.add).then_inc(dve.tick(), 1)
            T.mark("x out", *dve.last)

    return {**T.marks, "bank": T.banks}


_INS = ["x", "c", "ada_w", "ada_b", "ln_g", "ln_b", "conv_in_w", "conv_in_b", "conv_dw_w", "conv_dw_b",
        "conv_norm_g", "conv_norm_b", "conv_out_w", "conv_out_b", "kv_ada_w", "kv_ada_b", "w_kv", "w_q", "w_o",
        "ffn_w13", "ffn_w2", "router_w", "router_b", "moe_w13", "moe_w2", "p_2", "ln_in_g_2", "ln_in_b_2",
        "rel_bias_2", "w_in_2", "tok_mix_2", "decay_base_2", "decay_up_2", "aaa_base_2", "aaa_up_2",
        "gate_up_2", "k_k_2", "k_a_2", "r_k_2", "gn_g_2", "gn_b_2", "w_branch_attn_2", "w_branch_rwkv_2",
        "w_out_2", "router_grp_2", "router_grp_bias_2", "router_exp_2", "router_exp_bias_2", "exp_gate_2",
        "exp_up_2", "exp_down_2", "ple_proj_2", "ple_gate_2", "ln_g_2", "ln_b_2"]


def kernel(**inputs):
    import numpy as _np
    import concourse.bacc as _bacc
    from concourse import mybir as _mybir
    from concourse.bass_utils import run_bass_kernel_spmd as _run

    arrays = {f"in_{name}": _np.ascontiguousarray(inputs[name]) for name in _INS}

    def program(known):
        nc = _bacc.Bacc("TRN2", target_bir_lowering=False, num_devices=1)
        A = {name: nc.dram_tensor(f"in_{name}", arrays[f"in_{name}"].shape,
                                  _mybir.dt.from_np(arrays[f"in_{name}"].dtype), kind="ExternalInput").ap()
             for name in _INS}
        out = nc.dram_tensor("out_0", inputs["x"].shape, _mybir.dt.float32, kind="ExternalOutput").ap()
        return nc, block_pair(nc, A, out, known)

    _, known = program({})
    nc, _ = program(known)
    r = _run(nc, [arrays], core_ids=[0])
    return r.results[0]["out_0"]
```

```python
import math
from contextlib import ExitStack

import concourse.bass as bass
from concourse import mybir

F32 = mybir.dt.float32
F32R = mybir.dt.float32r
I32 = mybir.dt.int32
ALU = mybir.AluOpType
ACT = mybir.ActivationFunctionType
AX = mybir.AxisListType.X

P = 128
UNIT = 2048
POOL_BLOCKS = 3
SLOTS = 128
RAW, SPLIT = 6, 3
LN_EPS = 1e-5
GN_EPS = 64e-5
NEG = -1e30


class Tally:

    def __init__(self, nc, ctx, known):
        self.nc, self.ctx, self.known = nc, ctx, known
        self.sems, self.count, self.marks = {}, {}, {}
        self.banks, self.rot, self.occupant = {}, {}, {}

    def sem(self, name):
        if name not in self.sems:
            self.sems[name] = self.ctx.enter_context(self.nc.semaphore(name.replace(" ", "_")))
        return self.sems[name]

    def mark(self, label, sem, value):
        self.marks[label] = (sem, value)

    def at(self, label):
        if label not in self.marks and not self.known:
            return self.sem("stored"), 1
        sem, value = self.marks.get(label) or self.known[label]
        return self.sem(sem), value


class Engine:

    def __init__(self, tally, eng, name):
        self.t, self.eng, self.name = tally, eng, name
        self.stage = "start"
        self.last = None

    def tick(self, label=None):
        name = f"{self.name} {self.stage}"
        self.t.count[name] = self.t.count.get(name, 0) + 1
        self.last = (name, self.t.count[name])
        if label:
            self.t.mark(label, *self.last)
        return self.t.sem(name)

    def own(self):
        return self.t.sem(self.last[0]), self.last[1]


class Moe:

    def __init__(self, name, experts, together, chunks, first, groups, f):
        self.name, self.E, self.G, self.first, self.groups = name, experts, together, first, groups
        self.NG = experts // together
        self.NCH = chunks * together
        self.per = 3 * self.NCH
        self.units = self.NG * self.per
        self.f = f

    @staticmethod
    def unit(c, what):
        if what < 2:
            return what if c == 0 else 3 * c - 1 + what
        return 3 * c + 4

    def last_down(self, end):
        return self.per - 1 if end else self.unit(self.NCH - 1, 2)

    def steps(self, eng, g, end, step, inner=None):
        for c in range(1, self.NCH + 1 - (1 if end else 0)):
            if self.G == 1 and 2 <= c < self.NCH - 2:
                continue
            if self.G == 1 and c == self.NCH - 2:
                with eng.Fori(0, (self.NCH - 4) // 2) as jt:
                    for d in range(2):
                        step(2 + d, jt)
            step(c, None)


def col_rows():
    at, n = {}, 0
    for name, rows in (("conv_dw_w", 31), ("conv_dw_b", 1), ("conv_norm_g", 1), ("conv_norm_b", 1),
                       ("conv_out_b", 1), ("conv_in_b", 2), ("ada_b", 12), ("kv_ada_b", 2),
                       ("ln_g", 4), ("ln_b", 4), ("ln_in_g_2", 1), ("ln_in_b_2", 1), ("ln_g_2", 3),
                       ("ln_b_2", 3), ("c", 1), ("tok_mix_2", 3), ("decay_base_2", 1),
                       ("aaa_base_2", 1), ("k_k_2", 1), ("k_a_2", 1), ("r_k_2", 1), ("gn_g_2", 1),
                       ("gn_b_2", 1)):
        at[name] = n
        n += rows
    return at, n


def block_pair(nc, A, out, known):
    D, S = 1024, A["x"].shape[1]
    KT, TT = D // P, S // P
    DEPTH = A["ada_w"].shape[0]
    ALPHA = (2.0 * DEPTH) ** 0.25
    HEADS, HEADS2, DA = 16, 8, 512
    ALPHA2 = 2.0 ** 0.25
    TAPS = A["conv_dw_w"].shape[1]
    PAD = TAPS - 1
    FF = A["ffn_w2"].shape[1]
    NP = FF // 256
    ROW, NROW = col_rows()
    NV = 14

    units = []

    def kmajor(w, c0, cols, kt=KT):
        return w[0:kt * P, c0:c0 + cols].rearrange("(k p) n -> p k n", p=P)

    def add(key, w, c0, cols=256, kt=KT, split=True, r0=0):
        src = w[r0:r0 + kt * P, c0:c0 + cols].rearrange("(k p) n -> p k n", p=P)
        units.append((key, split, kt, cols, src))

    def ada(l, v0, v1):
        for j in range(4 * v0, 4 * v1):
            add(("ada", l, j), A["ada_w"][l], 256 * j, split=False)

    ada(0, 0, 2)
    w = A["conv_in_w"][0]
    for j in range(4):
        add(("conv a", j), w, 256 * j)
        add(("conv g", j), w, D + 256 * j)
    ada(0, 2, 6)
    for j in range(8):
        add(("ada", 2, j), A["kv_ada_w"], 256 * j, split=False)
    for j in range(4):
        add(("conv_out", j), A["conv_out_w"][0], 256 * j)
    w13, w2 = A["ffn_w13"][0], A["ffn_w2"][0]
    late = [("ada", 1, j) for j in range(24)]

    def down(j):
        add(("ffn2", j), w2, 0, D, 2, r0=256 * j)
        for _ in range(3):
            if late:
                key = late.pop(0)
                add(key, A["ada_w"][1], 256 * key[2], split=False)

    for j in range(NP):
        add(("ffn a", j), w13, 256 * j)
        add(("ffn b", j), w13, FF + 256 * j)
        if j:
            down(j - 1)
    down(NP - 1)
    for j in range(4):
        add(("k", j), A["w_kv"], 256 * j)
    for j in range(4):
        add(("v", j), A["w_kv"], D + 256 * j)
    for j in range(4):
        add(("q", j), A["w_q"][0], 256 * j)
    for j in range(4):
        add(("wo", j), A["w_o"][0], 256 * j)

    m1 = Moe("m1", experts=8, together=1, chunks=A["moe_w2"].shape[2] // 256, first=len(units), groups=1,
             f=A["moe_w2"].shape[2])
    for i in range(m1.units):
        units.append(((m1.name, i), True, KT // 2, 512, None))
    w = A["w_in_2"][0]
    RW0 = 3 * DA
    for j in range(7):
        add(("rw", j), w, RW0 + 256 * j)
    add(("rw", 7), w, RW0 + A["tok_mix_2"].shape[1] - P, P)
    for j in range(2):
        add(("v2", j), w, 2 * DA + 256 * j)
    for j in range(2):
        add(("q2", j), w, 256 * j)
    for j in range(2):
        add(("k2", j), w, DA + 256 * j)
    G0 = RW0 + A["tok_mix_2"].shape[1]
    for j in range(4):
        add(("ga", j), w, G0 + 256 * j)
    for j in range(2):
        add(("wa", j), A["w_branch_attn_2"][0], 512 * j, 512, 4)
    for j in range(4):
        add(("gb", j), w, G0 + D + 256 * j)
    for j in range(2):
        add(("wb", j), A["w_branch_rwkv_2"][0], 512 * j, 512, 4)
    for j in range(4):
        add(("w_out", j), A["w_out_2"][0], 256 * j)
    m2 = Moe("m2", experts=32, together=4, chunks=1, first=len(units), groups=4, f=256)
    for i in range(m2.units):
        units.append(((m2.name, i), True, KT // 2, 512, None))
    for j in range(4):
        add(("pg", j), A["ple_gate_2"][0], 256 * j)
    add(("pp", 0), A["ple_proj_2"][0], 0, D, 2)

    at_unit = {u[0]: n for n, u in enumerate(units)}
    split_before = [0]
    for u in units:
        split_before.append(split_before[-1] + u[1])

    with ExitStack() as ctx:
        T = Tally(nc, ctx, known)

        def sb(name, shape, dt=F32):
            return ctx.enter_context(nc.sbuf_tensor(name, shape, dt))

        ring_raw = sb("ring_raw", [P, RAW, UNIT])
        ring_hi = sb("ring_hi", [P, SPLIT, UNIT], F32R)
        ring_lo = sb("ring_lo", [P, SPLIT, UNIT], F32R)
        bank = [ctx.enter_context(nc.psum_tensor(f"bank{i}", [P, 512], F32)) for i in range(8)]
        xT = sb("xT", [P, KT, S])
        Hh, Hl = sb("Hh", [P, KT, S], F32R), sb("Hl", [P, KT, S], F32R)
        g_at = nc.sbuf_base
        Gh, Gl = sb("Gh", [P, KT, S], F32R), sb("Gl", [P, KT, S], F32R)
        GhF = nc.alloc_sbuf_tensor_at("GhF", [P, KT, S], F32, offset=g_at)
        GlF = nc.alloc_sbuf_tensor_at("GlF", [P, KT, S], F32, offset=g_at + 4 * KT * S)
        tA, tB, tC, tD = (sb(n, [P, KT, S]) for n in ("tA", "tB", "tC", "tD"))
        cols = sb("cols", [P, KT, NROW])
        mods = sb("mods", [P, NV, KT])
        uT = sb("uT", [P, KT, PAD + S])
        gb = sb("gb", [P, KT])
        ident = sb("ident", [P, P])
        means = sb("means", [P, P])
        mh_at = nc.sbuf_base
        mh = sb("mh", [P, 4, P], F32R)
        stat = nc.alloc_sbuf_tensor_at("stat", [P, 2, S], F32, offset=mh_at)
        eps = sb("eps", [P, 2])
        warm = sb("warm", [P, 1])
        alibi = sb("alibi", [P, 3 * P])
        pr = sb("pr", [P, 3, 3 * P])
        prT = sb("prT", [P, 3, 3 * P])
        small = sb("small", [P, 3, 6])
        ones = sb("ones", [P, P])
        before = sb("before", [P, P])
        slots = sb("slots", [P, P])
        part = sb("part", [P, 1])
        lower = sb("lower", [P, 8, 8])
        psel_r = sb("psel_r", [P, TT, P], F32R)
        EM, GM = 32, 4
        rw = sb("rw", [P, KT, EM + GM])
        rbias = sb("rbias", [P, EM + GM])
        RT = pr[:, :, :].rearrange("p a b -> p (a b)")[:, 0:12 * TT * EM].rearrange("p (r a e) -> p r a e", r=12, a=TT)
        scr = sb("scr", [P, KT, S])
        m_iu = sb("m_iu", [P, P])[:, :]
        eLC = sb("eLC", [P, 4, 4])
        rmax = sb("rmax", [P, TT, 8])
        pos = sb("pos", [P, 9, TT, GM])
        gates = sb("gates", [P, 9, TT, GM])
        mask = sb("mask", [P, 9, GM])
        posg = sb("posg", [P, TT, GM])
        gateg = sb("gateg", [P, 2, TT, GM])
        maskg = sb("maskg", [P, 2, GM])
        ge = sb("ge", [P, 2, GM])
        most = sb("most", [P, 2])
        overflow = sb("overflow", [P, 1], I32)

        raw_landed = [ctx.enter_context(nc.semaphore(f"raw_landed{i}")) for i in range(RAW)]
        for i in range(RAW):
            T.sems[f"raw_landed {i}"] = raw_landed[i]

        def view(ring, slot, kt, n):
            return ring[:, slot, 0:kt * n].rearrange("p (k n) -> p k n", k=kt)

        def weights(n):
            key, split, kt, c, _ = units[n]
            if split:
                s = split_before[n] % SPLIT
                return view(ring_hi, s, kt, c), view(ring_lo, s, kt, c)
            return view(ring_raw, n % RAW, kt, c), None

        def landed(e, n):
            e.eng.wait_ge(T.sem(f"raw_landed {n % RAW}"), 32 * (n // RAW + 1))

        GROUPS = {"A": [0, 1, 2, 3], "B": [4, 5], "C": [6, 7], "D": [4, 5, 6, 7]}

        def take(pe, job, group="A"):
            i = T.rot.get(group, 0)
            T.rot[group] = i + 1
            b = GROUPS[group][i % len(GROUPS[group])]
            if T.occupant.get(b):
                pe.eng.wait_ge(*T.at("ev " + T.occupant[b]))
            T.occupant[b] = job
            T.banks[job] = b
            return bank[b]

        def ps(job):
            return bank[T.known.get("bank", {}).get(job, 0)]

        VEC = lambda l, v: 6 * l + v
        def mod(l, v, kt):
            return mods[:, VEC(l, v), kt:kt + 1]

        def col(name, kt, i=0):
            r = ROW[name] + i
            return cols[:, kt, r:r + 1]

        flat = lambda t: t[:, :, :].rearrange("p a b -> p (a b)")
        uF = flat(uT)
        relb = uF[:, 0:HEADS2 * S].rearrange("p (h k) -> p h k", h=HEADS2)
        rel = flat(tC)[0:HEADS2, 1024:1024 + 3 * P]
        du, gu1, gu2 = (flat(scr)[:, 512 * i:512 * i + 512] for i in range(3))
        Q2, K2 = tD[:, 0:4, :], tD[:, 4:8, :]
        V2 = tC[:, 0:4, :].rearrange("p (a k) t -> p a (k t)", a=TT)
        MA = GlF[:, :, :]
        prF, prTF, sF, gF = flat(pr), flat(prT), flat(scr), flat(GhF)
        m_su, m_sl16, m_d16 = (alibi[:, P * i:P * i + P] for i in range(3))
        m_o32, m_o64, m_d64 = prF[:, 1024:1152], prTF[:, 1024:1152], uF[:, 2048:2176]
        four = lambda t: t.rearrange("p (i n) -> p i n", i=4)
        bc4 = lambda m: m.unsqueeze(1).to_broadcast([P, 4, P])
        rt_, kt_, bt_, at_ = tA[:, 0:4, :], tA[:, 4:8, :], tC[:, 4:8, :], tD[:, 0:4, :]
        bonus, gg = tC[:, 0:4, :], tD[:, 4:8, :]
        Vtok = tB[:, 4:8, :].rearrange("p (a k) t -> p a (k t)", a=TT)
        XA = flat(tB)[:, 0:1024].rearrange("p (h t) -> p h t", h=HEADS2)
        ArbT = uF[:, 0:1024].rearrange("p (h t) -> p h t", h=HEADS2)
        ArkT = uF[:, 1024:2048].rearrange("p (h t) -> p h t", h=HEADS2)
        mS, mAt, mSt = (prF[:, 0:512], prTF[:, 0:512]), prF[:, 512:1024], prTF[:, 512:1024]
        mT = stat[:, :, :].rearrange("p a b -> p (a b)")
        ktok, btok, ZV, Pm = (gF[:, 512 * i:512 * i + 512] for i in range(4))
        U, Sbd = sF[:, 0:512], sF[:, 512:1024]
        yT = scr[:, 4:8, :]

        tok_hi = Gh[:, :, :].rearrange("p (a k) t -> p a (k t)", a=TT)
        tok_lo = Gl[:, :, :].rearrange("p (a k) t -> p a (k t)", a=TT)
        xg_hi, xg_lo = ([t[:, :, 0:P], t[:, :, P:2 * P]] for t in (Hh, Hl))
        mh_hi, mh_lo = mh[:, 0:2, :], mh[:, 2:4, :]
        ysb = tA[:, 0:4, :].rearrange("p k t -> p (k t)")
        pself = [tA[:, 4 + i, :].rearrange("p (a s) -> p a s", a=TT) for i in range(2)]
        pselT = [tA[:, 6 + i, :] for i in range(2)]

        cpad = scr[:, 0, :].rearrange("p (k m) -> p k m", k=KT)
        pairs = [(0, p) for p in range(12)] + [(2, p) for p in range(4)] + [(1, p) for p in range(12)]
        at_pair = {p: n for n, p in enumerate(pairs)}

        def ada_row(pair):
            r = 2 + 2 * (at_pair[pair] % 3)
            return scr[:, r:r + 2, :].rearrange("p k t -> p (k t)")

        nxt = {"act": 0, "dve": 0}

        def split_hi(act, upto):
            while nxt["act"] <= min(upto, len(units) - 1):
                n = nxt["act"]
                if units[n][4] is None:
                    break
                nxt["act"] += 1
                key, split, kt, c, _ = units[n]
                if not split:
                    continue
                i = split_before[n]
                landed(act, n)
                if i >= SPLIT:
                    act.eng.wait_ge(T.sem("unit_done"), after_split(i - SPLIT) + 1)
                nc.scalar.activation(ring_hi[:, i % SPLIT, 0:kt * c], ring_raw[:, n % RAW, 0:kt * c],
                                     ACT.Copy).then_inc(T.sem("hi_done"), 1)

        def split_lo(dve, upto):
            while nxt["dve"] <= min(upto, len(units) - 1):
                n = nxt["dve"]
                if units[n][4] is None:
                    break
                nxt["dve"] += 1
                key, split, kt, c, _ = units[n]
                if not split:
                    continue
                i = split_before[n]
                landed(dve, n)
                dve.eng.wait_ge(T.sem("hi_done"), i + 1)
                if i >= SPLIT:
                    dve.eng.wait_ge(T.sem("unit_done"), after_split(i - SPLIT) + 1)
                nc.vector.tensor_tensor(ring_lo[:, i % SPLIT, 0:kt * c], ring_raw[:, n % RAW, 0:kt * c],
                                        ring_hi[:, i % SPLIT, 0:kt * c].bitcast(F32),
                                        ALU.subtract).then_inc(T.sem("lo_done"), 1)

        split_units = [n for n, u in enumerate(units) if u[1]]
        after_split = lambda i: split_units[i]

        def attention(pe, name, heads, Q, K, V):
            mm = nc.tensor.matmul
            bank_o = {}
            for i in range(heads + 3):
                if i < heads:
                    h = i
                    b = take(pe, f"{name} s {h}")
                    k, r = h // 2, slice(64 * (h % 2), 64 * (h % 2) + 64)
                    pe.eng.wait_ge(*T.at(f"{name} qT {k // 2}"))
                    pe.eng.wait_ge(*T.at(f"{name} kT {k // 2}"))
                    mm(b[:, 0:P], Q[r, k, 0:P], K[r, k, 0:P], start=True, stop=True)
                    mm(b[:, P:3 * P], Q[r, k, P:S], K[r, k, :], start=True, stop=True).then_inc(pe.tick(f"mm {name} s {h}"), 1)
                if 2 <= i < heads + 2:
                    h = i - 2
                    b = take(pe, f"{name} pT {h}", "B")
                    pe.eng.wait_ge(*T.at(f"{name} p {h}"))
                    for c in range(3):
                        last = nc.tensor.transpose(b[:, c * P:(c + 1) * P], pr[:, h % 3, c * P:(c + 1) * P],
                                                   ident[:, :])
                    last.then_inc(pe.tick(f"mm {name} pT {h}"), 1)
                if i >= 3:
                    h = i - 3
                    k, r = h // 2, slice(64 * (h % 2), 64 * (h % 2) + 64)
                    if h % 2 == 0:
                        bank_o[k] = take(pe, f"{name} o {k}", "C")
                    b = bank_o[k]
                    pe.eng.wait_ge(*T.at(f"{name} pT {h}"))
                    pe.eng.wait_ge(*T.at(f"{name} v"))
                    hs = slice(64 * h, 64 * h + 64)
                    mm(b[r, 0:S], V[:, 0, hs], prT[:, h % 3, 0:2 * P], start=True, stop=False,
                       skip_group_check=True)
                    mm(b[r, P:S], V[:, 1, hs], prT[:, h % 3, 2 * P:3 * P], start=False, stop=True,
                               skip_group_check=True).then_inc(pe.tick(f"mm {name} o {h}"), 1)

        def rwkv_pe(pe):
            mm = nc.tensor.matmul
            pe.stage = "rwkv"

            def job(name, body, waits=()):
                b = take(pe, name)
                for label in waits:
                    pe.eng.wait_ge(*T.at(label))
                body(b).then_inc(pe.tick("mm " + name), 1)

            def each(n, one):
                def body(b):
                    for i in range(n):
                        last = one(b, i)
                    return last
                return body

            pe.eng.wait_ge(*T.at("lora landed"))
            for j in range(2):
                blk = lambda w, i: w[:, (2 * j + i) * P:(2 * j + i + 1) * P]
                job(f"zw {j}", each(2, lambda b, i: mm(b[:, i * S:(i + 1) * S], blk(du[0:64, :], i),
                                                           tB[0:64, 7, :], start=True, stop=True)), ["tanh w"])
                job(f"za {j}", each(2, lambda b, i: mm(b[:, i * S:(i + 1) * S], blk(du[64:P, :], i),
                                                           tB[64:P, 4, :], start=True, stop=True)), ["mix 7"])

                def gate(b, i):
                    mm(b[:, i * S:(i + 1) * S], blk(gu1, i), tB[:, 5, :], start=True, stop=False)
                    return mm(b[:, i * S:(i + 1) * S], blk(gu2, i), tB[:, 6, :], start=False, stop=True)
                job(f"gg {j}", each(2, gate), ["sigmoid g"])
            pe.eng.wait_ge(*T.at("chunk masks"))
            for a in range(TT):
                job(f"vtok {a}", each(4, lambda b, i: nc.tensor.transpose(
                    b[:, i * P:(i + 1) * P], tB[:, i, a * P:(a + 1) * P], ident[:, :])), ["mix 7"])
            for name, tile, w in (("ss", lambda k: tC[:, k, :], "k squared"), ("rk", lambda k: tC[:, k, :], "r k")):
                for j in range(2):
                    job(f"{name} {j}", each(2, lambda b, i: mm(b[:, i * S:(i + 1) * S], m_d64,
                                                                   tile(2 * j + i), start=True, stop=True)), [w])
            pe.eng.wait_ge(*T.at("decayed"))
            for a in range(TT):
                cs = slice(a * P, (a + 1) * P)
                for name, src in (("ktok", kt_), ("btok", bt_)):
                    job(f"{name} {a}", each(4, lambda b, i: nc.tensor.transpose(
                        b[:, i * P:(i + 1) * P], src[:, i, cs], ident[:, :])))
                for q in range(2):
                    r = slice(64 * q, 64 * q + 64)
                    n = f"{a} {q}"

                    def outer(l, rr):
                        return each(4, lambda b, i: mm(b[:, i * P:(i + 1) * P], l[r, i, cs], rr[r, i, cs],
                                                       start=True, stop=True))
                    job(f"A {n}", outer(at_, bt_))
                    job(f"At {n}", outer(bt_, at_))
                    job(f"Mak {n}", outer(kt_, at_))
                    X = lambda i: XA[:, 2 * i + q, :]

                    def prod(l, rr):
                        return each(4, lambda b, i: mm(b[:, i * P:(i + 1) * P], l(i), rr(i), start=True, stop=True))
                    f4 = lambda t: (lambda i: t[:, i * P:(i + 1) * P])
                    pe.eng.wait_ge(*T.at(f"TX {n} 0"))
                    job(f"S2 {n} 0", prod(f4(mSt), f4(mS[0])))
                    job(f"S2t {n} 0", prod(f4(mS[0]), f4(mSt)))
                    pe.eng.wait_ge(*T.at(f"Mak {n}"))
                    pe.eng.wait_ge(*T.at("Vtok"))
                    job(f"ZV {n}", each(4, lambda b, i: mm(
                        b[:, i * 64:i * 64 + 64], mS[1][:, i * P:(i + 1) * P],
                        Vtok[:, a, 128 * i + 64 * q:128 * i + 64 * q + 64], start=True, stop=True)))
                    job(f"Arb {n}", outer(bt_, rt_))
                    job(f"Ark {n}", outer(kt_, rt_))
                    for lev in range(3):
                        pe.eng.wait_ge(*T.at(f"S2 {n} {lev}"))
                        power = mS[(lev + 1) % 2]
                        if lev < 2:
                            job(f"S2 {n} {lev + 1}", prod(f4(mSt), f4(power)))
                        if lev < 1:
                            job(f"S2t {n} {lev + 1}", prod(f4(power), f4(mSt)))
                        pe.eng.wait_ge(*T.at(f"TX {n} {lev}"))
                        job(f"XS {n} {lev}", prod(f4(power), X))
                    for o in range(2):
                        pe.eng.wait_ge(*T.at(f"TX {n} {3 + o}"))
                        job(f"TR {n} {o}", each(4, lambda b, i: nc.tensor.transpose(
                            b[:, i * P:(i + 1) * P], X(i), ident[:, :])))
                        pe.eng.wait_ge(*T.at(f"off {n} {o}"))
                        pe.eng.wait_ge(*T.at(f"ev TR {n} {o}"))
                        job(f"Q {n} {o}", prod(f4(mSt), f4(mT)))
                        pe.eng.wait_ge(*T.at(f"ev Q {n} {o}"))
                        job(f"XQ {n} {o}", prod(f4(mS[0]), X))
                    pe.eng.wait_ge(*T.at(f"TX {n} 5"))
                ys = take(pe, f"ys {a}", "C")
                for cc in range(2):
                    c = 2 * a + cc
                    b0 = slice(64 * cc, 64 * cc + 64)
                    t64 = slice(a * P + 64 * cc, a * P + 64 * cc + 64)
                    pe.eng.wait_ge(*T.at(f"S {c}"))
                    job(f"P {c}", each(4, lambda b, i: mm(b[b0, i * P:(i + 1) * P], at_[:, i, t64],
                                                              Sbd[:, i * P:(i + 1) * P], start=True, stop=True)))
                    for i in range(4):
                        last = mm(ys[:, i * P + 64 * cc:i * P + 64 * cc + 64], Sbd[:, i * P:(i + 1) * P],
                                  rt_[:, i, t64], start=True, stop=True)
                    last.then_inc(pe.tick(f"mm ys {a}"), 1)
                    pe.eng.wait_ge(*T.at(f"P {c}"))
                    job(f"U {c}", each(8, lambda b, h: mm(b[b0, 64 * h:64 * h + 64], XA[b0, h, b0],
                                                              Pm[b0, 64 * h:64 * h + 64], start=True, stop=True)))
                    pe.eng.wait_ge(*T.at(f"U {c}"))
                    pe.eng.wait_ge(*T.at(f"tok {a}"))

                    def state(b, i):
                        ks = slice(i * P, (i + 1) * P)
                        mm(b[:, ks], ktok[b0, ks], Vtok[b0, a, ks], start=True, stop=False)
                        return mm(b[:, ks], btok[b0, ks], U[b0, ks], start=False, stop=True)
                    if c < 3:
                        job(f"S {c}", each(4, state))
                yu = take(pe, f"yu {a}", "B")
                pe.eng.wait_ge(*T.at(f"Ark {a} 1"))
                pe.eng.wait_ge(*T.at(f"Arb {a} 1"))
                for h in range(HEADS2):
                    o = yu[64 * (h % 2):64 * (h % 2) + 64, (h // 2) * P:(h // 2 + 1) * P]
                    hs = slice(64 * h, 64 * h + 64)
                    mm(o, U[:, hs], ArbT[:, h, :], start=True, stop=False, skip_group_check=True)
                    last = mm(o, Vtok[:, a, hs], ArkT[:, h, :], start=False, stop=True, skip_group_check=True)
                last.then_inc(pe.tick(f"mm yu {a}"), 1)
            for name, tile, w in (("gm", lambda k: yT[:, k, :], "y 1"), ("gv", lambda k: GhF[:, k, :], "y squared")):
                for j in range(2):
                    job(f"{name} {j}", each(2, lambda b, i: mm(b[:, i * S:(i + 1) * S], m_d64,
                                                                   tile(2 * j + i), start=True, stop=True)), [w])

        def rwkv_act(act):
            run = nc.scalar.activation
            act.stage = "rwkv"
            act.eng.wait_ge(*T.at("mix 7"))
            run(tB[0:64, 7, :], tB[0:64, 4, :], ACT.Tanh).then_inc(act.tick("tanh w"), 1)
            run(tB[:, 5:7, :], tB[:, 5:7, :], ACT.Sigmoid).then_inc(act.tick("sigmoid g"), 1)
            for j in range(2):
                act.eng.wait_ge(*T.at(f"mm zw {j}"))
                for i in range(2):
                    run(tC[:, 2 * j + i, :], ps(f"zw {j}")[:, i * S:(i + 1) * S], ACT.Sigmoid,
                                 bias=col("decay_base_2", 2 * j + i)).then_inc(act.tick(f"ev zw {j}"), 1)
                act.eng.wait_ge(*T.at(f"mm za {j}"))
                for i in range(2):
                    run(tC[:, 4 + 2 * j + i, :], ps(f"za {j}")[:, i * S:(i + 1) * S], ACT.Sigmoid,
                                 bias=col("aaa_base_2", 2 * j + i)).then_inc(act.tick(f"ev za {j}"), 1)
                act.eng.wait_ge(*T.at(f"mm gg {j}"))
                run(gg[:, 2 * j:2 * j + 2, :], ps(f"gg {j}")[:, :].rearrange("p (k t) -> p k t", k=2),
                             ACT.Copy).then_inc(act.tick(f"ev gg {j}"), 1)
            T.mark("w a g", *act.last)
            for a in range(TT):
                act.eng.wait_ge(*T.at(f"mm vtok {a}"))
                run(Vtok[:, a, :], ps(f"vtok {a}")[:, :], ACT.Copy).then_inc(act.tick(f"ev vtok {a}"), 1)
            T.mark("Vtok", *act.last)
            act.eng.wait_ge(*T.at("k k_k"))
            act.eng.wait_ge(*T.at("ld done"))
            run(tC[:, 0:4, :], tD[:, 0:4, :], ACT.Square).then_inc(act.tick("k squared"), 1)
            act.eng.wait_ge(*T.at("norm2"))
            run(tC[:, 0:4, :], tC[:, 0:4, :], ACT.Sqrt).then_inc(act.tick("norm"), 1)
            act.eng.wait_ge(*T.at("L done"))
            act.eng.wait_ge(*T.at("mm wa 1.1"))
            run(GhF[:, 0:4, :], four(uF[:, 0:1024]), ACT.Exp).then_inc(act.tick(), 1)
            run(GhF[:, 4:8, :], four(uF[:, 0:1024]), ACT.Exp, scale=-1.0).then_inc(act.tick(), 1)
            run(four(uF[:, 1024:2048]), four(uF[:, 1024:2048]), ACT.Exp).then_inc(act.tick(), 1)
            ends = GhF[:, 0:4, :].rearrange("p k (c t) -> p k c t", t=64)[:, :, :, 63]
            act.eng.wait_ge(*act.own())
            run(eLC[:, :, :], ends, ACT.Copy).then_inc(act.tick("exps"), 1)
            act.eng.wait_ge(*T.at("decayed"))
            for a in range(TT):
                for name, dst in (("ktok", ktok), ("btok", btok)):
                    act.eng.wait_ge(*T.at(f"mm {name} {a}"))
                    if a:
                        act.eng.wait_ge(*T.at("mm S 1"))
                        act.eng.wait_ge(*T.at(f"mm ys {0}"))
                    run(dst, ps(f"{name} {a}")[:, :], ACT.Copy).then_inc(act.tick(f"ev {name} {a}"), 1)
                T.mark(f"tok {a}", *act.last)
                for q in range(2):
                    n = f"{a} {q}"
                    act.eng.wait_ge(*T.at(f"mm ZV {n}"))
                    zv = ZV.rearrange("p (i q v) -> p i q v", i=4, q=2)[:, :, q, :]
                    if a and q == 0:
                        act.eng.wait_ge(*T.at("P 1"))
                    run(zv, ps(f"ZV {n}")[:, 0:256].rearrange("p (i v) -> p i v", i=4), ACT.Copy).then_inc(act.tick(f"ev ZV {n}"), 1)
                    for lev in range(3):
                        last = f"S2t {n} {lev}" if lev < 2 else f"S2 {n} {lev}"
                        act.eng.wait_ge(*T.at("mm " + last))
                        run(mS[(lev + 1) % 2], ps(f"S2 {n} {lev}")[:, :], ACT.Copy)\
                            .then_inc(act.tick(f"ev S2 {n} {lev}"), 1)
                        if lev < 2:
                            run(mSt, ps(f"S2t {n} {lev}")[:, :], ACT.Copy).then_inc(act.tick(f"ev S2t {n} {lev}"), 1)
                        T.mark(f"S2 {n} {lev}", *act.last)
                    for o in range(2):
                        act.eng.wait_ge(*T.at(f"mm TR {n} {o}"))
                        run(mT, ps(f"TR {n} {o}")[:, :], ACT.Copy).then_inc(act.tick(f"ev TR {n} {o}"), 1)
                        act.eng.wait_ge(*T.at(f"mm Q {n} {o}"))
                        run(mS[0], ps(f"Q {n} {o}")[:, :], ACT.Copy).then_inc(act.tick(f"ev Q {n} {o}"), 1)
                for cc in range(2):
                    c = 2 * a + cc
                    b0 = slice(64 * cc, 64 * cc + 64)
                    act.eng.wait_ge(*T.at(f"mm U {c}"))
                    if a:
                        act.eng.wait_ge(*T.at("mm yu 0"))
                    run(U[b0, :], ps(f"U {c}")[b0, :], ACT.Copy).then_inc(act.tick(f"ev U {c}"), 1)
                    T.mark(f"U {c}", *act.last)
                act.eng.wait_ge(*T.at(f"mm ys {a}"))
                run(yT[:, :, a * P:(a + 1) * P], four(ps(f"ys {a}")[:, :]), ACT.Copy).then_inc(act.tick(f"ev ys {a}"), 1)
            act.eng.wait_ge(*T.at("y centred"))
            run(GhF[:, 0:4, :], yT, ACT.Square).then_inc(act.tick("y squared"), 1)
            for j in range(2):
                act.eng.wait_ge(*T.at(f"mm gv {j}"))
                run(GhF[:, 4 + 2 * j:6 + 2 * j, :], ps(f"gv {j}")[:, :].rearrange("p (k t) -> p k t", k=2),
                             ACT.Sqrt, scale=1.0 / 64, bias=eps[:, 1:2]).then_inc(act.tick(f"ev gv {j}"), 1)
            T.mark("y std", *act.last)
            act.eng.wait_ge(*T.at("y out"))
            run(Gh[:, 0:4, :], yT, ACT.Copy).then_inc(act.tick("Gh wb"), 1)

        def rwkv_dve(dve):
            tt, ts, stt = nc.vector.tensor_tensor, nc.vector.tensor_scalar, nc.vector.scalar_tensor_tensor
            dve.stage = "rwkv"
            dve.eng.wait_ge(*T.at("w a g"))
            dve.eng.wait_ge(*T.at("routing constants"))
            for j in range(2):
                s = slice(2 * j, 2 * j + 2)
                ts(tC[:, s, :], tC[:, s, :], -math.exp(-0.5), None, ALU.mult).then_inc(dve.tick(), 1)
            dve.eng.wait_ge(*T.at("mix 7"))
            for k in range(4):
                ts(tD[:, k, :], tA[:, 4 + k, :], col("k_k_2", k), None, ALU.mult).then_inc(dve.tick(), 1)
            T.mark("k k_k", *dve.last)
            dve.eng.wait_ge(*dve.own())
            for k in range(4):
                for c in range(4):
                    cs = slice(64 * c, 64 * c + 64)
                    nc.vector.tensor_tensor_scan(uF[:, 256 * k + 64 * c:256 * k + 64 * c + 64],
                                                          ones[:, 0:64], tC[:, k, cs], 0.0, ALU.mult, ALU.add).then_inc(dve.tick(), 1)
            dve.eng.wait_ge(*dve.own())
            tt(four(uF[:, 1024:2048]), four(uF[:, 0:1024]), tC[:, 0:4, :], ALU.subtract).then_inc(dve.tick("L done"), 1)
            T.mark("ld done", *dve.last)
            for j in range(2):
                dve.eng.wait_ge(*T.at(f"mm ss {j}"))
                ts(tC[:, 2 * j:2 * j + 2, :], ps(f"ss {j}")[:, :].rearrange("p (k t) -> p k t", k=2),
                            1e-24, None, ALU.max).then_inc(dve.tick(f"ev ss {j}"), 1)
            T.mark("norm2", *dve.last)
            dve.eng.wait_ge(*T.at("norm"))
            nc.vector.reciprocal(tC[:, 0:4, :], tC[:, 0:4, :]).then_inc(dve.tick(), 1)
            dve.eng.wait_ge(*dve.own())
            tt(tD[:, 0:4, :], tD[:, 0:4, :], tC[:, 0:4, :], ALU.mult).then_inc(dve.tick(), 1)
            dve.eng.wait_ge(*dve.own())
            for k in range(4):
                ts(tC[:, k, :], tC[:, 4 + k, :], 1.0, col("k_a_2", k), ALU.subtract, ALU.mult).then_inc(dve.tick(), 1)
            dve.eng.wait_ge(*dve.own())
            tt(tC[:, 4:8, :], tC[:, 4:8, :], tD[:, 0:4, :], ALU.mult).then_inc(dve.tick(), 1)
            dve.eng.wait_ge(*dve.own())
            for k in range(4):
                stt(tA[:, 4 + k, :], tC[:, k, :], 1.0, tA[:, 4 + k, :], ALU.add, ALU.mult).then_inc(dve.tick(), 1)
            dve.eng.wait_ge(*dve.own())
            for k in range(4):
                stt(tC[:, k, :], tA[:, 4 + k, :], col("r_k_2", k), tA[:, k, :], ALU.mult, ALU.mult).then_inc(dve.tick(), 1)
            T.mark("r k", *dve.last)
            dve.eng.wait_ge(*dve.own())
            dve.eng.wait_ge(*T.at("exps"))
            tt(rt_, rt_, GhF[:, 0:4, :], ALU.mult).then_inc(dve.tick(), 1)
            tt(kt_, kt_, GhF[:, 4:8, :], ALU.mult).then_inc(dve.tick(), 1)
            tt(bt_, bt_, GhF[:, 4:8, :], ALU.mult).then_inc(dve.tick(), 1)
            stt(at_.rearrange("p k t -> p (k t)"), at_.rearrange("p k t -> p (k t)"), -1.0,
                         uF[:, 1024:2048], ALU.mult, ALU.mult).then_inc(dve.tick(), 1)
            T.mark("decayed", *dve.last)
            for j in range(2):
                s = slice(2 * j, 2 * j + 2)
                dve.eng.wait_ge(*T.at(f"mm rk {j}"))
                dve.eng.wait_ge(*T.at("mm rk 1"))
                tt(tC[:, s, :], tB[:, s, :], ps(f"rk {j}")[:, :].rearrange("p (k t) -> p k t", k=2),
                            ALU.mult).then_inc(dve.tick(f"ev rk {j}"), 1)
            nc.vector.memset(Sbd, 0.0).then_inc(dve.tick("S 0"), 1)
            dve.eng.wait_ge(*T.at("chunk masks"))
            dve.eng.wait_ge(*T.at("ev vtok 1"))
            for a in range(TT):
                for q in range(2):
                    n = f"{a} {q}"

                    def masked(job, dst, mask, waits=()):
                        dve.eng.wait_ge(*T.at("mm " + job))
                        for label in waits:
                            dve.eng.wait_ge(*T.at(label))
                        tt(dst, four(ps(job)[:, :]), bc4(mask), ALU.mult).then_inc(dve.tick("ev " + job), 1)
                        T.mark(job, *dve.last)
                    by_head = lambda t: t.rearrange("p (i q) t -> p i q t", q=2)[:, :, q, :]
                    masked(f"A {n}", four(mS[0]), m_sl16)
                    masked(f"At {n}", four(mAt), m_su)
                    masked(f"Mak {n}", four(mS[1]), m_su)
                    dve.eng.wait_ge(*T.at(f"At {n}"))
                    tt(four(mSt), four(mAt), bc4(m_d16), ALU.mult).then_inc(dve.tick(), 1)
                    dve.eng.wait_ge(*dve.own())
                    if a:
                        dve.eng.wait_ge(*T.at("mm U 1"))
                    tt(by_head(XA), four(mSt), bc4(ident[:, :]), ALU.add).then_inc(dve.tick(f"TX {n} 0"), 1)
                    late = ["mm yu 0"] if a else []
                    masked(f"Arb {n}", by_head(ArbT), m_iu, late)
                    masked(f"Ark {n}", by_head(ArkT), m_iu)

                    def add(job):
                        dve.eng.wait_ge(*T.at("mm " + job))
                        tt(by_head(XA), by_head(XA), four(ps(job)[:, :]), ALU.add).then_inc(dve.tick("ev " + job), 1)
                    for lev in range(3):
                        add(f"XS {n} {lev}")
                        T.mark(f"TX {n} {lev + 1}", *dve.last)
                    for o, mk in enumerate((m_o32, m_o64)):
                        tt(four(mSt), four(mAt), bc4(mk), ALU.mult).then_inc(dve.tick(f"off {n} {o}"), 1)
                        add(f"XQ {n} {o}")
                        T.mark(f"TX {n} {4 + o}", *dve.last)
                for cc in range(2):
                    c = 2 * a + cc
                    b0 = slice(64 * cc, 64 * cc + 64)
                    dve.eng.wait_ge(*T.at(f"mm P {c}"))
                    dve.eng.wait_ge(*T.at(f"ev ZV {a} 1"))
                    tt(Pm[b0, :], ps(f"P {c}")[b0, :], ZV[b0, :], ALU.add).then_inc(dve.tick(f"ev P {c}"), 1)
                    T.mark(f"P {c}", *dve.last)
                    if c < 3:
                        dve.eng.wait_ge(*T.at(f"mm S {c}"))
                        tt(Sbd, Sbd, ps(f"S {c}")[:, :], ALU.add).then_inc(dve.tick(f"ev S {c}"), 1)
                        dve.eng.wait_ge(*dve.own())
                        tt(four(Sbd), four(Sbd), bc4(m_d64), ALU.mult).then_inc(dve.tick(), 1)
                        dve.eng.wait_ge(*dve.own())
                        tt(four(Sbd), four(Sbd), eLC[:, :, c].unsqueeze(2).to_broadcast([P, 4, P]),
                                    ALU.mult).then_inc(dve.tick(f"S {c + 1}"), 1)
                dve.eng.wait_ge(*T.at(f"ev ys {a}"))
                dve.eng.wait_ge(*T.at(f"mm yu {a}"))
                o = yT[:, :, a * P:(a + 1) * P]
                tt(o, o, four(ps(f"yu {a}")[:, :]), ALU.add).then_inc(dve.tick(f"ev yu {a}"), 1)
                T.mark(f"y {a}", *dve.last)
            for j in range(2):
                o = yT[:, 2 * j:2 * j + 2, :].rearrange("p k t -> p (k t)")
                dve.eng.wait_ge(*T.at(f"mm gm {j}"))
                dve.eng.wait_ge(*T.at("mm gm 1"))
                stt(o, ps(f"gm {j}")[:, :], -1.0 / 64, o, ALU.mult, ALU.add).then_inc(dve.tick(f"ev gm {j}"), 1)
            T.mark("y centred", *dve.last)
            dve.eng.wait_ge(*T.at("y std"))
            nc.vector.reciprocal(GhF[:, 4:8, :], GhF[:, 4:8, :]).then_inc(dve.tick(), 1)
            dve.eng.wait_ge(*dve.own())
            tt(yT, yT, GhF[:, 4:8, :], ALU.mult).then_inc(dve.tick(), 1)
            dve.eng.wait_ge(*dve.own())
            for k in range(4):
                ts(yT[:, k, :], yT[:, k, :], col("gn_g_2", k), col("gn_b_2", k), ALU.mult, ALU.add).then_inc(dve.tick(), 1)
            dve.eng.wait_ge(*dve.own())
            tt(yT, yT, bonus, ALU.add).then_inc(dve.tick(), 1)
            dve.eng.wait_ge(*dve.own())
            tt(yT, yT, gg, ALU.mult).then_inc(dve.tick("y out"), 1)
            dve.eng.wait_ge(*T.at("Gh wb"))
            tt(Gh[:, 4:8, :], yT, Gh[:, 0:4, :].bitcast(F32), ALU.subtract).then_inc(dve.tick("Gl wb"), 1)

        def moe_pe(pe, m, H):
            mm, eng, nm = nc.tensor.matmul, pe.eng, m.name
            n_log = m.E + (m.groups if m.groups > 1 else 0)
            b = take(pe, nm + " logits")
            pe.eng.wait_ge(*T.at(f"{nm} router landed"))
            pe.eng.wait_ge(*T.at(f"Hf {nm}"))
            for a in range(TT):
                for k in range(KT):
                    last = mm(b[:, a * n_log:(a + 1) * n_log], H[:, k, a * P:(a + 1) * P], rw[:, k, 0:n_log],
                              start=(k == 0), stop=(k == KT - 1))
            last.then_inc(pe.tick(f"mm {nm} logits"), 1)
            for j in range(4):
                b = take(pe, f"{nm} tok {j}")
                for a in range(TT):
                    for k in range(2):
                        last = nc.tensor.transpose(b[:, (2 * a + k) * P:(2 * a + k + 1) * P],
                                                   H[:, 2 * j + k, a * P:(a + 1) * P], ident[:, :])
                last.then_inc(pe.tick(f"mm {nm} tok {j}"), 1)
            b = take(pe, nm + " count")
            pe.eng.wait_ge(*T.at(f"{nm} sel"))
            pe.eng.wait_ge(*T.at("routing constants"))
            sel = RT[:, 0, :, 0:m.E]
            mm(b[:, 0:m.E], before[:, :], sel[:, 0, :], start=True, stop=True)
            mm(b[:, m.E:2 * m.E], ones[:, :], sel[:, 0, :], start=True, stop=False)
            mm(b[:, m.E:2 * m.E], before[:, :], sel[:, 1, :], start=False, stop=True)
            for a in range(TT):
                last = mm(b[:, 2 * m.E:3 * m.E], ones[:, :], sel[:, a, :], start=(a == 0), stop=(a == 1))
            last.then_inc(pe.tick(f"mm {nm} count"), 1)
            for b_ in range(8):
                if T.occupant.get(b_):
                    pe.eng.wait_ge(*T.at("ev " + T.occupant[b_]))
                T.occupant[b_] = None

            S_ = lambda what: T.sem(f"{nm}_{what}")
            U, SB = m.first, split_before[m.first]

            def halves(g, i0, more=None):
                v = g * m.per + (SB + i0 + 1)
                if more is not None:
                    v = v + more
                eng.wait_ge(T.sem("hi_done"), v)
                eng.wait_ge(T.sem("lo_done"), v)
                s = (SB + i0) % SPLIT
                return ring_hi[:, s, :], ring_lo[:, s, :]

            def up(g, c, h, par, more=None, q=None):
                if h == 0:
                    eng.wait_ge(S_("hidden"), q + 1)
                wh, wl = halves(g, m.unit(c, h), more)
                o = bank[c % 2][:, :]
                wh = wh.rearrange("p (k n) -> p k n", n=512)
                wl = wl.rearrange("p (k n) -> p k n", n=512)
                for k in range(4):
                    kk = 4 * h + k
                    mm(o, xg_hi[par][:, kk, :], wh[:, k, :], start=(kk == 0), stop=False)
                    mm(o, xg_lo[par][:, kk, :], wh[:, k, :], start=False, stop=False)
                    last = mm(o, xg_hi[par][:, kk, :], wl[:, k, :], start=False, stop=(kk == KT - 1))
                last.then_inc(T.sem("unit_done"), 1)

            def turn(c, q):
                eng.wait_ge(S_("hidden"), q + 3)
                for k in range(2):
                    last = nc.tensor.transpose(bank[2][:, k * P:(k + 1) * P],
                                               tC[:, 2 + c % 2, k * P:(k + 1) * P], ident[:, :])
                last.then_inc(S_("turned"), 1)

            def down(g, c, i0, more, q, first):
                wh, wl = halves(g, i0, more)
                eng.wait_ge(S_("turned_lo"), q + 1)
                wh = wh.rearrange("p (k n) -> p k n", n=D)
                wl = wl.rearrange("p (k n) -> p k n", n=D)
                end = c == m.NCH - 1
                for n in range(2):
                    o = bank[4 + n][:, :]
                    for k in range(2):
                        ns = slice(512 * n, 512 * n + 512)
                        mm(o, mh_hi[:, k, :], wh[:, k, ns], start=(first and k == 0), stop=False,
                           skip_group_check=True)
                        mm(o, mh_lo[:, k, :], wh[:, k, ns], start=False, stop=False, skip_group_check=True)
                        last = mm(o, mh_hi[:, k, :], wl[:, k, ns], start=False, stop=(end and k == 1),
                                  skip_group_check=True)
                last.then_inc(T.sem("unit_done"), 1)

            def gather(par, g):
                eng.wait_ge(S_("selected"), g + 1)
                for a in range(TT):
                    nc.tensor.transpose(bank[3][:, a * P:(a + 1) * P], pself[par][:, a, :], ident[:, :])
                for a in range(TT):
                    last = mm(bank[3][:, 2 * P:2 * P + m.G], pself[par][:, a, :], gateg[:, par, a, 0:m.G],
                              start=(a == 0), stop=(a == 1))
                last.then_inc(S_("sel_turned"), 1)
                if not isinstance(g, int) or g > 0:
                    eng.wait_ge(S_("scattered"), g * 4)
                for r in range(4):
                    src = tok_hi if r < 2 else tok_lo
                    if r == 2:
                        eng.wait_ge(S_("gathered_hi"), g * 2 + 2)
                    o = bank[6 + r % 2]
                    for k in range(4):
                        kk = 4 * (r % 2) + k
                        for a in range(TT):
                            last = mm(o[:, k * P:(k + 1) * P], src[:, a, kk * P:(kk + 1) * P], psel_r[:, a, :],
                                      start=(a == 0), stop=(a == 1))
                    last.then_inc(S_("gathering"), 1)

            def scatter(par, g):
                eng.wait_ge(S_("y"), g * 2 + 2)
                end = isinstance(g, int) and g == m.NG
                eng.wait_ge(S_("selT"), m.NG if end else g + 1)
                for r in range(4):
                    if r < 2 and end:
                        eng.wait_ge(S_("scattered"), g * 4 - 1 + r)
                    elif r < 2:
                        eng.wait_ge(S_("gathered_lo"), g * 2 + 2)
                    else:
                        eng.wait_ge(S_("scattered"), g * 4 + (r - 1))
                    o = bank[6 + r % 2]
                    for k in range(2):
                        kk = 2 * r + k
                        last = mm(o[:, k * S:(k + 1) * S], ysb[:, kk * P:(kk + 1) * P], pselT[par],
                                  start=True, stop=True)
                    last.then_inc(S_("scatter"), 1)

            pe.eng.wait_ge(*T.at(f"{nm} tok_hi"))
            pe.eng.wait_ge(*T.at(f"{nm} tok_lo"))
            pe.eng.wait_ge(*T.at(f"{nm} cleared"))
            gather(0, 0)
            eng.wait_ge(S_("gathered_hi"), 2)
            eng.wait_ge(S_("gathered_lo"), 2)
            up(0, 0, 0, 0, q=0)
            up(0, 0, 1, 0)

            def group(g, par, end=False):
                def step(c, jt):
                    q, more = g * m.NCH + c, None
                    if jt is not None:
                        q, more = q + jt * 2, jt * 6
                    ahead = c == m.NCH
                    p = 1 - par if ahead else par
                    if ahead:
                        eng.wait_ge(S_("gathered_hi"), g * 2 + 4)
                        eng.wait_ge(S_("gathered_lo"), g * 2 + 4)
                    up(g, c, 0, p, more, q=q)
                    turn(c - 1, q - 1)
                    up(g, c, 1, p, more)
                    if c == 1:
                        scatter(1 - par, g)
                    down(g, c - 1, m.unit(c - 1, 2), more, q - 1, c == 1)
                    if c == m.NCH - 2 and jt is None and not end:
                        gather(1 - par, g + 1)
                m.steps(eng, g, end, step)
                if end:
                    turn(m.NCH - 1, g * m.NCH + m.NCH - 1)
                    down(g, m.NCH - 1, m.last_down(True), None, g * m.NCH + m.NCH - 1, False)

            with eng.Fori(0, m.NG // 2 - 1) as it:
                for par in range(2):
                    group(it * 2 + par, par)
            group(m.NG - 2, 0)
            group(m.NG - 1, 1, end=True)
            scatter(1, m.NG)
            T.mark(f"{nm} scatter", f"{nm}_scatter", 4 * (m.NG + 1))
            T.mark("ev moe", f"{nm}_scattered", 4 * (m.NG + 1))

        def moe_act(act, m):
            run, eng, nm = nc.scalar.activation, act.eng, m.name
            act.eng.wait_ge(*T.at(f"{nm} shifted"))
            for a in range(TT):
                run(RT[:, 1, a, 0:m.E], RT[:, 2, a, 0:m.E], ACT.Exp, bias=rmax[:, a, 1:2],
                             accum_out=rmax[:, a, 2:3]).then_inc(act.tick(f"{nm} exps"), 1)
            if m.groups > 1:
                for a in range(TT):
                    run(RT[:, 3, a, 0:m.groups], RT[:, 4, a, 0:m.groups], ACT.Exp,
                                 bias=rmax[:, a, 4:5], accum_out=rmax[:, a, 5:6]).then_inc(act.tick(f"{nm} exps"), 1)
            for j in range(4):
                act.eng.wait_ge(*T.at(f"mm {nm} tok {j}"))
                run(tok_hi[:, :, 256 * j:256 * j + 256],
                             bank_view(ps(f"{nm} tok {j}")), ACT.Copy).then_inc(act.tick(f"{nm} tok_hi {j}"), 1)
            T.mark(f"{nm} tok_hi", *act.last)
            S_ = lambda what: T.sem(f"{nm}_{what}")
            U, SB = m.first, split_before[m.first]

            def hi(g, i0, more=None):
                r, s = (U + i0) % RAW, (SB + i0) % SPLIT
                v = g * (32 * m.per // RAW) + 32 * ((U + i0) // RAW + 1)
                if more is not None:
                    v = v + more * 32
                eng.wait_ge(raw_landed[r], v)
                v = g * m.per + (U + i0 - SPLIT + 1)
                if more is not None:
                    v = v + more * 6
                eng.wait_ge(T.sem("unit_done"), v)
                run(ring_hi[:, s, :], ring_raw[:, r, :], ACT.Copy).then_inc(T.sem("hi_done"), 1)

            def silu(c, q):
                eng.wait_ge(T.sem("unit_done"), q)
                run(tC[:, c % 2, :], bank[c % 2][:, 0:256], ACT.Silu).then_inc(S_("silu"), 1)

            def turned(q):
                eng.wait_ge(S_("turned"), q + 1)
                run(mh_hi, bank[2][:, 0:256].rearrange("p (k s) -> p k s", k=2), ACT.Copy)\
                    .then_inc(S_("turned_hi"), 1)

            def gathered(par, g):
                eng.wait_ge(S_("sel_turned"), g + 1)
                run(pselT[par], bank[3][:, 0:2 * P], ACT.Copy).then_inc(S_("selT"), 1)
                for r in range(2):
                    eng.wait_ge(S_("gathering"), g * 4 + (r + 1))
                    run(xg_hi[par][:, 4 * r:4 * r + 4, :], bank[6 + r][:, :].rearrange("p (k s) -> p k s", k=4),
                        ACT.Copy).then_inc(S_("gathered_hi"), 1)

            hi(0, 0)
            act.eng.wait_ge(*T.at(f"{nm} cleared"))
            gathered(0, 0)
            hi(0, 1)
            hi(0, m.unit(1, 0))
            silu(0, U + 2)
            hi(0, m.unit(1, 1))

            def group(g, par, end=False):
                ud = lambda i0: g * m.per + (U + i0 + 1)

                def step(c, jt):
                    q, more = g * m.NCH + c, None
                    if jt is not None:
                        q, more = q + jt * 2, jt
                    if c == 1:
                        outputs(g)
                    hi(g, m.unit(c - 1, 2), more)
                    turned(q - 1)
                    if end and c == m.NCH - 1:
                        hi(g, m.last_down(True))
                        silu(c, ud(m.unit(c, 1)))
                        turned(q)
                        return
                    hi(g, m.unit(c + 1, 0), more)
                    done = ud(m.unit(c, 1))
                    silu(c, done if jt is None else done + jt * 6)
                    hi(g, m.unit(c + 1, 1), more)
                    if c == m.NCH - 2 and jt is None and not end:
                        gathered(1 - par, g + 1)
                m.steps(eng, g, end, step)

            def outputs(g):
                if isinstance(g, int) and g == m.NG:
                    eng.wait_ge(T.sem("unit_done"), U + m.units)
                else:
                    eng.wait_ge(T.sem("unit_done"), g * m.per + (U + 2))
                for n in range(2):
                    run(ysb[:, 512 * n:512 * n + 512], bank[4 + n][:, :], ACT.Copy).then_inc(S_("y"), 1)

            with eng.Fori(0, m.NG // 2 - 1) as it:
                for par in range(2):
                    group(it * 2 + par, par)
            group(m.NG - 2, 0)
            group(m.NG - 1, 1, end=True)
            outputs(m.NG)
            nxt["act"] = m.first + m.units
            split_hi(act, nxt["act"] + 1)

        def bank_view(b):
            return b[:, :].rearrange("p (a c) -> p a c", a=TT)

        def moe_dve(dve, m):
            tt, ts, stt = nc.vector.tensor_tensor, nc.vector.tensor_scalar, nc.vector.scalar_tensor_tensor
            eng, nm, E = dve.eng, m.name, m.E
            R = m.groups
            n_log = E + (R if R > 1 else 0)
            L, sel, sh = RT[:, 5, :, :], RT[:, 0, :, :], RT[:, 2, :, :]
            dve.eng.wait_ge(*T.at(f"mm {nm} logits"))
            lg = ps(f"{nm} logits")
            for a in range(TT):
                tt(L[:, a, 0:E], lg[:, a * n_log:a * n_log + E], rbias[:, 0:E], ALU.add).then_inc(dve.tick(), 1)
                if R > 1:
                    tt(RT[:, 4, a, 0:R], lg[:, a * n_log + E:(a + 1) * n_log], rbias[:, E:E + R], ALU.add).then_inc(dve.tick(), 1)
            T.mark(f"ev {nm} logits", *dve.last)
            dve.eng.wait_ge(*dve.own())
            dve.eng.wait_ge(*T.at("routing constants"))

            def rank(src, n, k, dst):
                shape = [P, k, n, n]
                v = src.rearrange("p (g e) -> p g e", g=k)
                other, own = v.unsqueeze(2).to_broadcast(shape), v.unsqueeze(3).to_broadcast(shape)
                w1 = tC[:, 4, 0:k * n * n].rearrange("p (g e j) -> p g e j", g=k, e=n)
                w2 = tC[:, 5, 0:k * n * n].rearrange("p (g e j) -> p g e j", g=k, e=n)
                tt(w1, other, own, ALU.is_equal).then_inc(dve.tick(), 1)
                tt(w2, other, own, ALU.is_gt).then_inc(dve.tick(), 1)
                dve.eng.wait_ge(*dve.own())
                tt(w1, w1, lower[:, 0:n, 0:n].unsqueeze(1).to_broadcast(shape), ALU.mult).then_inc(dve.tick(), 1)
                dve.eng.wait_ge(*dve.own())
                tt(w1, w1, w2, ALU.add).then_inc(dve.tick(), 1)
                dve.eng.wait_ge(*dve.own())
                nc.vector.tensor_reduce(dst, w1.rearrange("p g e j -> p (g e) j"), AX, ALU.add).then_inc(dve.tick(), 1)
                dve.eng.wait_ge(*dve.own())

            for a in range(TT):
                rank(L[:, a, 0:E], 8, R, sel[:, a, 0:E])
                ts(sel[:, a, 0:E], sel[:, a, 0:E], 1.5, None, ALU.is_lt).then_inc(dve.tick(), 1)
                dve.eng.wait_ge(*dve.own())
                if R > 1:
                    rank(RT[:, 4, a, 0:R], R, 1, RT[:, 6, a, 0:R])
                    ts(RT[:, 6, a, 0:R], RT[:, 6, a, 0:R], 0.5, None, ALU.is_lt).then_inc(dve.tick(), 1)
                    dve.eng.wait_ge(*dve.own())
                    s3 = sel[:, a, 0:E].rearrange("p (g e) -> p g e", g=R)
                    tt(s3, s3, RT[:, 6, a, 0:R].unsqueeze(2).to_broadcast([P, R, 8]), ALU.mult).then_inc(dve.tick(), 1)
                    dve.eng.wait_ge(*dve.own())
                T.mark(f"{nm} sel", *dve.last)
            for a in range(TT):
                ts(sh[:, a, 0:E], sel[:, a, 0:E], -NEG, NEG, ALU.mult, ALU.add).then_inc(dve.tick(), 1)
                dve.eng.wait_ge(*dve.own())
                tt(sh[:, a, 0:E], sh[:, a, 0:E], L[:, a, 0:E], ALU.add).then_inc(dve.tick(), 1)
                dve.eng.wait_ge(*dve.own())
                nc.vector.tensor_reduce(rmax[:, a, 1:2], sh[:, a, 0:E], AX, ALU.max, negate=True).then_inc(dve.tick(), 1)
                if R > 1:
                    nc.vector.tensor_reduce(rmax[:, a, 4:5], RT[:, 4, a, 0:R], AX, ALU.max, negate=True).then_inc(dve.tick(), 1)
            T.mark(f"{nm} shifted", *dve.last)
            for j in range(4):
                dve.eng.wait_ge(*T.at(f"{nm} tok_hi {j}"))
                cs = slice(256 * j, 256 * j + 256)
                tt(tok_lo[:, :, cs], bank_view(ps(f"{nm} tok {j}")), tok_hi[:, :, cs].bitcast(F32),
                            ALU.subtract).then_inc(dve.tick(f"ev {nm} tok {j}"), 1)
            T.mark(f"{nm} tok_lo", *dve.last)
            dve.eng.wait_ge(*T.at(f"mm {nm} count"))
            cb = ps(f"{nm} count")
            cum, tot, off = RT[:, 7, :, :], RT[:, 8, 0, :], RT[:, 8, 1, :]
            nc.vector.tensor_copy(cum[:, :, 0:E], cb[:, 0:2 * E].rearrange("p (a e) -> p a e", a=TT)).then_inc(dve.tick(), 1)
            nc.vector.tensor_copy(tot[:, 0:E], cb[:, 2 * E:3 * E]).then_inc(dve.tick(f"ev {nm} count"), 1)
            nc.vector.memset(off[:, 0:E], 0.0).then_inc(dve.tick(), 1)
            nc.vector.memset(pos[:, :, :, :], -1.0).then_inc(dve.tick(), 1)
            nc.vector.memset(gates[:, :, :, :], 0.0).then_inc(dve.tick(), 1)
            nc.vector.memset(mask[:, :, :], 0.0).then_inc(dve.tick(), 1)
            dve.eng.wait_ge(*dve.own())
            o3 = off[:, 0:E].rearrange("p (g i) -> p g i", i=m.G)
            t3 = tot[:, 0:E].rearrange("p (g i) -> p g i", i=m.G)
            for i in range(1, m.G):
                tt(o3[:, :, i], o3[:, :, i - 1], t3[:, :, i - 1], ALU.add).then_inc(dve.tick(), 1)
                dve.eng.wait_ge(*dve.own())
            lo_, hi_ = RT[:, 9, 0, 0:E], RT[:, 9, 1, 0:E]
            tt(hi_, off[:, 0:E], tot[:, 0:E], ALU.add).then_inc(dve.tick(), 1)
            dve.eng.wait_ge(*dve.own())
            nc.vector.tensor_reduce(most[:, 0:1], hi_, AX, ALU.max).then_inc(dve.tick(), 1)
            dve.eng.wait_ge(*dve.own())
            nc.vector.tensor_copy(overflow[:, :], most[:, 0:1]).then_inc(dve.tick(f"{nm} overflow"), 1)
            tt(lo_, off[:, 0:E], part[:, 0:1].to_broadcast([P, E]), ALU.is_le).then_inc(dve.tick(), 1)
            dve.eng.wait_ge(*dve.own())
            tt(hi_, hi_, part[:, 0:1].to_broadcast([P, E]), ALU.is_gt).then_inc(dve.tick(), 1)
            dve.eng.wait_ge(*dve.own())
            tt(mask[:, 0:m.NG, 0:m.G], lo_.rearrange("p (g i) -> p g i", i=m.G),
                        hi_.rearrange("p (g i) -> p g i", i=m.G), ALU.mult).then_inc(dve.tick(), 1)
            for a in range(TT):
                c = cum[:, a, 0:E]
                stt(c, c, 1.0, off[:, 0:E], ALU.add, ALU.add).then_inc(dve.tick(), 1)
                dve.eng.wait_ge(*dve.own())
                tt(c, c, sel[:, a, 0:E], ALU.mult).then_inc(dve.tick(), 1)
                dve.eng.wait_ge(*dve.own())
                ts(pos[:, 0:m.NG, a, 0:m.G], c.rearrange("p (g i) -> p g i", i=m.G), -1.0, None, ALU.add).then_inc(dve.tick(), 1)
            dve.eng.wait_ge(*T.at(f"{nm} exps"))
            for a in range(TT):
                nc.vector.reciprocal(rmax[:, a, 3:4], rmax[:, a, 2:3]).then_inc(dve.tick(), 1)
                if R > 1:
                    nc.vector.reciprocal(rmax[:, a, 6:7], rmax[:, a, 5:6]).then_inc(dve.tick(), 1)
                    dve.eng.wait_ge(*dve.own())
                    tt(rmax[:, a, 3:4], rmax[:, a, 3:4], rmax[:, a, 6:7], ALU.mult).then_inc(dve.tick(), 1)
                dve.eng.wait_ge(*dve.own())
                ts(gates[:, 0:m.NG, a, 0:m.G], RT[:, 1, a, 0:E].rearrange("p (g i) -> p g i", i=m.G),
                            rmax[:, a, 3:4], None, ALU.mult).then_inc(dve.tick(), 1)
            S_ = lambda what: T.sem(f"{nm}_{what}")
            U, SB = m.first, split_before[m.first]
            nc.vector.memset(tB[:, :, :], 0.0).then_inc(dve.tick(), 1)
            nc.vector.memset(pselT[1], 0.0).then_inc(dve.tick(), 1)
            for n in range(2):
                nc.vector.memset(bank[4 + n][:, :], 0.0).then_inc(dve.tick(f"{nm} cleared"), 1)
            nc.vector.memset(tC[:, 2, :], 0.0).then_inc(S_("hidden"), 1)
            nc.vector.memset(tC[:, 3, :], 0.0).then_inc(S_("hidden"), 1)

            def lo(g, i0, more=None):
                r, s = (U + i0) % RAW, (SB + i0) % SPLIT
                v = g * m.per + (SB + i0 + 1)
                if more is not None:
                    v = v + more * 6
                eng.wait_ge(T.sem("hi_done"), v)
                tt(ring_lo[:, s, :], ring_raw[:, r, :], ring_hi[:, s, :].bitcast(F32),
                   ALU.subtract).then_inc(T.sem("lo_done"), 1)

            def hidden(c, par, q):
                eng.wait_ge(S_("silu"), q + 1)
                i = 0 if m.G == 1 else c % m.NCH
                stt(tC[:, 2 + c % 2, :], tC[:, c % 2, :], ge[:, par, i:i + 1],
                    bank[c % 2][:, 256:512], ALU.mult, ALU.mult).then_inc(S_("hidden"), 1)

            def turned(q):
                eng.wait_ge(S_("turned_hi"), q + 1)
                tt(mh_lo, bank[2][:, 0:256].rearrange("p (k s) -> p k s", k=2), mh_hi.bitcast(F32),
                   ALU.subtract).then_inc(S_("turned_lo"), 1)

            def select(par, g):
                steps = 3 + TT * m.G + 1
                n = [0]

                def step(ins):
                    n[0] += 1
                    ins.then_inc(S_("step"), 1)
                    eng.wait_ge(S_("step"), g * steps + n[0])

                step(nc.vector.tensor_copy(posg[:, :, 0:m.G], pos[:, bass.ds(g, 1), :, 0:m.G]
                                           .rearrange("p o a i -> p (o a) i")))
                step(nc.vector.tensor_copy(gateg[:, par, :, 0:m.G], gates[:, bass.ds(g, 1), :, 0:m.G]
                                           .rearrange("p o a i -> p (o a) i")))
                step(nc.vector.tensor_copy(maskg[:, par, 0:m.G], mask[:, bass.ds(g, 1), 0:m.G]
                                           .rearrange("p o i -> p (o i)")))
                for i in range(m.G):
                    for a in range(TT):
                        o = pself[par][:, a, :]
                        if i == 0:
                            step(ts(o, slots[:, :], posg[:, a, 0:1], None, ALU.is_equal))
                        else:
                            step(stt(o, slots[:, :], posg[:, a, i:i + 1], o, ALU.is_equal, ALU.add))
                step(nc.vector.tensor_copy(psel_r[:, :, :], pself[par]))
                nc.vector.tensor_copy(small[:, 0, 0:1], part[:, 0:1]).then_inc(S_("selected"), 1)

            def gathered(par, g):
                eng.wait_ge(S_("selT"), g + 1)
                tt(ge[:, par, 0:m.G], bank[3][:, 2 * P:2 * P + m.G], maskg[:, par, 0:m.G], ALU.mult)\
                    .then_inc(S_("gate"), 1)
                for r in range(2):
                    eng.wait_ge(S_("gathering"), g * 4 + (r + 3))
                    nc.vector.tensor_copy(xg_lo[par][:, 4 * r:4 * r + 4, :],
                                          bank[6 + r][:, :].rearrange("p (k s) -> p k s", k=4))\
                        .then_inc(S_("gathered_lo"), 1)
                eng.wait_ge(S_("gate"), g + 1)

            def scattered(g):
                for r in range(4):
                    eng.wait_ge(S_("scatter"), g * 4 + (r + 1))
                    o = tB[:, 2 * r:2 * r + 2, :]
                    tt(o, o, bank[6 + r % 2][:, :].rearrange("p (k t) -> p k t", k=2), ALU.add)\
                        .then_inc(S_("scattered"), 1)

            dve.eng.wait_ge(*dve.own())
            select(0, 0)
            lo(0, 0)
            gathered(0, 0)
            lo(0, 1)
            lo(0, m.unit(1, 0))
            hidden(0, 0, 0)
            lo(0, m.unit(1, 1))

            def group(g, par, end=False):
                def step(c, jt):
                    q, more = g * m.NCH + c, None
                    if jt is not None:
                        q, more = q + jt * 2, jt
                    lo(g, m.unit(c - 1, 2), more)
                    turned(q - 1)
                    if end and c == m.NCH - 1:
                        lo(g, m.last_down(True))
                        hidden(c, par, q)
                        turned(q)
                        return
                    lo(g, m.unit(c + 1, 0), more)
                    hidden(c, 1 - par if c == m.NCH else par, q)
                    if c == 1:
                        scattered(g)
                    lo(g, m.unit(c + 1, 1), more)
                    if c == 1 and not end:
                        select(1 - par, g + 1)
                    if c == m.NCH - 2 and jt is None and not end:
                        gathered(1 - par, g + 1)
                m.steps(eng, g, end, step)

            with eng.Fori(0, m.NG // 2 - 1) as it:
                for par in range(2):
                    group(it * 2 + par, par)
            group(m.NG - 2, 0)
            group(m.NG - 1, 1, end=True)
            scattered(m.NG)
            T.mark(f"{nm} done", f"{nm}_scattered", 4 * (m.NG + 1))
            nxt["dve"] = m.first + m.units
            split_lo(dve, nxt["dve"] + 1)

        rest_w = scr[:, :, :]
        rest_down = scr[:, :, :].rearrange("p (k j) t -> p k (j t)", k=2)
        rest_gates = tC[:, 6, :].rearrange("p (a e) -> p a e", a=TT)
        rest_col = tC[:, 7, :].rearrange("p (a m) -> p a m", a=TT)
        rest_h = tC[:, 0:2, :]

        def rest_chunks(eng, m):
            per = m.NCH // m.G
            return per, m.E * per

        def when_full(engine, m):
            engine.eng.wait_ge(*T.at(f"{m.name} overflow"))
            return engine.eng.If(engine.eng.value_load(overflow[0:1, 0:1], min_val=0, max_val=4 * S) > SLOTS)

        def rest_sp(sp, m, w_gate, w_up, w_down):
            eng, R = sp.eng, lambda what: T.sem(f"{m.name}_rest_{what}")
            per, total = rest_chunks(eng, m)
            with when_full(sp, m):
                with eng.Fori(0, m.E) as e:
                    with eng.Fori(0, per) as c:
                        n = e * per + c
                        eng.wait_ge(R("dve"), n * 7 + 1)
                        for h in range(2):
                            eng.dma_start(rest_w[:, 4 * h:4 * h + 4, :], w_gate(e, slice(512 * h, 512 * h + 512), c))\
                               .then_inc(R("load"), 16)
                        eng.wait_ge(R("pe"), n * 4 + 2)
                        for h in range(2):
                            eng.dma_start(rest_w[:, 4 * h:4 * h + 4, :], w_up(e, slice(512 * h, 512 * h + 512), c))\
                               .then_inc(R("load"), 16)
                        eng.wait_ge(R("pe"), n * 4 + 3)
                        for k in range(2):
                            eng.dma_start(rest_down[:, k:k + 1, :], w_down(e, c, k)).then_inc(R("load"), 16)

        def rest_pe(pe, m, H):
            mm, eng, R = nc.tensor.matmul, pe.eng, lambda what: T.sem(f"{m.name}_rest_{what}")
            per, total = rest_chunks(eng, m)
            with when_full(pe, m):
                with eng.Fori(0, total) as n:
                    eng.wait_ge(R("dve"), n * 7 + 1)
                    for a in range(TT):
                        last = mm(bank[2][:, a * P:(a + 1) * P], rest_col[:, a, :], ident[:, :], start=True, stop=True)
                    last.then_inc(R("pe"), 1)
                    for what in range(2):
                        eng.wait_ge(R("load"), n * 96 + 32 * (what + 1))
                        for b in range(2):
                            for k in range(KT):
                                last = mm(bank[what][:, b * S:(b + 1) * S], rest_w[:, k, b * P:(b + 1) * P],
                                          H[:, k, :], start=(k == 0), stop=(k == KT - 1))
                        last.then_inc(R("pe"), 1)
                    eng.wait_ge(R("load"), n * 96 + 96)
                    eng.wait_ge(R("dve"), n * 7 + 3)
                    for cb in range(KT):
                        for k in range(2):
                            last = mm(bank[4 + cb // 2][:, (cb % 2) * S:(cb % 2 + 1) * S],
                                      rest_down[:, k, cb * P:(cb + 1) * P], rest_h[:, k, :],
                                      start=(k == 0), stop=(k == 1))
                    last.then_inc(R("pe"), 1)
                eng.wait_ge(R("dve"), total * 7)

        def rest_act(act, m):
            eng, R = act.eng, lambda what: T.sem(f"{m.name}_rest_{what}")
            per, total = rest_chunks(eng, m)
            with when_full(act, m):
                with eng.Fori(0, total) as n:
                    eng.wait_ge(R("pe"), n * 4 + 2)
                    nc.scalar.activation(rest_h, bank[0][:, :].rearrange("p (k t) -> p k t", k=2), ACT.Silu)\
                        .then_inc(R("act"), 1)
                eng.wait_ge(R("dve"), total * 7)

        def rest_dve(dve, m):
            tt, eng, R = nc.vector.tensor_tensor, dve.eng, lambda what: T.sem(f"{m.name}_rest_{what}")
            per, total = rest_chunks(eng, m)
            dve.eng.wait_ge(*T.at(f"{m.name} done"))
            with when_full(dve, m):
                for a in range(TT):
                    nc.vector.scalar_tensor_tensor(
                        rest_gates[:, a, 0:m.E].rearrange("p (g i) -> p g i", i=m.G), pos[:, 0:m.NG, a, 0:m.G],
                        SLOTS - 0.5, gates[:, 0:m.NG, a, 0:m.G], ALU.is_ge, ALU.mult).then_inc(R("gates"), 1)
                eng.wait_ge(R("gates"), TT)
                with eng.Fori(0, m.E) as e:
                    with eng.Fori(0, per) as c:
                        n = e * per + c
                        nc.vector.tensor_copy(rest_col, rest_gates[:, :, bass.ds(e, 1)].to_broadcast([P, TT, P]))\
                            .then_inc(R("dve"), 1)
                        eng.wait_ge(R("act"), n + 1)
                        eng.wait_ge(R("pe"), n * 4 + 3)
                        tt(rest_h, rest_h, bank[1][:, :].rearrange("p (k t) -> p k t", k=2), ALU.mult)\
                            .then_inc(R("dve"), 1)
                        eng.wait_ge(R("dve"), n * 7 + 2)
                        tt(rest_h, rest_h, bank[2][:, 0:S].unsqueeze(1).to_broadcast([P, 2, S]), ALU.mult)\
                            .then_inc(R("dve"), 1)
                        eng.wait_ge(R("pe"), n * 4 + 4)
                        for j in range(4):
                            o = tB[:, 2 * j:2 * j + 2, :]
                            tt(o, o, bank[4 + j][:, :].rearrange("p (k t) -> p k t", k=2), ALU.add)\
                                .then_inc(R("dve"), 1)
                        eng.wait_ge(R("dve"), n * 7 + 7)

        def conv_ready(engine, blocks):
            for k in blocks:
                engine.eng.wait_ge(*T.at(f"ev conv a {k // 2}"))
            engine.eng.wait_ge(*T.at("ev cols 1"))
            engine.eng.wait_ge(*T.at("mm cols 1"))
            engine.eng.wait_ge(*T.at("u padded"))

        def conv_dve(dve, blocks):
            taps = []
            conv_ready(dve, blocks)
            for i in range(TAPS):
                for k in blocks:
                    if i == 0:
                        ins = nc.vector.tensor_scalar(tA[:, k, :], uT[:, k, 0:S], col("conv_dw_w", k, 0),
                                                      col("conv_dw_b", k), ALU.mult, ALU.add)
                    else:
                        dve.eng.wait_ge(*taps[-len(blocks)])
                        ins = nc.vector.scalar_tensor_tensor(tA[:, k, :], uT[:, k, i:i + S],
                                                             col("conv_dw_w", k, i), tA[:, k, :],
                                                             ALU.mult, ALU.add)
                    ins.then_inc(dve.tick(f"z conv {k}"), 1)
                    taps.append(dve.own())

        pool_blocks = range(KT - POOL_BLOCKS, KT)
        product = lambda i, k: tD[:, 2 * (k - pool_blocks[0]) + i % 2, :]

        def conv_pool(pool):
            conv_ready(pool, pool_blocks)
            for k in pool_blocks:
                nc.gpsimd.tensor_scalar(tA[:, k, :], uT[:, k, 0:S], col("conv_dw_w", k, 0), col("conv_dw_b", k),
                                        ALU.mult, ALU.add).then_inc(pool.tick(f"sum 0 {k}"), 1)
            for i in range(1, TAPS):
                for k in pool_blocks:
                    pool.eng.wait_ge(*T.at(f"sum {i - 1} {k}"))
                    pool.eng.wait_ge(*T.at(f"tap {i} {k}"))
                    nc.gpsimd.tensor_tensor(tA[:, k, :], tA[:, k, :], product(i, k), ALU.add)\
                        .then_inc(pool.tick(f"sum {i} {k}"), 1)
                    T.mark(f"z conv {k}", *pool.last)

        def conv_act(act, row_out):
            conv_ready(act, pool_blocks)
            act.eng.wait_ge(*T.at("Hl conv"))
            rows = [(0, p) for p in range(4, 12)] + [(2, p) for p in range(4)]
            for i in range(1, TAPS):
                for k in pool_blocks:
                    if i > 2:
                        act.eng.wait_ge(*T.at(f"sum {i - 2} {k}"))
                    nc.scalar.activation(product(i, k), uT[:, k, i:i + S], ACT.Identity,
                                         scale=col("conv_dw_w", k, i)).then_inc(act.tick(f"tap {i} {k}"), 1)
                if i % 5 in (2, 4) and rows:
                    row_out(*rows.pop(0))
            for pair in rows:
                row_out(*pair)

        def softmax_exp(act, name, heads, dst):
            run = nc.scalar.activation
            for i in range(heads + 3):
                if i < heads:
                    h = i
                    act.eng.wait_ge(*T.at(f"{name} max {h}"))
                    sm = small[:, h % 3, :]
                    run(pr[:, h % 3, 0:P], pr[:, h % 3, 0:P], ACT.Exp, bias=sm[:, 0:1],
                                 accum_out=sm[:, 2:3]).then_inc(act.tick(), 1)
                    run(pr[:, h % 3, P:3 * P], pr[:, h % 3, P:3 * P], ACT.Exp, bias=sm[:, 1:2],
                                 accum_out=sm[:, 3:4]).then_inc(act.tick(f"{name} exp {h}"), 1)
                if 2 <= i < heads + 2:
                    h = i - 2
                    act.eng.wait_ge(*T.at(f"mm {name} pT {h}"))
                    if h >= 3:
                        act.eng.wait_ge(*T.at(f"mm {name} o {h - 3}"))
                    run(prT[:, h % 3, :], ps(f"{name} pT {h}")[:, 0:3 * P], ACT.Copy).then_inc(act.tick(f"ev {name} pT {h}"), 1)
                    T.mark(f"{name} pT {h}", *act.last)
                if i >= 3 and (i - 3) % 2 == 1:
                    k = (i - 3) // 2
                    act.eng.wait_ge(*T.at(f"mm {name} o {2 * k + 1}"))
                    run(dst[:, k, :], ps(f"{name} o {k}")[:, 0:S], ACT.Copy).then_inc(act.tick(f"hi {name} o {k}"), 1)

        def softmax_rest(dve, name, heads, bias, lo, hi):
            tt, ts, stt = nc.vector.tensor_tensor, nc.vector.tensor_scalar, nc.vector.scalar_tensor_tensor
            dve.eng.wait_ge(*T.at("alibi"))
            for i in range(heads + 5):
                if i < heads:
                    h = i
                    dve.eng.wait_ge(*T.at(f"mm {name} s {h}"))
                    if h >= 3:
                        dve.eng.wait_ge(*T.at(f"mm {name} pT {h - 3}"))
                    b, sm = ps(f"{name} s {h}"), small[:, h % 3, :]
                    for c0, w in ((0, P), (P, 2 * P)) if bias(h, 0, P)[1] is None else ((0, 3 * P),):
                        tab, slope = bias(h, c0, w)
                        o, s = pr[:, h % 3, c0:c0 + w], b[:, c0:c0 + w]
                        if slope is None:
                            tt(o, s, tab, ALU.add).then_inc(dve.tick(f"ev {name} s {h}"), 1)
                        else:
                            stt(o, tab, slope, s, ALU.mult, ALU.add).then_inc(dve.tick(f"ev {name} s {h}"), 1)
                    dve.eng.wait_ge(*dve.own())
                    for m, (c0, w) in enumerate(((0, P), (P, 2 * P))):
                        nc.vector.tensor_reduce(sm[:, m:m + 1], pr[:, h % 3, c0:c0 + w], AX, ALU.max,
                                                         negate=True).then_inc(dve.tick(f"{name} max {h}"), 1)
                if 1 <= i < heads + 1:
                    h = i - 1
                    sm = small[:, h % 3, :]
                    dve.eng.wait_ge(*T.at(f"{name} exp {h}"))
                    nc.vector.reciprocal(sm[:, 4:6], sm[:, 2:4]).then_inc(dve.tick(), 1)
                    dve.eng.wait_ge(*dve.own())
                    for m, (c0, w) in enumerate(((0, P), (P, 2 * P))):
                        o = pr[:, h % 3, c0:c0 + w]
                        ts(o, o, sm[:, 4 + m:5 + m], None, ALU.mult).then_inc(dve.tick(f"{name} p {h}"), 1)
                if i >= 5 and (i - 5) % 2 == 1:
                    k = (i - 5) // 2
                    dve.eng.wait_ge(*T.at(f"hi {name} o {k}"))
                    tt(lo[:, k, :], ps(f"{name} o {k}")[:, 0:S], hi[:, k, :].bitcast(F32),
                                ALU.subtract).then_inc(dve.tick(f"ev {name} o {k}"), 1)


        block = ctx.enter_context(nc.Block())

        @block.sync
        def _(eng):
            sp = Engine(T, eng, "sp")

            def small_load(label, dst, src):
                eng.dma_start(dst, src).then_inc(T.sem(label), 16)
                T.count[label] = T.count.get(label, 0) + 16
                T.mark(label, label, T.count[label])

            rows = tA[:, 0:4, :].rearrange("p k t -> p (k t)")
            sp.eng.wait_ge(*T.at("rows cleared"))
            flat = lambda ap: ap
            sources = [
                ("conv_dw_w", A["conv_dw_w"][0], TAPS, D), ("conv_dw_b", A["conv_dw_b"], 1, D),
                ("conv_norm_g", A["conv_norm_g"], 1, D), ("conv_norm_b", A["conv_norm_b"], 1, D),
                ("conv_out_b", A["conv_out_b"], 1, D),
                ("conv_in_b", A["conv_in_b"].rearrange("a (r d) -> (a r) d", d=D), 2, D),
                ("ada_b", A["ada_b"].rearrange("a (r d) -> (a r) d", d=D), 12, D),
                ("kv_ada_b", A["kv_ada_b"].rearrange("(r d) -> r d", d=D), 2, D),
                ("ln_g", A["ln_g"].rearrange("a b d -> (a b) d"), 4, D),
                ("ln_b", A["ln_b"].rearrange("a b d -> (a b) d"), 4, D),
                ("ln_in_g_2", A["ln_in_g_2"].rearrange("(r d) -> r d", r=1), 1, D),
                ("ln_in_b_2", A["ln_in_b_2"].rearrange("(r d) -> r d", r=1), 1, D),
                ("ln_g_2", A["ln_g_2"][0], 3, D), ("ln_b_2", A["ln_b_2"][0], 3, D),
                ("c", A["c"], 1, D),
                ("tok_mix_2", A["tok_mix_2"][:, 0:D], 1, D),
            ]
            for name, src, n, width in sources:
                r = ROW[name]
                small_load("rows landed", rows[r:r + n, 0:width], src)
            r = ROW["tok_mix_2"] + 1
            rest = A["tok_mix_2"].shape[1] - D
            small_load("rows landed", rows[r:r + 1, 0:rest], A["tok_mix_2"][:, D:D + rest])
            small_load("rows landed", rows[r + 1:r + 2, 0:P], A["tok_mix_2"][:, D + rest - P:D + rest])
            for name in ("decay_base_2", "aaa_base_2", "k_k_2", "k_a_2", "gn_g_2", "gn_b_2"):
                r = ROW[name]
                small_load("rows landed", rows[r:r + 1, 0:512], A[name])
            r = ROW["r_k_2"]
            small_load("rows landed", rows[r:r + 1, 0:512], A["r_k_2"].rearrange("a h d -> a (h d)"))
            x_in = tB[:, :, :].rearrange("p (a k) t -> p a (k t)", a=TT)
            small_load("x landed", x_in, A["x"][0].rearrange("(a p) d -> p a d", p=P))

            small_load("m1 router landed", rw[:, :, 0:8], A["router_w"][0].rearrange("(k p) n -> p k n", p=P))
            small_load("m1 router landed", rbias[:, 0:8], A["router_b"].to_broadcast([P, 8]))

            def moe_load(m, w_gate, w_up, w_down):
                base, sbase = m.first, split_before[m.first]

                def load(i, g, parts):
                    i0, more = i if isinstance(i, tuple) else (i, None)
                    slot = (base + i0) % RAW
                    done = g * m.per + (sbase + i0 - RAW + 1)
                    if more is not None:
                        done = done + more
                    eng.wait_ge(T.sem("hi_done"), done)
                    eng.wait_ge(T.sem("lo_done"), done)
                    for dst, src in parts:
                        eng.dma_start(dst, src).then_inc(raw_landed[slot], 16)

                def columns(i, g, e, c, h):
                    i0 = i[0] if isinstance(i, tuple) else i
                    v = view(ring_raw, (base + i0) % RAW, KT // 2, 512)
                    r = slice(h * 512, (h + 1) * 512)
                    load(i, g, [(v[:, :, 0:256], w_gate(e, r, c)), (v[:, :, 256:512], w_up(e, r, c))])

                def rows(i, g, e, c):
                    i0 = i[0] if isinstance(i, tuple) else i
                    v = view(ring_raw, (base + i0) % RAW, 2, D)
                    load(i, g, [(v[:, k:k + 1, :], w_down(e, c, k)) for k in range(2)])

                chunk = (lambda g, c: (g, c)) if m.G == 1 else (lambda g, c: (g * m.G + c, 0))

                def group(g, end=False):
                    def step(c, jt):
                        at = lambda i0: i0 if jt is None else (i0, jt * 6)
                        turn = (lambda c: c) if jt is None else (lambda c: jt * 2 + c)
                        for h in range(2):
                            where = chunk(g + 1, 0) if c == m.NCH else chunk(g, turn(c))
                            columns(at(m.unit(c, h)), g, *where, h)
                        rows(at(m.unit(c - 1, 2)), g, *chunk(g, turn(c - 1)))
                    m.steps(eng, g, end, step)
                    if end:
                        rows(m.last_down(True), g, *chunk(g, m.NCH - 1))

                for h in range(2):
                    columns(h, 0, *chunk(0, 0), h)
                with eng.Fori(0, m.NG // 2 - 1) as it:
                    for par in range(2):
                        group(it * 2 + par)
                group(m.NG - 2)
                group(m.NG - 1, end=True)

            def m1_w(half):
                w = A["moe_w13"][0]
                return lambda e, r, c: w[bass.ds(e, 1), r, bass.ds(c * 256 + half * m1.f, 256)]\
                    .rearrange("a (k p) n -> p (a k) n", p=P)

            def m1_down(e, c, k):
                return A["moe_w2"][0][bass.ds(e, 1), bass.ds(c * 256 + k * P, P), :].rearrange("a p n -> p a n")

            def m2_w(name):
                w = A[name][0]
                return lambda e, r, c: w[bass.ds(e, 1), r, :].rearrange("a (k p) n -> p (a k) n", p=P)

            def m2_down(e, c, k):
                return A["exp_down_2"][0][bass.ds(e, 1), k * P:(k + 1) * P, :].rearrange("a p n -> p a n")

            def second_small():
                sp.eng.wait_ge(*T.at("shifted"))
                n_rel = A["rel_bias_2"].shape[1]
                rb = A["rel_bias_2"]
                back = bass.AP(rb.tensor, rb.offset + n_rel - 1, [[n_rel, HEADS2], [-1, n_rel]])
                with nc.allow_non_contiguous_dma(reason="a small table, read backwards"):
                    small_load("rel landed", rel[:, P - 1:P - 1 + n_rel], back)
                sp.eng.wait_ge(*T.at("rel ready"))
                for h in range(HEADS2):
                    row = rel[h:h + 1, :]
                    src = bass.AP(row.tensor, row.offset + P - 1, [list(row.ap[0]), [-1, P], [1, S]])
                    small_load("bias landed", relb[:, h, :], src)
                small_load("lora landed", du[0:64, :], A["decay_up_2"][0])
                small_load("lora landed", du[64:P, :], A["aaa_up_2"][0])
                small_load("lora landed", gu1, A["gate_up_2"][0, 0:P, :])
                sp.eng.wait_ge(*T.at("gu2 cleared"))
                small_load("lora landed", gu2[96:P, :], A["gate_up_2"][0, P:P + 32, :])

            for n, (key, split, kt, c, src) in enumerate(units):
                if src is None:
                    if n == m1.first:
                        moe_load(m1, m1_w(0), m1_w(1), m1_down)
                    if n == m2.first:
                        moe_load(m2, m2_w("exp_gate_2"), m2_w("exp_up_2"), m2_down)
                    continue
                if n == m1.first + m1.units + 2:
                    rest_sp(sp, m1, m1_w(0), m1_w(1), m1_down)
                if n == m2.first + m2.units + 2:
                    rest_sp(sp, m2, m2_w("exp_gate_2"), m2_w("exp_up_2"), m2_down)
                if key == ("q2", 0):
                    second_small()
                if key == ("gb", 0):
                    sp.eng.wait_ge(*T.at("m1 done"))
                    small_load("m2 router landed", rw[:, :, 0:32], A["router_exp_2"][0].rearrange("(k p) n -> p k n", p=P))
                    small_load("m2 router landed", rw[:, :, 32:36], A["router_grp_2"][0].rearrange("(k p) n -> p k n", p=P))
                    small_load("m2 router landed", rbias[:, 0:32], A["router_exp_bias_2"].to_broadcast([P, 32]))
                    small_load("m2 router landed", rbias[:, 32:36], A["router_grp_bias_2"].to_broadcast([P, 4]))
                if key == ("pg", 0):
                    sp.eng.wait_ge(*T.at("y out"))
                    sp.eng.wait_ge(*T.at("Hf m2"))
                    small_load("p landed", tD[:, 0:2, :], A["p_2"][0, 0].rearrange("(a p) d -> p a d", p=P))
                if n >= RAW:
                    m = n - RAW
                    if units[m][1]:
                        sp.eng.wait_ge(T.sem("hi_done"), split_before[m] + 1)
                        sp.eng.wait_ge(T.sem("lo_done"), split_before[m] + 1)
                    else:
                        sp.eng.wait_ge(T.sem("unit_done"), m + 1)
                dst = view(ring_raw, n % RAW, kt, c)
                half = kt // 2
                for h in range(2):
                    eng.dma_start(dst[:, h * half:(h + 1) * half, :], src[:, h * half:(h + 1) * half, :])\
                       .then_inc(raw_landed[n % RAW], 16)

            y = tB[:, :, :].rearrange("p (a k) t -> p a (k t)", a=TT)
            for a in range(TT):
                sp.eng.wait_ge(*T.at(f"out {a}"))
                eng.dma_start(out[0, a * P:(a + 1) * P, :], y[:, a, :]).then_inc(T.sem("stored"), 16)
            eng.wait_ge(T.sem("stored"), 16 * TT)

        @block.gpsimd
        def _(eng):
            pool = Engine(T, eng, "pool")
            eng.memset(tA[:, 0:4, :], 0.0).then_inc(pool.tick("rows cleared"), 1)
            eng.memset(scr[:, 0, :], 0.0).then_inc(pool.tick("c padded"), 1)
            eng.memset(ident[:, :], 0.0).then_inc(pool.tick(), 1)
            pool.eng.wait_ge(*pool.own())
            eng.affine_select(out=ident[:, :], in_=ident[:, :], compare_op=ALU.not_equal, fill=1.0,
                                        base=0, pattern=[[-1, P]], channel_multiplier=1).then_inc(pool.tick("ident"), 1)
            eng.memset(means[:, :], 1.0 / D).then_inc(pool.tick("means"), 1)
            eng.memset(eps[:, 0:1], LN_EPS).then_inc(pool.tick(), 1)
            eng.memset(eps[:, 1:2], GN_EPS).then_inc(pool.tick("eps"), 1)
            eng.memset(uT[:, :, 0:PAD], 0.0).then_inc(pool.tick("u padded"), 1)
            eng.memset(ones[:, :], 1.0).then_inc(pool.tick(), 1)
            eng.memset(before[:, :], 1.0).then_inc(pool.tick(), 1)
            eng.memset(lower[:, :, :], 1.0).then_inc(pool.tick(), 1)
            eng.iota(slots[:, :], pattern=[[1, P]], base=0, channel_multiplier=0,
                               allow_small_or_imprecise_dtypes=True).then_inc(pool.tick(), 1)
            eng.iota(part[:, :], pattern=[[0, 1]], base=0, channel_multiplier=1,
                               allow_small_or_imprecise_dtypes=True).then_inc(pool.tick(), 1)
            pool.eng.wait_ge(*pool.own())
            eng.affine_select(out=before[:, :], in_=before[:, :], compare_op=ALU.is_gt, fill=0.0,
                                        base=0, pattern=[[1, P]], channel_multiplier=-1).then_inc(pool.tick(), 1)
            eng.affine_select(out=lower[:, :, :], in_=lower[:, :, :], compare_op=ALU.is_gt, fill=0.0,
                                        base=0, pattern=[[1, 8], [-1, 8]], channel_multiplier=0).then_inc(pool.tick("routing constants"), 1)
            eng.iota(alibi[:, 0:P], pattern=[[1, P]], base=0, channel_multiplier=-1,
                               allow_small_or_imprecise_dtypes=True).then_inc(pool.tick(), 1)
            eng.iota(alibi[:, P:3 * P], pattern=[[1, 2 * P]], base=-P, channel_multiplier=-1,
                               allow_small_or_imprecise_dtypes=True).then_inc(pool.tick(), 1)
            pool.eng.wait_ge(*pool.own())
            for c0, base in ((0, 0), (P, -P)):
                w = P if c0 == 0 else 2 * P
                eng.affine_select(out=alibi[:, c0:c0 + w], in_=alibi[:, c0:c0 + w],
                                            compare_op=ALU.is_ge, fill=NEG, base=-base,
                                            pattern=[[-1, w]], channel_multiplier=1).then_inc(pool.tick("alibi"), 1)

            conv_pool(pool)
            pool.eng.wait_ge(*T.at("a1 done"))

            def keep_blocks(m, n):
                v = m.rearrange("p (b j) -> p b j", j=n)
                pool.eng.wait_ge(*pool.own())
                eng.affine_select(out=v, in_=v, compare_op=ALU.is_ge, fill=0.0, base=0,
                                            pattern=[[-n, P // n], [0, n]], channel_multiplier=1).then_inc(pool.tick(), 1)
                pool.eng.wait_ge(*pool.own())
                eng.affine_select(out=v, in_=v, compare_op=ALU.is_ge, fill=0.0, base=n - 1,
                                            pattern=[[n, P // n], [0, n]], channel_multiplier=-1).then_inc(pool.tick(), 1)

            for m, sign, op, n in ((m_su, 1, ALU.is_gt, 64), (m_sl16, -1, ALU.is_gt, 16), (m_iu, 1, ALU.is_ge, 64)):
                eng.memset(m, 1.0).then_inc(pool.tick(), 1)
                pool.eng.wait_ge(*pool.own())
                eng.affine_select(out=m, in_=m, compare_op=op, fill=0.0, base=0,
                                            pattern=[[sign, P]], channel_multiplier=-sign).then_inc(pool.tick(), 1)
                keep_blocks(m, n)
            eng.memset(m_d16, 1.0).then_inc(pool.tick(), 1)
            keep_blocks(m_d16, 16)
            pool.eng.wait_ge(*T.at("shifted"))
            eng.memset(gu2, 0.0).then_inc(pool.tick("gu2 cleared"), 1)
            pool.eng.wait_ge(*T.at("a2 done"))
            pool.eng.wait_ge(*T.at("Gh b2"))
            for m, n in ((m_o32, 32), (m_o64, 64), (m_d64, 64)):
                eng.memset(m, 1.0).then_inc(pool.tick(), 1)
                keep_blocks(m, n)
            pool.eng.wait_ge(*pool.own())
            eng.tensor_tensor(m_o64, m_o64, m_o32, ALU.subtract).then_inc(pool.tick(), 1)
            pool.eng.wait_ge(*pool.own())
            eng.tensor_tensor(m_o32, m_o32, m_d16, ALU.subtract).then_inc(pool.tick("chunk masks"), 1)

        @block.tensor
        def _(eng):
            pe = Engine(T, eng, "pe")
            mm = nc.tensor.matmul

            def ready(n):
                if units[n][1]:
                    pe.eng.wait_ge(T.sem("hi_done"), split_before[n] + 1)
                    pe.eng.wait_ge(T.sem("lo_done"), split_before[n] + 1)
                else:
                    landed(pe, n)

            def unit_end(ins, n, job=None):
                ins.then_inc(T.sem("unit_done"), 1)
                if job:
                    T.mark("mm " + job, "unit_done", n + 1)

            def columns(key, job, Xh, Xl):
                n = at_unit[key]
                kt, c = units[n][2], units[n][3]
                jobs = [job] if c <= 2 * P else [f"{job}.{i}" for i in range(c // (2 * P))]
                banks = [take(pe, i) for i in jobs]
                ready(n)
                wh, wl = weights(n)
                for blk in range(c // P):
                    o = banks[blk // 2][:, (blk % 2) * S:(blk % 2 + 1) * S]
                    for k in range(kt):
                        cs = slice(blk * P, (blk + 1) * P)
                        mm(o, wh[:, k, cs], Xh[:, k, :], start=(k == 0), stop=False)
                        mm(o, wh[:, k, cs], Xl[:, k, :], start=False, stop=False)
                        last = mm(o, wl[:, k, cs], Xh[:, k, :], start=False, stop=(k == kt - 1))
                unit_end(last, n)
                for i in jobs:
                    T.mark("mm " + i, "unit_done", n + 1)

            def rows_of(key, job, Xh, Xl):
                n = at_unit[key]
                b = take(pe, job)
                ready(n)
                wh, wl = weights(n)
                kt, c = units[n][2], units[n][3]
                for t in range(TT):
                    o = b[:, t * c:(t + 1) * c]
                    ts = slice(t * P, (t + 1) * P)
                    for k in range(kt):
                        mm(o, Xh[:, k, ts], wh[:, k, :], start=(k == 0), stop=False)
                        mm(o, Xl[:, k, ts], wh[:, k, :], start=False, stop=False)
                        last = mm(o, Xh[:, k, ts], wl[:, k, :], start=False, stop=(k == kt - 1))
                unit_end(last, n, job)

            to_turn = []

            def adaptive(l, j, turned):
                n = at_unit[("ada", l, j)]
                if j % 2 == 0:
                    take(pe, f"ada {l} {j // 2}")
                b = bank[T.banks[f"ada {l} {j // 2}"]]
                ready(n)
                w, _ = weights(n)
                for k in range(KT):
                    q = 32 * (k % 4)
                    last = mm(b[q:q + 32, (j % 2) * 256:(j % 2) * 256 + 256], cpad[:, k, :], w[:, k, :],
                              start=(k < 4), stop=(k >= 4), skip_group_check=True)
                unit_end(last, n, f"ada {l} {j // 2}" if j % 2 else None)
                if j % 2:
                    to_turn.append((l, j // 2))
                    if len(to_turn) > 1:
                        turn_row(turned)

            def turn_row(turned):
                l, p = to_turn.pop(0)
                o = turned(l, p)
                pe.eng.wait_ge(*T.at(f"row {l} {p}"))
                for i in range(4):
                    last = mm(o[:, i:i + 1], ada_row((l, p))[:, i * P:(i + 1) * P], ones[:, 0:1],
                              start=True, stop=True)
                last.then_inc(pe.tick(f"mm turn {l} {p}"), 1)

            def transposes(job, pairs, group="A"):
                b = take(pe, job, group)
                for o, src in pairs:
                    last = nc.tensor.transpose(b[:, o * P:(o + 1) * P], src, ident[:, :])
                last.then_inc(pe.tick("mm " + job), 1)

            def ln_stats(name, z):
                b = take(pe, "ln " + name)
                pe.eng.wait_ge(*T.at("means"))
                for k in range(KT):
                    pe.eng.wait_ge(*T.at(f"z {name} {k}"))
                    last = mm(b[:, 0:S], means[:, :], z[:, k, :], start=(k == 0), stop=(k == KT - 1))
                last.then_inc(pe.tick(f"mm mean {name}"), 1)
                b = take(pe, "lv " + name)
                for k in range(KT):
                    pe.eng.wait_ge(*T.at(f"square {name} {k // 2}"))
                    last = mm(b[:, 0:S], means[:, :], tC[:, k, :], start=(k == 0), stop=(k == KT - 1))
                last.then_inc(pe.tick(f"mm var {name}"), 1)

            pe.eng.wait_ge(*T.at("rows landed"))
            pe.eng.wait_ge(*T.at("ident"))
            rows = tA[:, 0:4, :].rearrange("p k t -> p (k t)")
            for j in range(2):
                transposes(f"cols {j}", [(k, rows[:, (4 * j + k) * P:(4 * j + k + 1) * P]) for k in range(4)])
            pe.eng.wait_ge(*T.at("x landed"))
            x_in = tB[:, :, :].rearrange("p (a k) t -> p a (k t)", a=TT)
            for j in range(4):
                transposes(f"x {j}", [(2 * k + a, x_in[:, a, (2 * j + k) * P:(2 * j + k + 1) * P])
                                      for k in range(2) for a in range(TT)])
            pe.stage = "conv"
            pe.eng.wait_ge(*T.at("ccol"))
            pe.eng.wait_ge(*T.at("routing constants"))
            b = take(pe, "turn first", "B")
            first = lambda l, p: b[:, 4 * p:4 * p + 4]
            for j in range(8):
                adaptive(0, j, first)
            turn_row(first)
            pe.eng.wait_ge(*T.at("Hh conv"))
            pe.eng.wait_ge(*T.at("Hl conv"))
            for j in range(4):
                columns(("conv a", j), f"conv a {j}", Hh, Hl)
                columns(("conv g", j), f"conv g {j}", Hh, Hl)
            b2 = take(pe, "turn rest", "B")
            rest = lambda l, p: b2[:, 4 * (p - 4 if l == 0 else 8 + p):][:, 0:4]
            for j in range(8, 24):
                adaptive(0, j, rest)
            for j in range(8):
                adaptive(2, j, rest)
            turn_row(rest)
            ln_stats("conv", tA)
            pe.eng.wait_ge(*T.at("Gh conv"))
            pe.eng.wait_ge(*T.at("Gl conv"))
            for j in range(4):
                columns(("conv_out", j), f"out0 {j}", Gh, Gl)
            ln_stats("ln0", tA)
            pe.stage = "ffn"
            pe.eng.wait_ge(*T.at("Hh ffn"))
            pe.eng.wait_ge(*T.at("Hl ffn"))
            acc = [take(pe, f"ffn acc {i}", "D") for i in range(4)]
            late = list(range(24))

            def turned(l, p):
                if p % 2 == 0:
                    take(pe, f"turn {l} {p // 2}")
                return bank[T.banks[f"turn {l} {p // 2}"]][:, 4 * (p % 2):4 * (p % 2) + 4]

            def ffn_down(j):
                n = at_unit[("ffn2", j)]
                pe.eng.wait_ge(*T.at(f"fh {j}"))
                pe.eng.wait_ge(*T.at(f"fl {j}"))
                ready(n)
                wh, wl = weights(n)
                for cb in range(KT):
                    cs = slice(cb * P, (cb + 1) * P)
                    o = acc[cb // 2][:, (cb % 2) * S:(cb % 2 + 1) * S]
                    for k in range(2):
                        g = 2 * (j % 4) + k
                        first = j == 0 and cb % 2 == 0 and k == 0
                        end = j == NP - 1 and k == 1
                        mm(o, wh[:, k, cs], Gh[:, g, :], start=first, stop=False, skip_group_check=True)
                        mm(o, wh[:, k, cs], Gl[:, g, :], start=False, stop=False, skip_group_check=True)
                        last = mm(o, wl[:, k, cs], Gh[:, g, :], start=False, stop=end, skip_group_check=True)
                unit_end(last, n)
                T.mark(f"ffn down {j}", "unit_done", n + 1)
                for _ in range(3):
                    if late:
                        adaptive(1, late.pop(0), turned)
                        if not late:
                            turn_row(turned)

            for j in range(NP):
                columns(("ffn a", j), f"ffn a {j}", Hh, Hl)
                columns(("ffn b", j), f"ffn b {j}", Hh, Hl)
                if j:
                    ffn_down(j - 1)
            ffn_down(NP - 1)
            ln_stats("ln1", tA)
            pe.stage = "attn"
            pe.eng.wait_ge(*T.at("Hh kv"))
            pe.eng.wait_ge(*T.at("Hl kv"))
            for j in range(4):
                columns(("k", j), f"k {j}", Hh, Hl)
            for j in range(4):
                rows_of(("v", j), f"v {j}", Hh, Hl)
            pe.eng.wait_ge(*T.at("Gh q"))
            pe.eng.wait_ge(*T.at("Gl q"))
            for j in range(4):
                columns(("q", j), f"q {j}", Gh, Gl)
            attention(pe, "a1", HEADS, tD, tB, tC[:, :, :].rearrange("p (a k) t -> p a (k t)", a=TT))
            pe.eng.wait_ge(*T.at("Hh wo"))
            pe.eng.wait_ge(*T.at("Hl wo"))
            for j in range(4):
                columns(("wo", j), f"wo {j}", Hh, Hl)
            ln_stats("ln2", tA)
            pe.stage = "m1"
            moe_pe(pe, m1, tD)
            rest_pe(pe, m1, tD)
            ln_stats("ln3", tA)
            pe.stage = "b2"
            ln_stats("ln4", tA)
            pe.eng.wait_ge(*T.at("Hh b2"))
            pe.eng.wait_ge(*T.at("Hl b2"))
            for j in range(8):
                columns(("rw", j), f"rw {j}", Hh, Hl)
            for j in range(2):
                rows_of(("v2", j), f"v2 {j}", Hh, Hl)
            for key in ("q2", "k2"):
                for j in range(2):
                    columns((key, j), f"{key} {j}", Hh, Hl)
            for j in range(4):
                columns(("ga", j), f"ga {j}", Hh, Hl)
            attention(pe, "a2", HEADS2, Q2, K2, V2)
            pe.eng.wait_ge(*T.at("Gh b2"))
            pe.eng.wait_ge(*T.at("Gl b2"))
            for j in range(2):
                columns(("wa", j), f"wa {j}", Gh[:, 0:4, :], Gh[:, 4:8, :])
            rwkv_pe(pe)
            for j in range(4):
                columns(("gb", j), f"gb {j}", Hh, Hl)
            pe.eng.wait_ge(*T.at("Gh wb"))
            pe.eng.wait_ge(*T.at("Gl wb"))
            for j in range(2):
                columns(("wb", j), f"wb {j}", Gh[:, 0:4, :], Gh[:, 4:8, :])
            pe.eng.wait_ge(*T.at("Hh mix"))
            pe.eng.wait_ge(*T.at("Hl mix"))
            for j in range(4):
                columns(("w_out", j), f"w_out {j}", Hh, Hl)
            ln_stats("ln5", tA)
            pe.stage = "m2"
            moe_pe(pe, m2, xT)
            rest_pe(pe, m2, xT)
            ln_stats("ln6", tA)
            pe.stage = "ple"
            pe.eng.wait_ge(*T.at("p landed"))
            transposes("pT", [(2 * k + a, tD[:, a, k * P:(k + 1) * P]) for k in range(2) for a in range(TT)])
            pe.eng.wait_ge(*T.at("Hh ple"))
            pe.eng.wait_ge(*T.at("Hl ple"))
            for j in range(4):
                columns(("pg", j), f"pg {j}", Hh, Hl)
            pe.eng.wait_ge(*T.at("Gh ple"))
            pe.eng.wait_ge(*T.at("Gl ple"))
            columns(("pp", 0), "pp", Gh[:, 0:2, :], Gl[:, 0:2, :])
            ln_stats("ln7", tA)
            pe.eng.wait_ge(*T.at("x out"))
            for a in range(TT):
                for j in range(2):
                    transposes(f"out {a} {j}", [(k, tD[:, 4 * j + k, a * P:(a + 1) * P]) for k in range(4)])

        @block.scalar
        def _(eng):
            act = Engine(T, eng, "act")
            run = nc.scalar.activation

            def halves_hi(name, dst, src):
                for j in range(4):
                    act.eng.wait_ge(*T.at(f"f {name} {j}"))
                    run(dst[:, 2 * j:2 * j + 2, :], src[:, 2 * j:2 * j + 2, :], ACT.Copy).then_inc(act.tick(f"hi {name} {j}"), 1)

            def ln(name):
                for h in range(4):
                    act.eng.wait_ge(*T.at(f"centred {name} {h}"))
                    run(tC[:, 2 * h:2 * h + 2, :], tA[:, 2 * h:2 * h + 2, :], ACT.Square)\
                        .then_inc(act.tick(f"square {name} {h}"), 1)
                act.eng.wait_ge(*T.at("eps"))
                run(warm[:, :], eps[:, 0:1], ACT.Sqrt)
                act.eng.wait_ge(*T.at(f"mm var {name}"))
                act.eng.wait_ge(*T.at("eps"))
                run(stat[:, 0, :], ps("lv " + name)[:, 0:S], ACT.Sqrt, bias=eps[:, 0:1]).then_inc(act.tick(f"ev lv {name}"), 1)
                T.mark(f"std {name}", *act.last)

            def row_out(l, p):
                split_hi(act, at_unit[("ada", l, 2 * p + 1)] + 2)
                act.eng.wait_ge(*T.at(f"mm ada {l} {p}"))
                n = at_pair[(l, p)]
                if n >= 3:
                    act.eng.wait_ge(*T.at("mm turn %d %d" % pairs[n - 3]))
                run(ada_row((l, p)), ps(f"ada {l} {p}")[:, :], ACT.Copy).then_inc(act.tick(f"ev ada {l} {p}"), 1)
                T.mark(f"row {l} {p}", *act.last)

            split_hi(act, 0)
            for j in range(2):
                act.eng.wait_ge(*T.at(f"mm cols {j}"))
                run(cols[:, 4 * j:4 * j + 4, :],
                             ps(f"cols {j}")[:, :].rearrange("p (k r) -> p k r", r=P)[:, :, 0:NROW], ACT.Copy).then_inc(act.tick(f"ev cols {j}"), 1)
            act.eng.wait_ge(*act.own())
            act.eng.wait_ge(*T.at("c padded"))
            run(cpad[:, :, 0], cols[:, :, ROW["c"]], ACT.Silu).then_inc(act.tick("ccol"), 1)
            for j in range(4):
                act.eng.wait_ge(*T.at(f"mm x {j}"))
                run(xT[:, 2 * j:2 * j + 2, :], ps(f"x {j}")[:, :].rearrange("p (k t) -> p k t", k=2),
                             ACT.Copy).then_inc(act.tick(f"ev x {j}"), 1)
            act.stage = "conv"
            for p in range(4):
                row_out(0, p)
            halves_hi("conv", Hh, tD)
            T.mark("Hh conv", *act.last)
            for j in range(4):
                split_hi(act, at_unit[("conv g", j)] + 2)
                act.eng.wait_ge(*T.at(f"mm conv g {j}"))
                for b in range(2):
                    k = 2 * j + b
                    run(tC[:, k, :], ps(f"conv g {j}")[:, b * S:(b + 1) * S], ACT.Sigmoid,
                                 bias=col("conv_in_b", k, 1)).then_inc(act.tick(f"ev conv g {j}"), 1)
                T.mark(f"gate {j}", *act.last)
            conv_act(act, row_out)
            split_hi(act, at_unit[("conv_out", 2)])
            ln("conv")
            for j in range(4):
                act.eng.wait_ge(*T.at(f"normed conv {j // 2}"))
                for k in (2 * j, 2 * j + 1):
                    run(tD[:, k, :], tA[:, k, :], ACT.Silu, bias=col("conv_norm_b", k),
                                 scale=col("conv_norm_g", k)).then_inc(act.tick(), 1)
                T.mark(f"f convo {j}", *act.last)
                act.eng.wait_ge(*act.own())
                run(Gh[:, 2 * j:2 * j + 2, :], tD[:, 2 * j:2 * j + 2, :], ACT.Copy).then_inc(act.tick(f"hi convo {j}"), 1)
            T.mark("Gh conv", *act.last)

            def gated(l, v, key, job, bias=None):
                for j in range(4):
                    split_hi(act, at_unit[(key, j)] + 2)
                    act.eng.wait_ge(*T.at(f"mm {job} {j}"))
                    act.eng.wait_ge(*T.at(f"mods {l} {v}"))
                    for b in range(2):
                        k = 2 * j + b
                        run(tB[:, k, :], ps(f"{job} {j}")[:, b * S:(b + 1) * S], ACT.Identity,
                                     scale=mod(l, v, k), bias=gb[:, k:k + 1] if bias else 0.0).then_inc(act.tick(f"ev {job} {j}"), 1)
                    T.mark(f"gated {job} {j}", *act.last)

            act.eng.wait_ge(*T.at("gb"))
            gated(0, 2, "conv_out", "out0", True)
            split_hi(act, at_unit[("ffn b", 0)] + 1)
            ln("ln0")
            halves_hi("ffnin", Hh, tD)
            T.mark("Hh ffn", *act.last)
            act.stage = "ffn"
            late = list(range(24))
            for j in range(NP + 1):
                if j < NP:
                    split_hi(act, at_unit[("ffn b", j)] + 2)
                    act.eng.wait_ge(*T.at(f"mm ffn a {j}"))
                    if j >= 4:
                        act.eng.wait_ge(*T.at(f"fh {j - 4}"))
                        act.eng.wait_ge(*T.at(f"fl {j - 4}"))
                    run(tB[:, 2 * (j % 4):2 * (j % 4) + 2, :],
                                 ps(f"ffn a {j}")[:, :].rearrange("p (k t) -> p k t", k=2), ACT.Silu).then_inc(act.tick(f"ev ffn a {j}"), 1)
                    act.eng.wait_ge(*T.at(f"f ffn {j}"))
                    if j >= 4:
                        act.eng.wait_ge(*T.at(f"ffn down {j - 4}"))
                    g = 2 * (j % 4)
                    run(Gh[:, g:g + 2, :], tC[:, g:g + 2, :], ACT.Copy).then_inc(act.tick(f"fh {j}"), 1)
                if j:
                    for _ in range(3):
                        if late:
                            i = late.pop(0)
                            if i % 2:
                                row_out(1, i // 2)
            split_hi(act, at_unit[("ffn2", NP - 1)] + 3)
            for i in range(4):
                act.eng.wait_ge(*T.at(f"ffn down {NP - 1}"))
                act.eng.wait_ge(*T.at("mods 0 5"))
                for b in range(2):
                    k = 2 * i + b
                    run(tB[:, k, :], ps(f"ffn acc {i}")[:, b * S:(b + 1) * S], ACT.Identity,
                                 scale=mod(0, 5, k)).then_inc(act.tick(f"ev ffn acc {i}"), 1)
                T.mark(f"gated ffn {i}", *act.last)
            ln("ln1")
            act.stage = "attn"
            halves_hi("kv", Hh, tD)
            T.mark("Hh kv", *act.last)
            halves_hi("q", Gh, tB)
            T.mark("Gh q", *act.last)
            for j in range(4):
                split_hi(act, at_unit[("k", j)] + 2)
                act.eng.wait_ge(*T.at(f"mm k {j}"))
                if j == 0:
                    act.eng.wait_ge(*T.at("Gl q"))
                run(tB[:, 2 * j:2 * j + 2, :], ps(f"k {j}")[:, :].rearrange("p (k t) -> p k t", k=2),
                             ACT.Copy).then_inc(act.tick(f"ev k {j}"), 1)
                T.mark(f"a1 kT {j}", *act.last)
            V = tC[:, :, :].rearrange("p (a k) t -> p a (k t)", a=TT)
            for j in range(4):
                split_hi(act, at_unit[("v", j)] + 2)
                act.eng.wait_ge(*T.at(f"mm v {j}"))
                run(V[:, :, 256 * j:256 * j + 256],
                             ps(f"v {j}")[:, :].rearrange("p (a c) -> p a c", a=TT), ACT.Copy).then_inc(act.tick(f"ev v {j}"), 1)
            T.mark("a1 v", *act.last)
            for j in range(4):
                split_hi(act, at_unit[("q", j)] + 2)
                act.eng.wait_ge(*T.at(f"mm q {j}"))
                run(tD[:, 2 * j:2 * j + 2, :], ps(f"q {j}")[:, :].rearrange("p (k t) -> p k t", k=2),
                             ACT.Copy, scale=0.125).then_inc(act.tick(f"ev q {j}"), 1)
                T.mark(f"a1 qT {j}", *act.last)
            softmax_exp(act, "a1", HEADS, Hh)
            T.mark("Hh wo", *act.last)
            gated(1, 2, "wo", "wo")
            ln("ln2")
            act.stage = "m1"
            moe_act(act, m1)
            rest_act(act, m1)
            act.eng.wait_ge(*T.at("m1 done"))
            for k in range(KT):
                run(tD[:, k, :], tB[:, k, :], ACT.Identity, scale=mod(1, 5, k)).then_inc(act.tick(f"gated m1 {k}"), 1)
            ln("ln3")
            act.stage = "b2"
            ln("ln4")
            halves_hi("b2", Hh, xT)
            T.mark("Hh b2", *act.last)
            for j in range(8):
                split_hi(act, at_unit[("rw", j)] + 2)
                act.eng.wait_ge(*T.at(f"mm rw {j}"))
                w = 2 if j < 7 else 1
                k = (2 * j) % 8
                if j >= 4:
                    act.eng.wait_ge(*T.at(f"mix {j - 4}"))
                run(uT[:, k:k + w, PAD:PAD + S],
                             ps(f"rw {j}")[:, 0:w * S].rearrange("p (k t) -> p k t", k=w), ACT.Copy).then_inc(act.tick(f"ev rw {j}"), 1)
            for j in range(2):
                split_hi(act, at_unit[("v2", j)] + 2)
                act.eng.wait_ge(*T.at(f"mm v2 {j}"))
                run(V2[:, :, 256 * j:256 * j + 256], bank_view(ps(f"v2 {j}")), ACT.Copy).then_inc(act.tick(f"ev v2 {j}"), 1)
            T.mark("a2 v", *act.last)
            for key, dst, sc in (("q2", Q2, 0.125), ("k2", K2, 1.0)):
                for j in range(2):
                    split_hi(act, at_unit[(key, j)] + 2)
                    act.eng.wait_ge(*T.at(f"mm {key} {j}"))
                    run(dst[:, 2 * j:2 * j + 2, :],
                                 ps(f"{key} {j}")[:, :].rearrange("p (k t) -> p k t", k=2), ACT.Copy, scale=sc).then_inc(act.tick(f"ev {key} {j}"), 1)
                    T.mark(f"a2 {key[0]}T {j}", *act.last)
            for j in range(4):
                split_hi(act, at_unit[("ga", j)] + 2)
                act.eng.wait_ge(*T.at(f"mm ga {j}"))
                run(MA[:, 2 * j:2 * j + 2, :], ps(f"ga {j}")[:, :].rearrange("p (k t) -> p k t", k=2),
                             ACT.Sigmoid).then_inc(act.tick(f"ev ga {j}"), 1)
            T.mark("gate a", *act.last)
            softmax_exp(act, "a2", HEADS2, Gh)
            T.mark("Gh b2", *act.last)
            split_hi(act, at_unit[("wa", 1)] + 2)
            rwkv_act(act)
            act.stage = "b2 end"
            for j in range(4):
                split_hi(act, at_unit[("gb", j)] + 2)
                act.eng.wait_ge(*T.at(f"mm gb {j}"))
                act.eng.wait_ge(*T.at("y out"))
                run(tA[:, 2 * j:2 * j + 2, :], ps(f"gb {j}")[:, :].rearrange("p (k t) -> p k t", k=2),
                             ACT.Sigmoid).then_inc(act.tick(f"ev gb {j}"), 1)
            T.mark("gate b", *act.last)
            split_hi(act, at_unit[("wb", 1)] + 2)
            halves_hi("mix", Hh, tC)
            T.mark("Hh mix", *act.last)
            for j in range(4):
                split_hi(act, at_unit[("w_out", j)] + 2)
            ln("ln5")
            act.stage = "m2"
            moe_act(act, m2)
            rest_act(act, m2)
            ln("ln6")
            act.stage = "ple"
            halves_hi("ple", Hh, xT)
            T.mark("Hh ple", *act.last)
            act.eng.wait_ge(*T.at("mm pT"))
            run(Gh[:, 0:2, :], ps("pT")[:, :].rearrange("p (k t) -> p k t", k=2), ACT.Copy).then_inc(act.tick("Gh ple"), 1)
            for j in range(4):
                split_hi(act, at_unit[("pg", j)] + 2)
                act.eng.wait_ge(*T.at(f"mm pg {j}"))
                run(tB[:, 2 * j:2 * j + 2, :], ps(f"pg {j}")[:, :].rearrange("p (k t) -> p k t", k=2),
                             ACT.Sigmoid).then_inc(act.tick(f"ev pg {j}"), 1)
                T.mark(f"gate p {j}", *act.last)
            ln("ln7")
            y = tB[:, :, :].rearrange("p (a k) t -> p a (k t)", a=TT)
            for a in range(TT):
                for j in range(2):
                    act.eng.wait_ge(*T.at(f"mm out {a} {j}"))
                    run(y[:, a, 512 * j:512 * j + 512], ps(f"out {a} {j}")[:, :], ACT.Copy).then_inc(act.tick(f"ev out {a} {j}"), 1)
                T.mark(f"out {a}", *act.last)

        @block.vector
        def _(eng):
            dve = Engine(T, eng, "dve")
            tt, ts, stt = nc.vector.tensor_tensor, nc.vector.tensor_scalar, nc.vector.scalar_tensor_tensor

            def halves_lo(name, dst, src, hi):
                for j in range(4):
                    s = slice(2 * j, 2 * j + 2)
                    dve.eng.wait_ge(*T.at(f"hi {name} {j}"))
                    tt(dst[:, s, :], src[:, s, :], hi[:, s, :].bitcast(F32), ALU.subtract).then_inc(dve.tick(), 1)

            def modulate(name, l, vs, vb, dst):
                dve.eng.wait_ge(*T.at(f"mods {l} {vs}"))
                dve.eng.wait_ge(*T.at(f"mods {l} {vb}"))
                for k in range(KT):
                    ts(dst[:, k, :], xT[:, k, :], mod(l, vs, k), mod(l, vb, k), ALU.mult, ALU.add).then_inc(dve.tick(), 1)
                    T.mark(f"f {name} {k // 2}", *dve.last)

            def ln(name):
                b = ps("ln " + name)
                dve.eng.wait_ge(*T.at(f"mm mean {name}"))
                for h in range(4):
                    s = slice(2 * h, 2 * h + 2)
                    tt(tA[:, s, :], tA[:, s, :], b[:, 0:S].unsqueeze(1).to_broadcast([P, 2, S]), ALU.subtract)\
                        .then_inc(dve.tick(f"centred {name} {h}"), 1)
                T.mark("ev ln " + name, *dve.last)
                dve.eng.wait_ge(*T.at(f"std {name}"))
                nc.vector.reciprocal(stat[:, 1, :], stat[:, 0, :]).then_inc(dve.tick(), 1)
                dve.eng.wait_ge(*dve.own())
                for h in range(2):
                    s = slice(4 * h, 4 * h + 4)
                    dve.eng.wait_ge(*T.at(f"square {name} {2 * h + 1}"))
                    tt(tA[:, s, :], tA[:, s, :], stat[:, 1, :].unsqueeze(1).to_broadcast([P, 4, S]),
                                ALU.mult).then_inc(dve.tick(f"normed {name} {h}"), 1)

            def affine(g, b, i):
                dve.eng.wait_ge(*dve.own())
                for k in range(KT):
                    ts(xT[:, k, :], tA[:, k, :], col(g, k, i), col(b, k, i), ALU.mult, ALU.add).then_inc(dve.tick(), 1)
                T.mark(f"x {g} {i}", *dve.last)
                dve.eng.wait_ge(*dve.own())

            def residual(name, job, key, l=None):
                for j in range(4):
                    if key:
                        split_lo(dve, at_unit[(key, j)] + 2)
                    dve.eng.wait_ge(*T.at(f"gated {job} {j}"))
                    for k in (2 * j, 2 * j + 1):
                        stt(tA[:, k, :], xT[:, k, :], ALPHA, tB[:, k, :], ALU.mult, ALU.add).then_inc(dve.tick(f"z {name} {k}"), 1)

            split_lo(dve, 0)
            dve.eng.wait_ge(*T.at("ev cols 1"))
            for l in range(2):
                for v in (1, 2, 4, 5):
                    c = cols[:, :, ROW["ada_b"] + VEC(l, v)]
                    nc.vector.tensor_scalar(c, c, 1.0, None, ALU.add).then_inc(dve.tick(), 1)
            c = cols[:, :, ROW["kv_ada_b"] + 1]
            nc.vector.tensor_scalar(c, c, 1.0, None, ALU.add).then_inc(dve.tick("bias"), 1)
            dve.stage = "conv"

            def biased(job, vectors):
                for i, (l, v) in enumerate(vectors):
                    dve.eng.wait_ge(*T.at(f"mm turn {l} {2 * v + 1}"))
                for i, (l, v) in enumerate(vectors):
                    row = ROW["ada_b"] + VEC(l, v) if l < 2 else ROW["kv_ada_b"] + v
                    tt(mods[:, VEC(l, v), :], ps(job)[:, 8 * i:8 * i + 8], cols[:, :, row], ALU.add)\
                        .then_inc(dve.tick("ev " + job), 1)
                for l, v in vectors:
                    T.mark(f"mods {l} {v}", *dve.last)

            dve.eng.wait_ge(*T.at("bias"))
            biased("turn first", [(0, 0), (0, 1)])
            for j in range(4):
                dve.eng.wait_ge(*T.at(f"ev x {j}"))
            modulate("conv", 0, 1, 0, tD)
            halves_lo("conv", Hl, tD, Hh)
            T.mark("Hl conv", *dve.last)
            for j in range(4):
                split_lo(dve, at_unit[("conv g", j)] + 2)
                dve.eng.wait_ge(*T.at(f"mm conv a {j}"))
                dve.eng.wait_ge(*T.at(f"gate {j}"))
                dve.eng.wait_ge(*T.at("u padded"))
                for b in range(2):
                    k = 2 * j + b
                    stt(uT[:, k, PAD:PAD + S], ps(f"conv a {j}")[:, b * S:(b + 1) * S],
                                 col("conv_in_b", k), tC[:, k, :], ALU.add, ALU.mult).then_inc(dve.tick(f"ev conv a {j}"), 1)
            conv_dve(dve, range(0, KT - POOL_BLOCKS))
            split_lo(dve, at_unit[("conv_out", 2)])
            biased("turn rest", [(0, v) for v in range(2, 6)] + [(2, 0), (2, 1)])
            ln("conv")
            halves_lo("convo", Gl, tD, Gh)
            T.mark("Gl conv", *dve.last)
            dve.eng.wait_ge(*T.at("mods 0 2"))
            tt(gb[:, :], cols[:, :, ROW["conv_out_b"]], mods[:, VEC(0, 2), :], ALU.mult).then_inc(dve.tick("gb"), 1)
            residual("ln0", "out0", "conv_out")
            split_lo(dve, at_unit[("ffn b", 0)] + 1)
            ln("ln0")
            affine("ln_g", "ln_b", 0)
            modulate("ffnin", 0, 4, 3, tD)
            halves_lo("ffnin", Hl, tD, Hh)
            T.mark("Hl ffn", *dve.last)
            dve.stage = "ffn"
            late = list(range(24))
            for j in range(NP + 1):
                if j < NP:
                    split_lo(dve, at_unit[("ffn b", j)] + 2)
                    dve.eng.wait_ge(*T.at(f"mm ffn b {j}"))
                    dve.eng.wait_ge(*T.at(f"ev ffn a {j}"))
                    if j >= 4:
                        dve.eng.wait_ge(*T.at(f"fh {j - 4}"))
                        dve.eng.wait_ge(*T.at(f"ffn down {j - 4}"))
                    g = 2 * (j % 4)
                    tt(tC[:, g:g + 2, :], tB[:, g:g + 2, :],
                                ps(f"ffn b {j}")[:, :].rearrange("p (k t) -> p k t", k=2), ALU.mult).then_inc(dve.tick(f"ev ffn b {j}"), 1)
                    T.mark(f"f ffn {j}", *dve.last)
                    dve.eng.wait_ge(*T.at(f"fh {j}"))
                    tt(Gl[:, g:g + 2, :], tC[:, g:g + 2, :], Gh[:, g:g + 2, :].bitcast(F32),
                                ALU.subtract).then_inc(dve.tick(f"fl {j}"), 1)
                if j:
                    for _ in range(3):
                        if late:
                            i = late.pop(0)
                            if i == 23 or (i >= 5 and i % 4 == 1):
                                split_lo(dve, at_unit[("ada", 1, i)] + 2)
                                v = 5 if i == 23 else (i - 5) // 4
                                biased(f"turn 1 {v}", [(1, v)])
            split_lo(dve, at_unit[("ffn2", NP - 1)] + 3)
            residual("ln1", "ffn", None)
            ln("ln1")
            affine("ln_g", "ln_b", 1)
            dve.stage = "attn"
            modulate("kv", 2, 1, 0, tD)
            halves_lo("kv", Hl, tD, Hh)
            T.mark("Hl kv", *dve.last)
            modulate("q", 1, 1, 0, tB)
            halves_lo("q", Gl, tB, Gh)
            T.mark("Gl q", *dve.last)
            for key in ("k", "v", "q"):
                for j in range(4):
                    split_lo(dve, at_unit[(key, j)] + (2 if key == "q" and j == 3 else 2))
            softmax_rest(dve, "a1", HEADS, lambda h, c0, w: (alibi[:, c0:c0 + w], 2.0 ** (-8.0 * (h + 1) / HEADS)), Hl, Hh)
            T.mark("Hl wo", *dve.last)
            T.mark("a1 done", *dve.last)
            residual("ln2", "wo", "wo")
            ln("ln2")
            affine("ln_g", "ln_b", 2)
            dve.stage = "m1"
            modulate("m1", 1, 4, 3, tD)
            T.mark("Hf m1", *dve.last)
            moe_dve(dve, m1)
            rest_dve(dve, m1)
            for k in range(KT):
                dve.eng.wait_ge(*T.at(f"gated m1 {k}"))
                stt(tA[:, k, :], xT[:, k, :], ALPHA, tD[:, k, :], ALU.mult, ALU.add).then_inc(dve.tick(f"z ln3 {k}"), 1)
            ln("ln3")
            dve.eng.wait_ge(*dve.own())
            for k in range(KT):
                ts(tA[:, k, :], tA[:, k, :], col("ln_g", k, 3), col("ln_b", k, 3), ALU.mult, ALU.add).then_inc(dve.tick(f"z ln4 {k}"), 1)
            dve.stage = "b2"
            ln("ln4")
            affine("ln_in_g_2", "ln_in_b_2", 0)
            for j in range(4):
                T.mark(f"f b2 {j}", *dve.last)
            halves_lo("b2", Hl, xT, Hh)
            T.mark("Hl b2", *dve.last)
            dve.eng.wait_ge(*T.at("mm mean ln4"))
            dve.eng.wait_ge(*T.at("mm var ln4"))
            for j in range(8):
                split_lo(dve, at_unit[("rw", j)] + 2)
                dve.eng.wait_ge(*T.at(f"ev rw {j}"))
                w = 2 if j < 7 else 1
                k = (2 * j) % 8
                u = uT[:, k:k + w, :]
                d = (tA if j < 4 else tB)[:, k:k + w, :]
                tt(d, u[:, :, PAD - 1:PAD - 1 + S], u[:, :, PAD:PAD + S], ALU.subtract).then_inc(dve.tick(), 1)
                dve.eng.wait_ge(*dve.own())
                for i in range(w):
                    blk = 2 * j + i
                    mu = (col("tok_mix_2", blk) if blk < 8 else col("tok_mix_2", blk - 8, 1) if blk < 14
                          else col("tok_mix_2", 0, 2))
                    stt(d[:, i, :], d[:, i, :], mu, u[:, i, PAD:PAD + S], ALU.mult, ALU.add).then_inc(dve.tick(f"mix {j}"), 1)
            T.mark("shifted", *dve.last)
            dve.eng.wait_ge(*T.at("rel landed"))
            nc.vector.tensor_copy(rel[:, 0:P - 1], rel[:, P - 1:P].to_broadcast([HEADS2, P - 1])).then_inc(dve.tick("rel ready"), 1)
            for key, n in (("v2", 2), ("q2", 2), ("k2", 2), ("ga", 4)):
                for j in range(n):
                    split_lo(dve, at_unit[(key, j)] + 2)
            dve.eng.wait_ge(*T.at("bias landed"))
            nc.vector.memset(relb[0:64, :, 3 * 64:4 * 64], NEG).then_inc(dve.tick(), 1)
            dve.eng.wait_ge(*dve.own())
            softmax_rest(dve, "a2", HEADS2, lambda h, c0, w: (relb[:, h, P:S] if c0 == 0 else relb[:, h, :], None),
                         Gh[:, 4:8, :], Gh)
            T.mark("Gl b2", *dve.last)
            T.mark("a2 done", *dve.last)
            split_lo(dve, at_unit[("wa", 1)] + 2)
            dve.eng.wait_ge(*T.at("gate a"))
            for j in range(2):
                for i in range(2):
                    dve.eng.wait_ge(*T.at(f"mm wa {j}.{i}"))
                    k = 4 * j + 2 * i
                    tt(MA[:, k:k + 2, :], MA[:, k:k + 2, :],
                                ps(f"wa {j}.{i}")[:, :].rearrange("p (k t) -> p k t", k=2), ALU.mult).then_inc(dve.tick(f"ev wa {j}.{i}"), 1)
            rwkv_dve(dve)
            dve.stage = "b2 end"
            for j in range(4):
                split_lo(dve, at_unit[("gb", j)] + 2)
            dve.eng.wait_ge(*T.at("gate b"))
            for j in range(2):
                split_lo(dve, at_unit[("wb", j)] + 2)
                for i in range(2):
                    dve.eng.wait_ge(*T.at(f"mm wb {j}.{i}"))
                    k = 4 * j + 2 * i
                    tt(tC[:, k:k + 2, :], tA[:, k:k + 2, :],
                                ps(f"wb {j}.{i}")[:, :].rearrange("p (k t) -> p k t", k=2), ALU.mult).then_inc(dve.tick(f"ev wb {j}.{i}"), 1)
                    dve.eng.wait_ge(*dve.own())
                    tt(tC[:, k:k + 2, :], tC[:, k:k + 2, :], MA[:, k:k + 2, :], ALU.add).then_inc(dve.tick(f"f mix {2 * j + i}"), 1)
            halves_lo("mix", Hl, tC, Hh)
            T.mark("Hl mix", *dve.last)
            for j in range(4):
                split_lo(dve, at_unit[("w_out", j)] + 2)
                dve.eng.wait_ge(*T.at(f"mm w_out {j}"))
                for b in range(2):
                    k = 2 * j + b
                    stt(tA[:, k, :], xT[:, k, :], ALPHA2, ps(f"w_out {j}")[:, b * S:(b + 1) * S],
                                 ALU.mult, ALU.add).then_inc(dve.tick(f"z ln5 {k}"), 1)
                T.mark(f"ev w_out {j}", *dve.last)
            ln("ln5")
            affine("ln_g_2", "ln_b_2", 0)
            dve.stage = "m2"
            T.mark("Hf m2", *dve.last)
            moe_dve(dve, m2)
            rest_dve(dve, m2)
            for k in range(KT):
                stt(tA[:, k, :], xT[:, k, :], ALPHA2, tB[:, k, :], ALU.mult, ALU.add).then_inc(dve.tick(f"z ln6 {k}"), 1)
            ln("ln6")
            affine("ln_g_2", "ln_b_2", 1)
            dve.stage = "ple"
            for j in range(4):
                T.mark(f"f ple {j}", *dve.last)
            halves_lo("ple", Hl, xT, Hh)
            T.mark("Hl ple", *dve.last)
            dve.eng.wait_ge(*T.at("Gh ple"))
            tt(Gl[:, 0:2, :], ps("pT")[:, :].rearrange("p (k t) -> p k t", k=2),
                        Gh[:, 0:2, :].bitcast(F32), ALU.subtract).then_inc(dve.tick("Gl ple"), 1)
            T.mark("ev pT", *dve.last)
            for j in range(4):
                split_lo(dve, at_unit[("pg", j)] + 2)
            for j in range(4):
                dve.eng.wait_ge(*T.at(f"gate p {j}"))
                dve.eng.wait_ge(*T.at(f"mm pp.{j}"))
                s = slice(2 * j, 2 * j + 2)
                tt(tB[:, s, :], tB[:, s, :], ps(f"pp.{j}")[:, :].rearrange("p (k t) -> p k t", k=2),
                            ALU.mult).then_inc(dve.tick(f"ev pp.{j}"), 1)
                dve.eng.wait_ge(*dve.own())
                for k in (2 * j, 2 * j + 1):
                    stt(tA[:, k, :], xT[:, k, :], ALPHA2, tB[:, k, :], ALU.mult, ALU.add).then_inc(dve.tick(f"z ln7 {k}"), 1)
            ln("ln7")
            dve.eng.wait_ge(*dve.own())
            for k in range(KT):
                ts(tD[:, k, :], tA[:, k, :], col("ln_g_2", k, 2), col("ln_b_2", k, 2), ALU.mult, ALU.add).then_inc(dve.tick(), 1)
            T.mark("x out", *dve.last)

    return {**T.marks, "bank": T.banks}


_INS = ["x", "c", "ada_w", "ada_b", "ln_g", "ln_b", "conv_in_w", "conv_in_b", "conv_dw_w", "conv_dw_b",
        "conv_norm_g", "conv_norm_b", "conv_out_w", "conv_out_b", "kv_ada_w", "kv_ada_b", "w_kv", "w_q", "w_o",
        "ffn_w13", "ffn_w2", "router_w", "router_b", "moe_w13", "moe_w2", "p_2", "ln_in_g_2", "ln_in_b_2",
        "rel_bias_2", "w_in_2", "tok_mix_2", "decay_base_2", "decay_up_2", "aaa_base_2", "aaa_up_2",
        "gate_up_2", "k_k_2", "k_a_2", "r_k_2", "gn_g_2", "gn_b_2", "w_branch_attn_2", "w_branch_rwkv_2",
        "w_out_2", "router_grp_2", "router_grp_bias_2", "router_exp_2", "router_exp_bias_2", "exp_gate_2",
        "exp_up_2", "exp_down_2", "ple_proj_2", "ple_gate_2", "ln_g_2", "ln_b_2"]


def kernel(**inputs):
    import numpy as _np
    import concourse.bacc as _bacc
    from concourse import mybir as _mybir
    from concourse.bass_utils import run_bass_kernel_spmd as _run

    arrays = {f"in_{name}": _np.ascontiguousarray(inputs[name]) for name in _INS}

    def program(known):
        nc = _bacc.Bacc("TRN2", target_bir_lowering=False, num_devices=1)
        A = {name: nc.dram_tensor(f"in_{name}", arrays[f"in_{name}"].shape,
                                  _mybir.dt.from_np(arrays[f"in_{name}"].dtype), kind="ExternalInput").ap()
             for name in _INS}
        out = nc.dram_tensor("out_0", inputs["x"].shape, _mybir.dt.float32, kind="ExternalOutput").ap()
        return nc, block_pair(nc, A, out, known)

    _, known = program({})
    nc, _ = program(known)
    r = _run(nc, [arrays], core_ids=[0])
    return r.results[0]["out_0"]
```
